# Optimizing a Trainium2 kernel written in Bass

```python
import math
import jax, jax.numpy as jnp
from jax import lax
import numpy as np

D_MODEL = 1024
BATCH = 1
SEQ = 256
DEPTH = 2

CHUNK = 64
N_MIXERS = 3
ALPHA = (2.0 * DEPTH) ** 0.25
BETA = (8.0 * DEPTH) ** -0.25
LN_EPS = 1e-5
RMS_EPS = 1e-6
SC_WIDTH = 3
MLA_HEADS = 8
QK_NOPE = 128
QK_ROPE = 64
V_HEAD = 128
Q_LORA = 3 * D_MODEL // 8
KV_LORA = D_MODEL // 4
ROPE_THETA = 10000.0
Q_BLOCK = 128
CONF_WIDTH = 31
D_FF = 4 * D_MODEL
N_A = len(range(0, DEPTH, N_MIXERS))
N_B = len(range(1, DEPTH, N_MIXERS))
N_C = len(range(2, DEPTH, N_MIXERS))


def _layer_norm(x, g, b):
    xf = x.astype(jnp.float32)
    mu = jnp.mean(xf, axis=-1, keepdims=True)
    var = jnp.mean(jnp.square(xf - mu), axis=-1, keepdims=True)
    y = (xf - mu) * lax.rsqrt(var + LN_EPS) * g.astype(jnp.float32) + b.astype(jnp.float32)
    return y.astype(x.dtype)

def _rms_norm(x, g):
    xf = x.astype(jnp.float32)
    y = xf * lax.rsqrt(jnp.mean(jnp.square(xf), axis=-1, keepdims=True) + RMS_EPS) * g.astype(jnp.float32)
    return y.astype(x.dtype)

def _causal_dwconv(x, w):
    k_width, c = w.shape
    return lax.conv_general_dilated(
        x, w[:, None, :].astype(x.dtype), window_strides=(1,), padding=[(k_width - 1, 0)],
        dimension_numbers=("NWC", "WIO", "NWC"), feature_group_count=c)

def _rope(x, cos, sin):
    x1, x2 = jnp.split(x, 2, axis=-1)
    c = cos[None, :, None, :].astype(x.dtype)
    s = sin[None, :, None, :].astype(x.dtype)
    return jnp.concatenate([x1 * c - x2 * s, x1 * s + x2 * c], axis=-1)

def _short_conv_mixer(x, w_in, conv_w, w_out):
    b_gate, c_gate, h = jnp.split(x @ w_in, 3, axis=-1)
    return (b_gate * _causal_dwconv(c_gate * h, conv_w)) @ w_out

def _mla_mixer(x, w_dq, g_q, w_uq, w_dkv, g_kv, w_uk, w_uv, w_o):
    bsz, seq, _ = x.shape
    pos = jnp.arange(seq, dtype=jnp.float32)
    inv_freq = ROPE_THETA ** (-jnp.arange(0, QK_ROPE, 2, dtype=jnp.float32) / QK_ROPE)
    ang = pos[:, None] * inv_freq[None, :]
    cos, sin = jnp.cos(ang), jnp.sin(ang)
    cq = _rms_norm(x @ w_dq, g_q)
    q = (cq @ w_uq).reshape(bsz, seq, MLA_HEADS, QK_NOPE + QK_ROPE)
    q_nope, q_pe = q[..., :QK_NOPE], _rope(q[..., QK_NOPE:], cos, sin)
    ckv_full = x @ w_dkv
    ckv = _rms_norm(ckv_full[..., :KV_LORA], g_kv)
    k_pe = _rope(ckv_full[..., None, KV_LORA:], cos, sin)[:, :, 0, :]
    k_nope = jnp.einsum("bsc,chd->bshd", ckv, w_uk)
    v = jnp.einsum("bsc,chd->bshd", ckv, w_uv)
    scale = (QK_NOPE + QK_ROPE) ** -0.5
    n_blk = seq // Q_BLOCK
    qn_b = q_nope.reshape(bsz, n_blk, Q_BLOCK, MLA_HEADS, QK_NOPE).transpose(1, 0, 2, 3, 4)
    qp_b = q_pe.reshape(bsz, n_blk, Q_BLOCK, MLA_HEADS, QK_ROPE).transpose(1, 0, 2, 3, 4)
    k_chunk = jnp.arange(seq) // CHUNK

    def block(args):
        qn, qp, blk = args
        s = (jnp.einsum("bqhd,bkhd->bhqk", qn, k_nope)
             + jnp.einsum("bqhd,bkd->bhqk", qp, k_pe)).astype(jnp.float32) * scale
        q_chunk = (blk * Q_BLOCK + jnp.arange(Q_BLOCK)) // CHUNK
        allowed = k_chunk[None, :] <= q_chunk[:, None]
        p = jax.nn.softmax(jnp.where(allowed[None, None], s, -jnp.inf), axis=-1).astype(v.dtype)
        return jnp.einsum("bhqk,bkhd->bqhd", p, v)

    o = lax.map(block, (qn_b, qp_b, jnp.arange(n_blk)))
    o = o.transpose(1, 0, 2, 3, 4).reshape(bsz, seq, MLA_HEADS * V_HEAD)
    return o @ w_o

def _conformer_conv_mixer(x, w_pw1, b_pw1, dw_w, dw_b, norm_g, norm_b, w_pw2, b_pw2):
    a, gate = jnp.split(x @ w_pw1 + b_pw1, 2, axis=-1)
    h = a * jax.nn.sigmoid(gate)
    h = _causal_dwconv(h, dw_w) + dw_b
    h = jax.nn.silu(_layer_norm(h, norm_g, norm_b))
    return h @ w_pw2 + b_pw2

def _sq_relu_mlp(x, w1, w2):
    return jnp.square(jax.nn.relu(x @ w1)) @ w2

def _normal(k, shape, fan_in, scale=1.0):
    return jax.random.normal(k, shape, jnp.float32) * (scale * fan_in ** -0.5)

def first_inputs(seed: int = 0) -> dict:
    key = jax.random.key(seed)
    ks = iter(jax.random.split(key, 40))
    D = D_MODEL
    gain = lambda shape: 1.0 + 0.02 * jax.random.normal(next(ks), shape, jnp.float32)
    bias = lambda shape: 0.02 * jax.random.normal(next(ks), shape, jnp.float32)
    return {
        "x": jax.random.normal(next(ks), (BATCH, SEQ, D), jnp.float32),
        "sc_w_in": _normal(next(ks), (N_A, D, 3 * D), D),
        "sc_conv_w": _normal(next(ks), (N_A, SC_WIDTH, D), SC_WIDTH),
        "sc_w_out": _normal(next(ks), (N_A, D, D), D, BETA),
        "mla_w_dq": _normal(next(ks), (N_B, D, Q_LORA), D),
        "mla_g_q": gain((N_B, Q_LORA)),
        "mla_w_uq": _normal(next(ks), (N_B, Q_LORA, MLA_HEADS * (QK_NOPE + QK_ROPE)), Q_LORA),
        "mla_w_dkv": _normal(next(ks), (N_B, D, KV_LORA + QK_ROPE), D),
        "mla_g_kv": gain((N_B, KV_LORA)),
        "mla_w_uk": _normal(next(ks), (N_B, KV_LORA, MLA_HEADS, QK_NOPE), KV_LORA),
        "mla_w_uv": _normal(next(ks), (N_B, KV_LORA, MLA_HEADS, V_HEAD), KV_LORA, BETA),
        "mla_w_o": _normal(next(ks), (N_B, MLA_HEADS * V_HEAD, D), MLA_HEADS * V_HEAD, BETA),
        "cf_w_pw1": _normal(next(ks), (N_C, D, 2 * D), D),
        "cf_b_pw1": bias((N_C, 2 * D)),
        "cf_dw_w": _normal(next(ks), (N_C, CONF_WIDTH, D), CONF_WIDTH),
        "cf_dw_b": bias((N_C, D)),
        "cf_norm_g": gain((N_C, D)),
        "cf_norm_b": bias((N_C, D)),
        "cf_w_pw2": _normal(next(ks), (N_C, D, D), D, BETA),
        "cf_b_pw2": bias((N_C, D)),
        "ff_w1": _normal(next(ks), (DEPTH, D, D_FF), D, BETA),
        "ff_w2": _normal(next(ks), (DEPTH, D_FF, D), D_FF, BETA),
        "ln_mix_g": gain((DEPTH, D)),
        "ln_mix_b": bias((DEPTH, D)),
        "ln_ff_g": gain((DEPTH, D)),
        "ln_ff_b": bias((DEPTH, D)),
    }

def first_block(x, sc_w_in, sc_conv_w, sc_w_out,
              mla_w_dq, mla_g_q, mla_w_uq, mla_w_dkv, mla_g_kv, mla_w_uk, mla_w_uv, mla_w_o,
              cf_w_pw1, cf_b_pw1, cf_dw_w, cf_dw_b, cf_norm_g, cf_norm_b, cf_w_pw2, cf_b_pw2,
              ff_w1, ff_w2, ln_mix_g, ln_mix_b, ln_ff_g, ln_ff_b):
    for i in range(DEPTH):
        m, j = i % N_MIXERS, i // N_MIXERS
        if m == 0:
            y = _short_conv_mixer(x, sc_w_in[j], sc_conv_w[j], sc_w_out[j])
        elif m == 1:
            y = _mla_mixer(x, mla_w_dq[j], mla_g_q[j], mla_w_uq[j], mla_w_dkv[j], mla_g_kv[j],
                           mla_w_uk[j], mla_w_uv[j], mla_w_o[j])
        else:
            y = _conformer_conv_mixer(x, cf_w_pw1[j], cf_b_pw1[j], cf_dw_w[j], cf_dw_b[j],
                                      cf_norm_g[j], cf_norm_b[j], cf_w_pw2[j], cf_b_pw2[j])
        x = _layer_norm(ALPHA * x + y, ln_mix_g[i], ln_mix_b[i])
        x = _layer_norm(ALPHA * x + _sq_relu_mlp(x, ff_w1[i], ff_w2[i]), ln_ff_g[i], ln_ff_b[i])
    return x


DEPTH_2 = 1

LEFT_CHUNKS = 8
BAND = LEFT_CHUNKS + 1
EPS = 1e-5
D_FF_2 = 2816
SSD_HEADS = 16
SSD_HEAD_DIM = 64
SSD_INNER = SSD_HEADS * SSD_HEAD_DIM
SSD_GROUPS = 2
SSD_STATE = 128
CONV_WIDTH = 4
CONV_DIM = SSD_INNER + 2 * SSD_GROUPS * SSD_STATE
ATT_HEADS = 8
ATT_HEAD_DIM = 64
ATT_INNER = ATT_HEADS * ATT_HEAD_DIM
MAX_REL = 256
MIX_WIDTH = SSD_INNER + ATT_INNER
PROJ_DIM = SSD_INNER + CONV_DIM + SSD_HEADS + 3 * ATT_INNER


def rms_norm(x, w):
    xf = x.astype(jnp.float32)
    y = xf * lax.rsqrt(jnp.mean(xf * xf, axis=-1, keepdims=True) + EPS)
    return (y * w.astype(jnp.float32)).astype(x.dtype)

def swiglu(h, w_gate, w_up, w_down):
    return (jax.nn.silu(h @ w_gate) * (h @ w_up)) @ w_down

def causal_depthwise_conv(u, w, b):
    k = w.shape[0]
    out = lax.conv_general_dilated(
        u, w.astype(u.dtype)[:, None, :], window_strides=(1,), padding=[(k - 1, 0)],
        dimension_numbers=('NWC', 'WIO', 'NWC'), feature_group_count=u.shape[-1])
    return out + b.astype(u.dtype)

def ssd_chunked(xs, dt, a, bmat, cmat, d_skip):
    bsz, seqlen, n_heads, hd = xs.shape
    n_groups, n_state = bmat.shape[-2], bmat.shape[-1]
    m = n_heads // n_groups
    nc = seqlen // CHUNK
    xf = xs.astype(jnp.float32)
    xdt = (xf * dt[..., None]).reshape(bsz, nc, CHUNK, n_groups, m, hd)
    a_cs = jnp.cumsum((dt * a).reshape(bsz, nc, CHUNK, n_groups, m), axis=2)
    bc = bmat.astype(jnp.float32).reshape(bsz, nc, CHUNK, n_groups, n_state)
    cc = cmat.astype(jnp.float32).reshape(bsz, nc, CHUNK, n_groups, n_state)
    causal = jnp.tril(jnp.ones((CHUNK, CHUNK), dtype=bool))[:, :, None, None]
    seg = a_cs[:, :, :, None] - a_cs[:, :, None, :]
    decay = jnp.exp(jnp.where(causal, seg, -jnp.inf))
    cb = jnp.einsum('bclgn,bcsgn->bclsg', cc, bc)
    y_diag = jnp.einsum('bclsg,bclsgm,bcsgmp->bclgmp', cb, decay, xdt)
    decay_out = jnp.exp(a_cs[:, :, -1:] - a_cs)
    states = jnp.einsum('bclgn,bclgm,bclgmp->bcgmpn', bc, decay_out, xdt)
    chunk_decay = jnp.exp(a_cs[:, :, -1])

    def step(h, inp):
        s_c, d_c = inp
        return h * d_c[..., None, None] + s_c, h

    h0 = jnp.zeros((bsz, n_groups, m, hd, n_state), jnp.float32)
    _, prev = lax.scan(step, h0, (jnp.moveaxis(states, 1, 0), jnp.moveaxis(chunk_decay, 1, 0)))
    prev = jnp.moveaxis(prev, 0, 1)
    y_off = jnp.einsum('bclgn,bcgmpn,bclgm->bclgmp', cc, prev, jnp.exp(a_cs))
    y = (y_diag + y_off).reshape(bsz, seqlen, n_heads, hd)
    return y + xf * d_skip.astype(jnp.float32)[:, None]

def chunked_rel_attention(q, k, v, rel_bias):
    bsz, seqlen, n_heads, hd = q.shape
    nc = seqlen // CHUNK
    qc = q.reshape(bsz, nc, CHUNK, n_heads, hd)
    pad = ((0, 0), (LEFT_CHUNKS * CHUNK, 0), (0, 0), (0, 0))
    kp = jnp.pad(k, pad).reshape(bsz, nc + LEFT_CHUNKS, CHUNK, n_heads, hd)
    vp = jnp.pad(v, pad).reshape(bsz, nc + LEFT_CHUNKS, CHUNK, n_heads, hd)
    kb = jnp.stack([kp[:, o:o + nc] for o in range(BAND)], axis=2).reshape(bsz, nc, BAND * CHUNK, n_heads, hd)
    vb = jnp.stack([vp[:, o:o + nc] for o in range(BAND)], axis=2).reshape(bsz, nc, BAND * CHUNK, n_heads, hd)
    qpos = LEFT_CHUNKS * CHUNK + jnp.arange(CHUNK)
    kpos = jnp.arange(BAND * CHUNK)
    rel = jnp.clip(qpos[:, None] - kpos[None, :], -MAX_REL, MAX_REL) + MAX_REL
    bias = rel_bias.astype(jnp.float32)[:, rel]
    s = jnp.einsum('bcqhd,bckhd->bhcqk', qc, kb).astype(jnp.float32) * (hd ** -0.5) + bias[None, :, None]
    valid = (jnp.arange(nc)[:, None] - LEFT_CHUNKS + jnp.arange(BAND)[None, :]) >= 0
    valid = jnp.repeat(valid, CHUNK, axis=1)
    s = jnp.where(valid[None, None, :, None, :], s, jnp.finfo(jnp.float32).min)
    p = jax.nn.softmax(s, axis=-1).astype(v.dtype)
    o = jnp.einsum('bhcqk,bckhd->bcqhd', p, vb)
    return o.reshape(bsz, seqlen, n_heads * hd)

def hybrid_mixer(x, mix_norm, w_in, conv_w, conv_b, dt_bias, a_log, d_skip, ssd_norm, rel_bias, w_out):
    bsz, seqlen, _ = x.shape
    h = rms_norm(x, mix_norm)
    proj = h @ w_in
    o1 = SSD_INNER
    o2 = o1 + CONV_DIM
    o3 = o2 + SSD_HEADS
    o4 = o3 + ATT_INNER
    o5 = o4 + ATT_INNER
    z, xbc, dt_raw = proj[..., :o1], proj[..., o1:o2], proj[..., o2:o3]
    q, k, v = proj[..., o3:o4], proj[..., o4:o5], proj[..., o5:]
    xbc = jax.nn.silu(causal_depthwise_conv(xbc, conv_w, conv_b))
    gn = SSD_GROUPS * SSD_STATE
    xs = xbc[..., :SSD_INNER].reshape(bsz, seqlen, SSD_HEADS, SSD_HEAD_DIM)
    bm = xbc[..., SSD_INNER:SSD_INNER + gn].reshape(bsz, seqlen, SSD_GROUPS, SSD_STATE)
    cm = xbc[..., SSD_INNER + gn:].reshape(bsz, seqlen, SSD_GROUPS, SSD_STATE)
    dt = jax.nn.softplus(dt_raw.astype(jnp.float32) + dt_bias.astype(jnp.float32))
    a = -jnp.exp(a_log.astype(jnp.float32))
    y = ssd_chunked(xs, dt, a, bm, cm, d_skip).reshape(bsz, seqlen, SSD_INNER)
    y = rms_norm(y * jax.nn.silu(z.astype(jnp.float32)), ssd_norm).astype(x.dtype)
    att = chunked_rel_attention(
        q.reshape(bsz, seqlen, ATT_HEADS, ATT_HEAD_DIM),
        k.reshape(bsz, seqlen, ATT_HEADS, ATT_HEAD_DIM),
        v.reshape(bsz, seqlen, ATT_HEADS, ATT_HEAD_DIM), rel_bias).astype(x.dtype)
    return jnp.concatenate([y, att], axis=-1) @ w_out

def second_inputs(seed: int = 0) -> dict:
    key = jax.random.key(seed)
    ks = jax.random.split(key, 24)

    def nrm(k, shape, scale):
        return jax.random.normal(k, shape, jnp.float32) * scale

    def gain(k, n):
        return 1.0 + nrm(k, (DEPTH_2, n), 0.02)

    u = jax.random.uniform(ks[10], (DEPTH_2, SSD_HEADS), jnp.float32)
    dt0 = jnp.exp(u * (np.log(0.1) - np.log(0.001)) + np.log(0.001))
    dt_bias = dt0 + jnp.log(-jnp.expm1(-dt0))
    a_log = jnp.log(jax.random.uniform(ks[11], (DEPTH_2, SSD_HEADS), jnp.float32, 1.0, 16.0))
    return {
        "x": nrm(ks[0], (BATCH, SEQ, D_MODEL), 1.0),
        "ffn1_norm": gain(ks[1], D_MODEL),
        "ffn1_w_gate": nrm(ks[2], (DEPTH_2, D_MODEL, D_FF_2), D_MODEL ** -0.5),
        "ffn1_w_up": nrm(ks[3], (DEPTH_2, D_MODEL, D_FF_2), D_MODEL ** -0.5),
        "ffn1_w_down": nrm(ks[4], (DEPTH_2, D_FF_2, D_MODEL), D_FF_2 ** -0.5),
        "mix_norm": gain(ks[5], D_MODEL),
        "w_in": nrm(ks[6], (DEPTH_2, D_MODEL, PROJ_DIM), D_MODEL ** -0.5),
        "conv_w": nrm(ks[7], (DEPTH_2, CONV_WIDTH, CONV_DIM), CONV_WIDTH ** -0.5),
        "conv_b": nrm(ks[8], (DEPTH_2, CONV_DIM), 0.02),
        "dt_bias": dt_bias,
        "a_log": a_log,
        "d_skip": 1.0 + nrm(ks[12], (DEPTH_2, SSD_HEADS), 0.1),
        "ssd_norm": gain(ks[13], SSD_INNER),
        "rel_bias": nrm(ks[14], (DEPTH_2, ATT_HEADS, 2 * MAX_REL + 1), 0.1),
        "w_out": nrm(ks[15], (DEPTH_2, MIX_WIDTH, D_MODEL), MIX_WIDTH ** -0.5),
        "ffn2_norm": gain(ks[16], D_MODEL),
        "ffn2_w_gate": nrm(ks[17], (DEPTH_2, D_MODEL, D_FF_2), D_MODEL ** -0.5),
        "ffn2_w_up": nrm(ks[18], (DEPTH_2, D_MODEL, D_FF_2), D_MODEL ** -0.5),
        "ffn2_w_down": nrm(ks[19], (DEPTH_2, D_FF_2, D_MODEL), D_FF_2 ** -0.5),
        "final_norm": 1.0 + nrm(ks[20], (D_MODEL,), 0.02),
    }

def second_block(x, ffn1_norm, ffn1_w_gate, ffn1_w_up, ffn1_w_down, mix_norm, w_in, conv_w, conv_b,
              dt_bias, a_log, d_skip, ssd_norm, rel_bias, w_out, ffn2_norm, ffn2_w_gate, ffn2_w_up,
              ffn2_w_down, final_norm):
    for i in range(DEPTH_2):
        x = x + 0.5 * swiglu(rms_norm(x, ffn1_norm[i]), ffn1_w_gate[i], ffn1_w_up[i], ffn1_w_down[i])
        x = x + hybrid_mixer(x, mix_norm[i], w_in[i], conv_w[i], conv_b[i], dt_bias[i], a_log[i],
                             d_skip[i], ssd_norm[i], rel_bias[i], w_out[i])
        x = x + 0.5 * swiglu(rms_norm(x, ffn2_norm[i]), ffn2_w_gate[i], ffn2_w_up[i], ffn2_w_down[i])
    return rms_norm(x, final_norm)


def setup_inputs(seed=0):
    out = dict(first_inputs(seed))
    for name, value in second_inputs(seed + 1).items():
        if name != "x":
            out[name + "_2"] = value
    return out


def reference(
    x, sc_w_in, sc_conv_w, sc_w_out, mla_w_dq, mla_g_q, mla_w_uq, mla_w_dkv, mla_g_kv, mla_w_uk,
    mla_w_uv, mla_w_o, cf_w_pw1, cf_b_pw1, cf_dw_w, cf_dw_b, cf_norm_g, cf_norm_b, cf_w_pw2,
    cf_b_pw2, ff_w1, ff_w2, ln_mix_g, ln_mix_b, ln_ff_g, ln_ff_b, ffn1_norm_2, ffn1_w_gate_2,
    ffn1_w_up_2, ffn1_w_down_2, mix_norm_2, w_in_2, conv_w_2, conv_b_2, dt_bias_2, a_log_2,
    d_skip_2, ssd_norm_2, rel_bias_2, w_out_2, ffn2_norm_2, ffn2_w_gate_2, ffn2_w_up_2,
    ffn2_w_down_2, final_norm_2,
):
    x = first_block(
        x, sc_w_in, sc_conv_w, sc_w_out, mla_w_dq, mla_g_q, mla_w_uq, mla_w_dkv, mla_g_kv,
        mla_w_uk, mla_w_uv, mla_w_o, cf_w_pw1, cf_b_pw1, cf_dw_w, cf_dw_b, cf_norm_g, cf_norm_b,
        cf_w_pw2, cf_b_pw2, ff_w1, ff_w2, ln_mix_g, ln_mix_b, ln_ff_g, ln_ff_b,
    )
    return second_block(
        x, ffn1_norm_2, ffn1_w_gate_2, ffn1_w_up_2, ffn1_w_down_2, mix_norm_2, w_in_2, conv_w_2,
        conv_b_2, dt_bias_2, a_log_2, d_skip_2, ssd_norm_2, rel_bias_2, w_out_2, ffn2_norm_2,
        ffn2_w_gate_2, ffn2_w_up_2, ffn2_w_down_2, final_norm_2,
    )


_drawn_inputs = setup_inputs


def setup_inputs(seed=0):
    import zlib

    import numpy as np

    out = dict(_drawn_inputs(seed))
    spreads = {}
    factors = {'mla_g_q': 8.0,
     'mla_g_kv': 8.0,
     'ffn1_norm_2': 5.394,
     'mix_norm_2': 2.936,
     'conv_b_2': 15.315,
     'ssd_norm_2': 27.529,
     'rel_bias_2': 26.563,
     'ffn2_norm_2': 23.028,
     'final_norm_2': 22.773,
     'd_skip_2': 46.108}
    for name, (base, spread) in spreads.items():
        noise = np.random.default_rng([zlib.crc32(name.encode()), seed]).standard_normal(out[name].shape)
        drawn = base * np.exp(spread * noise) if base else spread * noise
        out[name] = __import__('jax').numpy.asarray(drawn.astype(out[name].dtype))
    for name, factor in factors.items():
        out[name] = (out[name] * factor).astype(out[name].dtype)
    return out
```

```python
from contextlib import ExitStack

import numpy as np

import concourse.bass as bass
from concourse import mybir

F32 = mybir.dt.float32
F32R = mybir.dt.float32r
BF16 = mybir.dt.bfloat16
ACT = mybir.ActivationFunctionType
ALU = mybir.AluOpType
AX_X = mybir.AxisListType.X

P = 128
TOKENS = 256
TILES = TOKENS // P
D = 1024
KD = D // P
HALF = 512
CHUNK_F = 256
CT = CHUNK_F // P
RING = 4
SLAB = 2048
ATTN_CHUNK = 64

DEPTH = 2
ALPHA = (2.0 * DEPTH) ** 0.25
LN_EPS = 1e-5
MLA_EPS = 1e-6
RMS_EPS = 1e-5
D_FF = 4096
D_FF_2 = 2816
HEADS = 8
NOPE, ROPE, Q_LORA, KV_LORA = 128, 64, 384, 256
KQ, KKV = Q_LORA // P, KV_LORA // P
QK_SCALE = float(NOPE + ROPE) ** -0.5
SSD_HEADS, SSD_HD, SSD_GROUPS = 16, 64, 2
SSD_INNER = SSD_HEADS * SSD_HD
XBC = SSD_INNER + 2 * SSD_GROUPS * P
ATT_HD = 64
ATT_INNER = HEADS * ATT_HD
REL = 513
MIX = SSD_INNER + ATT_INNER
Z0, XBC0, DT0 = 0, SSD_INNER, SSD_INNER + XBC
Q0 = DT0 + SSD_HEADS
K0, V0 = Q0 + ATT_INNER, Q0 + 2 * ATT_INNER
MASKED = -1.0e30

SC_TAPS, XBC_TAPS = 3, 4
XT = XBC // P
ROW_SC, ROW_XBC, ROW_XBC_B = 0, SC_TAPS * KD, SC_TAPS * KD + XBC_TAPS * XT
ROWS = ROW_XBC_B + XT

C_ID, C_ANTI, C_TRI, C_AFTER, C_SWAP, C_COS, C_SIN, C_MROW = 0, 128, 256, 384, 512, 640, 896, 1152
C_ALL = 1280 + 64


def shape_constants():
    c = np.zeros((P, C_ALL), np.float32)
    i = np.arange(P)
    c[:, C_ID:C_ID + P] = np.eye(P)
    c[:, C_ANTI:C_ANTI + P] = np.eye(P)[::-1]
    c[:, C_TRI:C_TRI + P] = i[:, None] <= i[None, :]
    c[:, C_AFTER:C_AFTER + P] = i[:, None] > i[None, :]
    h = ROPE // 2
    for d in range(P):
        src, sign = (d + h, -1.0) if d % ROPE < h else (d - h, 1.0)
        c[src, C_SWAP + d] = sign
    inv = np.float32(10000.0) ** (-np.arange(0, ROPE, 2, dtype=np.float32) / np.float32(ROPE))
    ang = np.arange(TOKENS, dtype=np.float32)[None, :] * inv[i % h][:, None]
    c[:, C_COS:C_COS + TOKENS] = np.cos(ang)
    c[:, C_SIN:C_SIN + TOKENS] = np.sin(ang)
    c[0, C_MROW:C_MROW + ATTN_CHUNK] = MASKED
    c[0, C_MROW + P:C_MROW + P + ATTN_CHUNK] = 1.0
    return c


def two_blocks(nc, t, consts, out):
    FF_CHUNKS = D_FF // CHUNK_F
    SG_CHUNKS = D_FF_2 // CHUNK_F
    SC_CHUNKS = D // CHUNK_F
    N_SC = 4 * SC_CHUNKS
    N_FF = 2 * FF_CHUNKS
    N_MLA = 4 + 4 + 2 + 4
    N_SG = 4 * SG_CHUNKS
    GLU_PASSES = (SG_CHUNKS - 1) // 2 - 1
    N_HY = 6 + 1 + 4 + 2 + 4 + 6
    S_SC = 0
    S_FF = [S_SC + N_SC, S_SC + N_SC + N_FF + N_MLA]
    S_MLA = S_FF[0] + N_FF
    S_SG = [S_FF[1] + N_FF, S_FF[1] + N_FF + N_SG + N_HY]
    S_HY = S_SG[0] + N_SG
    N_SLABS = S_SG[1] + N_SG

    width = [SLAB] * N_SLABS
    loads = [1] * N_SLABS
    for s in S_SG:
        for i in range(SG_CHUNKS):
            d0 = s + 4 * i + 4 if i < SG_CHUNKS - 1 else s + 4 * i + 2
            width[d0] = width[d0 + 1] = D
    DQ, KV, UQ, UK, UV, WO = S_MLA, S_MLA + 2, S_MLA + 4, S_MLA + 8, S_MLA + 9, S_MLA + 10
    UQ_COLS = 2 * (NOPE + ROPE)
    KV_COLS = KV_LORA + 2 * ROPE
    for m in (DQ, DQ + 1):
        width[m] = 4 * Q_LORA
    for m in (KV, KV + 1):
        width[m], loads[m] = 4 * KV_COLS, 2
    for m in range(UQ, UQ + 4):
        width[m], loads[m] = KQ * UQ_COLS, 4
    HX, HDT, HQK, HV, HZ, HWO = S_HY, S_HY + 6, S_HY + 7, S_HY + 11, S_HY + 13, S_HY + 17
    width[HDT] = KD * SSD_HEADS
    landed_at, used_dmas = [], [0] * RING
    for m in range(N_SLABS):
        used_dmas[m % RING] += loads[m]
        landed_at.append(16 * used_dmas[m % RING])

    with ExitStack() as ctx:
        def sb(name, shape, dt=F32):
            return ctx.enter_context(nc.sbuf_tensor(name, shape, dt))

        def sem(name):
            return ctx.enter_context(nc.semaphore(name))

        raw = sb("raw", [P, RING, SLAB])
        weight_hi = sb("weight_hi", [P, RING, SLAB], F32R)
        weight_lo = sb("weight_lo", [P, RING, SLAB], F32R)
        x_tok = sb("x_tok", [P, TILES, D])
        normed = sb("normed", [P, TILES, D])
        xh = sb("xh", [P, KD, TOKENS], F32R)
        xl = sb("xl", [P, KD, TOKENS], F32R)
        hh = sb("hh", [P, 2 * CT, TOKENS], F32R)
        hl = sb("hl", [P, 2 * CT, TOKENS], F32R)
        tmp_a = sb("tmp_a", [P, HALF])
        tmp_b = sb("tmp_b", [P, HALF])
        tmp_c = sb("tmp_c", [P, HALF])
        tmp_d = sb("tmp_d", [P, HALF])
        gain = sb("gain", [P, D])
        bias = sb("bias", [P, D])
        gain2 = sb("gain2", [P, D])
        cst = sb("cst", [P, C_ALL])
        rows = sb("rows", [ROWS, P])
        cols = sb("cols", [P, ROWS])
        zeros = sb("zeros", [1, HALF], BF16)
        stat = sb("stat", [P, TILES, 2, 6])
        mean_var = sb("mean_var", [P, TILES, 2])
        rstd = sb("rstd", [P, 4])
        sumsq = sb("sumsq", [P, 4])
        half_neg = sb("half_neg", [P, 1])
        arena = sb("arena", [P, 10368])

        acc = ctx.enter_context(nc.psum_tensor("acc", [P, 4, HALF], F32))
        up = [ctx.enter_context(nc.psum_tensor(f"up{i}", [P, HALF], F32)) for i in range(4)]

        ident = cst[:, C_ID:C_ID + P]
        anti = cst[:, C_ANTI:C_ANTI + P]
        tri = cst[:, C_TRI:C_TRI + P]
        after = cst[:, C_AFTER:C_AFTER + P]
        swap = cst[:, C_SWAP:C_SWAP + P]
        cos = cst[:, C_COS:C_COS + TOKENS]
        sin = cst[:, C_SIN:C_SIN + TOKENS]
        mask_row = cst[0:1, C_MROW:C_MROW + P]
        mask_ones = cst[0:1, C_MROW + P:C_MROW + P + ATTN_CHUNK]

        at = [0]

        def take(n, *dims):
            a = arena[:, at[0]:at[0] + n]
            at[0] += n
            if len(dims) == 2:
                a = a.rearrange("p (a b) -> p a b", a=dims[0])
            return a

        q_nope = take(HEADS * TOKENS, HEADS, TOKENS)
        k_nope = take(HEADS * TOKENS, HEADS, TOKENS)
        q_rot = take(4 * TOKENS, 4, TOKENS)
        k_rot = take(TOKENS)
        pe_raw = take(2 * TOKENS, 2, TOKENS)
        g_q = take(Q_LORA)
        g_kv = take(KV_LORA)
        prob_a = take(2 * 384, 2, 384)
        prob_t_a = take(2 * 384, 2, 384)
        v_a = normed
        latent_q = normed[:, 0, 0:2 * Q_LORA].rearrange("p (t n) -> p t n", t=TILES)
        latent_kv = normed[:, 1, 0:2 * KV_LORA].rearrange("p (t n) -> p t n", t=TILES)
        at[0] = 0
        bc_t = take(4 * TOKENS, 4, TOKENS)
        xs_t = take(8 * TOKENS, 8, TOKENS)
        hankel = xs_t
        q_b = take(4 * TOKENS, 4, TOKENS)
        k_b = take(4 * TOKENS, 4, TOKENS)
        v_b = take(TILES * HALF, TILES, HALF)
        xdt = take(TILES * D, TILES, D)
        xdt_end = take(D)
        cb_diag = take(4 * P, 4, P)
        cb_off = take(2 * P, 2, P)
        prob_b = xdt[:, 0, 0:2 * 384].rearrange("p (a b) -> p a b", a=2)
        prob_t_b = xdt[:, 1, 0:2 * 384].rearrange("p (a b) -> p a b", a=2)
        dt_work = take(10 * 32, 10, 32)
        a_row = take(SSD_HEADS)
        dtb_row = take(SSD_HEADS)
        dskip_row = take(SSD_HEADS)
        y_tok = normed

        def adt_tile(tile):
            return dt_work[:, 8, tile * SSD_HEADS:(tile + 1) * SSD_HEADS]

        def nadt_tile(tile):
            return dt_work[:, 3, tile * SSD_HEADS:(tile + 1) * SSD_HEADS]

        head_max = sb("head_max", [P, 2, HEADS, 2])
        head_sum = sb("head_sum", [P, 2, HEADS, 2])

        x_landed, const_landed, out_landed = sem("x_landed"), sem("const_landed"), sem("out_landed")
        landed = [sem(f"landed{i}") for i in range(RING)]
        hi_done, lo_done, slab_used = sem("hi_done"), sem("lo_done"), sem("slab_used")
        act_step, dve_step, pool_step = sem("act_step"), sem("dve_step"), sem("pool_step")
        cols_turned, cols_ready, zeros_ready, pool_ready = (
            sem("cols_turned"), sem("cols_ready"), sem("zeros_ready"), sem("pool_ready"))

        class Sems:

            def __init__(self, part, names):
                self.s = {n: sem(f"{part}_{n}") for n in names.split()}

            def __getitem__(self, n):
                return self.s[n]

        NORMS = 8
        norm = [Sems(f"norm{b}", "rows stat rstd tok" + " resid" * (b >= 4)) if b else None for b in range(NORMS)]
        turned, operand_high, operand_low, tile0 = (
            sem("turned"), sem("operand_high"), sem("operand_low"), sem("tile0"))
        sc = Sems("sc", "c_copied ch_made conv0 y_made y_hi chunk")
        mlp = [Sems(f"mlp{i}", "relu squared hidden_hi chunk") for i in range(2)]
        glu = [Sems(f"glu{i}", "gate hidden hidden_hi chunk") for i in range(2)]
        mla = Sems("mla", "rows sumsq rstd latent turned t_hi t_lo pe q_out swapped rotated k_ps k_out v0 v1")
        att = [Sems(f"att{i}", "scores negmax probs normed turned t_out o_ps o_hi o_lo") for i in range(2)]
        hy = Sems("hy", "rows tap0 conv xbc dt_abs dt_exp adt qk_out v_out cum_ps decays xs_ps xdt "
                        "hank cb_ps cb_act cb seg_ps seg exp seg_w y_ps off_ps y_sum z_gate y_gated sumsq rstd y_n "
                        "y_ps_t y_hi y_lo")

        def up_view(w):
            return w.rearrange("(k p) n -> p k n", p=P)

        def up_chunks(w):
            return w.rearrange("(k p) (c f) -> p k c f", p=P, f=CHUNK_F)

        def down_chunks(w):
            return w.rearrange("(c j p) n -> p c j n", p=P, j=CT)

        def spread(v, n):
            return v.rearrange("(a n) -> a n", a=1).to_broadcast([P, n])

        def raw3(m, a, b):
            return raw[:, m % RING, 0:a * b].rearrange("p (a b) -> p a b", a=a)

        block = ctx.enter_context(nc.Block())

        @block.sync
        def _(sp):
            def load(m, dst, src):
                sp.dma_start(dst, src).then_inc(landed[m % RING], 16)

            def place_free(m):
                if m >= RING:
                    sp.wait_ge(lo_done, m - RING + 1)

            for tile in range(TILES):
                sp.dma_start(x_tok[:, tile, :], t["x"][0, tile * P:(tile + 1) * P, :]).then_inc(x_landed, 16)

            w_in = up_view(t["sc_w_in"][0])
            w_out = down_chunks(t["sc_w_out"][0])
            m = S_SC
            for c in range(SC_CHUNKS + 1):
                for part in range(3 if c < SC_CHUNKS else 0):
                    place_free(m)
                    f0 = part * D + c * CHUNK_F
                    load(m, raw3(m, KD, CHUNK_F), w_in[:, :, f0:f0 + CHUNK_F])
                    m += 1
                if c:
                    place_free(m)
                    load(m, raw3(m, CT, D), w_out[:, c - 1, :, :])
                    m += 1

            def mlp_weights(i):
                w1, w2 = up_chunks(t["ff_w1"][i]), down_chunks(t["ff_w2"][i])
                s = S_FF[i]

                def up_slab(m, c):
                    load(m, raw3(m, KD, CHUNK_F), w1[:, :, c, :])

                def down_slab(m, c):
                    load(m, raw3(m, CT, D), w2[:, c, :, :])

                place_free(s)
                up_slab(s, 0)
                with sp.Fori(0, FF_CHUNKS // 2 - 1) as it:
                    for j in range(4):
                        sp.wait_ge(lo_done, 4 * it + (s + 1 + j - RING + 1))
                        chunk = 2 * it + (1, 0, 2, 1)[j]
                        slot = (s + 1 + j) % RING
                        if j % 2 == 0:
                            sp.dma_start(raw3(slot, KD, CHUNK_F), w1[:, :, bass.ds(chunk, 1), :])\
                              .then_inc(landed[slot], 16)
                        else:
                            sp.dma_start(raw3(slot, CT, D), w2[:, bass.ds(chunk, 1), :, :])\
                              .then_inc(landed[slot], 16)
                e = s + N_FF - 3
                place_free(e)
                up_slab(e, FF_CHUNKS - 1)
                place_free(e + 1)
                down_slab(e + 1, FF_CHUNKS - 2)
                place_free(e + 2)
                down_slab(e + 2, FF_CHUNKS - 1)

            def glu_weights(i):
                name = ("ffn1", "ffn2")[i]
                wg, wu = up_chunks(t[f"{name}_w_gate_2"][0]), up_chunks(t[f"{name}_w_up_2"][0])
                wd = down_chunks(t[f"{name}_w_down_2"][0])
                s = S_SG[i]
                for j, w in enumerate((wg, wu)):
                    place_free(s + j)
                    load(s + j, raw3(s + j, KD, CHUNK_F), w[:, :, 0, :])
                with sp.Fori(0, (SG_CHUNKS - 1) // 2) as it:
                    for j in range(8):
                        sp.wait_ge(lo_done, 8 * it + (s + 2 + j - RING + 1))
                        slot = (s + 2 + j) % RING
                        c = 2 * it + j // 4
                        if j % 4 < 2:
                            sp.dma_start(raw3(slot, KD, CHUNK_F), (wg, wu)[j % 4][:, :, bass.ds(c + 1, 1), :])\
                              .then_inc(landed[slot], 16)
                        else:
                            sp.dma_start(raw3(slot, 1, D), wd[:, bass.ds(c, 1), j % 4 - 2, :])\
                              .then_inc(landed[slot], 16)
                for j in range(2):
                    e = s + N_SG - 2 + j
                    place_free(e)
                    load(e, raw3(e, 1, D), wd[:, SG_CHUNKS - 1, j:j + 1, :])

            mlp_weights(0)

            w = up_view(t["mla_w_dq"][0])
            for j in range(2):
                place_free(DQ + j)
                load(DQ + j, raw3(DQ + j, 4, Q_LORA), w[:, 4 * j:4 * j + 4, :])
            w = up_view(t["mla_w_dkv"][0])
            for j in range(2):
                place_free(KV + j)
                dst = raw3(KV + j, 4, KV_COLS)
                load(KV + j, dst[:, :, 0:KV_LORA + ROPE], w[:, 4 * j:4 * j + 4, :])
                load(KV + j, dst[:, :, KV_LORA + ROPE:], w[:, 4 * j:4 * j + 4, KV_LORA:])
            w = up_view(t["mla_w_uq"][0]).rearrange("p k (h c) -> p k h c", h=HEADS)
            for j in range(4):
                place_free(UQ + j)
                dst = raw3(UQ + j, KQ, UQ_COLS)
                for h in range(2):
                    load(UQ + j, dst[:, :, h * NOPE:(h + 1) * NOPE], w[:, :, 2 * j + h, 0:NOPE])
                    r0 = 2 * NOPE + h * ROPE
                    load(UQ + j, dst[:, :, r0:r0 + ROPE], w[:, :, 2 * j + h, NOPE:])
            for m, name in ((UK, "mla_w_uk"), (UV, "mla_w_uv")):
                place_free(m)
                load(m, raw3(m, KKV, D), t[name][0].rearrange("(k p) h d -> p k (h d)", p=P))
            w = down_chunks(t["mla_w_o"][0])
            for j in range(4):
                place_free(WO + j)
                load(WO + j, raw3(WO + j, CT, D), w[:, j, :, :])

            mlp_weights(1)
            glu_weights(0)

            w = up_view(t["w_in_2"][0])
            for j in range(6):
                place_free(HX + j)
                load(HX + j, raw3(HX + j, KD, CHUNK_F), w[:, :, XBC0 + j * CHUNK_F:XBC0 + (j + 1) * CHUNK_F])
            place_free(HDT)
            load(HDT, raw3(HDT, KD, SSD_HEADS), w[:, :, DT0:DT0 + SSD_HEADS])
            for j in range(4):
                place_free(HQK + j)
                load(HQK + j, raw3(HQK + j, KD, CHUNK_F), w[:, :, Q0 + j * CHUNK_F:Q0 + (j + 1) * CHUNK_F])
            for j in range(2):
                place_free(HV + j)
                load(HV + j, raw3(HV + j, 4, HALF), w[:, 4 * j:4 * j + 4, V0:V0 + HALF])
            for j in range(4):
                place_free(HZ + j)
                f0 = Z0 + (j // 2) * HALF
                load(HZ + j, raw3(HZ + j, 4, HALF), w[:, 4 * (j % 2):4 * (j % 2) + 4, f0:f0 + HALF])
            w = down_chunks(t["w_out_2"][0])
            for j in range(6):
                place_free(HWO + j)
                load(HWO + j, raw3(HWO + j, CT, D), w[:, (4, 5, 0, 1, 2, 3)[j], :, :])

            glu_weights(1)

            for tile in range(TILES):
                sp.wait_ge(norm[7]["tok"], tile + 1)
                sp.dma_start(out[0, tile * P:(tile + 1) * P, :], normed[:, tile, :]).then_inc(out_landed, 16)
            sp.wait_ge(out_landed, 16 * TILES)

        @block.gpsimd
        def _(pool):
            steps = [0]

            def then(ins):
                steps[0] += 1
                ins.then_inc(pool_step, 1)
                pool.wait_ge(pool_step, steps[0])

            pool.dma_start(cst[:, :], consts).then_inc(const_landed, 16)
            pool.dma_start(rows[ROW_SC:ROW_XBC, :], t["sc_conv_w"][0].rearrange("k (f p) -> (k f) p", p=P))\
                .then_inc(const_landed, 16)
            pool.dma_start(rows[ROW_XBC:ROW_XBC_B, :], t["conv_w_2"][0].rearrange("k (f p) -> (k f) p", p=P))\
                .then_inc(const_landed, 16)
            pool.dma_start(rows[ROW_XBC_B:ROWS, :], t["conv_b_2"][0].rearrange("(f p) -> f p", p=P))\
                .then_inc(const_landed, 16)
            nc.gpsimd.memset(zeros[:, :], 0.0).then_inc(zeros_ready, 1)
            then(nc.gpsimd.memset(half_neg[:, :], -0.5))

            def norm_rows(b, *pairs):
                for dst, v, n in pairs:
                    pool.dma_start(dst, spread(v, n)).then_inc(norm[b]["rows"], 16)

            def inverse_root(dst, src, mult, eps):
                n = dst.shape[-1]
                then(nc.gpsimd.tensor_scalar(dst, src, mult, eps, ALU.mult, ALU.add))
                return nc.gpsimd.tensor_tensor(dst, dst, half_neg[:, :].to_broadcast([P, n]), ALU.pow)

            def layer_norm_root(b):
                for tile in range(TILES):
                    pool.wait_ge(norm[b]["stat"], tile + 1)
                    inverse_root(rstd[:, tile:tile + 1], mean_var[:, tile, 1:2], 1.0, LN_EPS)\
                        .then_inc(norm[b]["rstd"], 1)

            norm_rows(1, (gain[:, :], t["ln_mix_g"][0], D), (bias[:, :], t["ln_mix_b"][0], D))
            layer_norm_root(1)
            pool.wait_ge(norm[1]["tok"], TILES)
            norm_rows(2, (gain[:, :], t["ln_ff_g"][0], D), (bias[:, :], t["ln_ff_b"][0], D))
            layer_norm_root(2)

            pool.dma_start(g_q, spread(t["mla_g_q"][0], Q_LORA)).then_inc(mla["rows"], 16)
            pool.dma_start(g_kv, spread(t["mla_g_kv"][0], KV_LORA)).then_inc(mla["rows"], 16)
            pool.wait_ge(norm[2]["tok"], TILES)
            norm_rows(3, (gain[:, :], t["ln_mix_g"][1], D), (bias[:, :], t["ln_mix_b"][1], D))
            pool.wait_ge(mla["sumsq"], 2 * TILES)
            inverse_root(rstd[:, 0:2], sumsq[:, 0:2], 1.0 / Q_LORA, MLA_EPS).then_inc(mla["rstd"], 1)
            inverse_root(rstd[:, 2:4], sumsq[:, 2:4], 1.0 / KV_LORA, MLA_EPS).then_inc(mla["rstd"], 1)
            layer_norm_root(3)

            pool.wait_ge(norm[3]["tok"], TILES)
            norm_rows(4, (gain[:, :], t["ln_ff_g"][1], D), (bias[:, :], t["ln_ff_b"][1], D),
                      (gain2[:, :], t["ffn1_norm_2"][0], D))
            layer_norm_root(4)

            def rms_root(b, first):
                for tile in range(TILES):
                    pool.wait_ge(norm[b]["stat"], first + tile + 1)
                    inverse_root(rstd[:, 2 + tile:3 + tile], sumsq[:, tile:tile + 1], 1.0 / D, RMS_EPS)\
                        .then_inc(norm[b]["rstd"], 1)

            rms_root(4, TILES)
            pool.wait_ge(norm[4]["tok"], TILES)
            norm_rows(5, (gain[:, :], t["mix_norm_2"][0], D))
            pool.dma_start(gain2[:, :], spread(t["ssd_norm_2"][0], D)).then_inc(hy["rows"], 16)
            rms_root(5, 0)

            pool.dma_start(a_row, spread(t["a_log_2"][0], SSD_HEADS)).then_inc(hy["rows"], 16)
            pool.dma_start(dtb_row, spread(t["dt_bias_2"][0], SSD_HEADS)).then_inc(hy["rows"], 16)
            pool.dma_start(dskip_row, spread(t["d_skip_2"][0], SSD_HEADS)).then_inc(hy["rows"], 16)
            pool.wait_ge(norm[5]["tok"], TILES)
            norm_rows(6, (gain[:, :], t["ffn2_norm_2"][0], D))
            pool.wait_ge(hy["xdt"], 4)
            rel = t["rel_bias_2"][0]
            for h in range(HEADS):
                window = bass.AP(rel.tensor, rel.offset + h * REL + P + 1, [[1, P], [1, TOKENS]])
                pool.dma_start(hankel[:, h, :], window).then_inc(hy["hank"], 16)
            for tile in range(TILES):
                pool.wait_ge(hy["sumsq"], tile + 1)
                inverse_root(rstd[:, tile:tile + 1], sumsq[:, 2 + tile:3 + tile], 1.0 / D, RMS_EPS)\
                    .then_inc(hy["rstd"], 1)
            rms_root(6, 0)
            pool.wait_ge(norm[6]["tok"], TILES)
            norm_rows(7, (gain[:, :], t["final_norm_2"], D))
            rms_root(7, 0)

        @block.scalar
        def _(act):
            steps = [0]

            def then(ins):
                steps[0] += 1
                ins.then_inc(act_step, 1)
                act.wait_ge(act_step, steps[0])

            def copy(dst, src, **kw):
                return nc.scalar.activation(dst, src, ACT.Copy, **kw)

            def round_slab(m):
                if m >= N_SLABS:
                    return
                act.wait_ge(landed[m % RING], landed_at[m])
                if m >= RING:
                    act.wait_ge(slab_used, m - RING + 1)
                copy(weight_hi[:, m % RING, 0:width[m]], raw[:, m % RING, 0:width[m]]).then_inc(hi_done, 1)

            def round_slab_at(m, off):
                act.wait_ge(landed[m % RING], off * (16 // RING) + landed_at[m])
                act.wait_ge(slab_used, off + (m - RING + 1))
                copy(weight_hi[:, m % RING, 0:width[m]], raw[:, m % RING, 0:width[m]]).then_inc(hi_done, 1)

            def operand_hi(b):
                for g in range(4):
                    tile, h = g // 2, g % 2
                    act.wait_ge(turned, 4 * b + g + 1)
                    copy(xh[:, 4 * h:4 * h + 4, tile * P:(tile + 1) * P],
                         up[g][:, :].rearrange("p (k n) -> p k n", k=4)).then_inc(operand_high, 1)

            def square_sums(b):
                for tile in range(TILES):
                    act.wait_ge(norm[b]["resid"], tile + 1)
                    nc.scalar.activation(normed[:, tile, :], x_tok[:, tile, :], ACT.Square,
                                         accum_out=sumsq[:, tile:tile + 1])\
                        .then_inc(norm[b]["stat"], 1)

            for m in range(RING):
                round_slab(m)
            operand_hi(0)
            act.wait_ge(cols_turned, 1)
            copy(cols[:, :], up[3][:, 0:ROWS]).then_inc(cols_ready, 1)

            act.wait_ge(cols_ready, 1)
            m = S_SC
            for c in range(SC_CHUNKS + 1):
                if c < SC_CHUNKS:
                    round_slab(m + RING)
                    act.wait_ge(slab_used, m + 2)
                    if c:
                        act.wait_ge(sc["ch_made"], c)
                    copy(tmp_a[:, :], up[1][:, :]).then_inc(sc["c_copied"], 1)
                    round_slab(m + 1 + RING)
                    round_slab(m + 2 + RING)
                    act.wait_ge(sc["ch_made"], c + 1)
                    if c:
                        act.wait_ge(sc["y_made"], c)
                    for f in range(CT):
                        tap = cols[:, ROW_SC + (SC_TAPS - 1) * KD + CT * c + f:][:, 0:1]
                        nc.scalar.activation(tmp_c[:, f * TOKENS:(f + 1) * TOKENS],
                                             tmp_b[:, f * TOKENS:(f + 1) * TOKENS], ACT.Copy, scale=tap)\
                            .then_inc(sc["conv0"], 1)
                    act.wait_ge(sc["y_made"], c + 1)
                    copy(hh[:, CT * (c % 2):CT * (c % 2) + CT, :],
                         tmp_d[:, :].rearrange("p (f n) -> p f n", f=CT)).then_inc(sc["y_hi"], 1)
                    m += 3
                if c:
                    round_slab(m + RING)
                    m += 1

            def mlp_part(i):
                s, q = S_FF[i], mlp[i]

                def relu(c, par):
                    nc.scalar.activation(tmp_a[:, :], up[par][:, :], ACT.Relu).then_inc(q["relu"], 1)

                def hidden_hi(par):
                    copy(hh[:, CT * par:CT * par + CT, :], tmp_b[:, :].rearrange("p (f n) -> p f n", f=CT))\
                        .then_inc(q["hidden_hi"], 1)

                act.wait_ge(slab_used, s + 1)
                relu(0, 0)
                round_slab(s + RING)
                act.wait_ge(q["squared"], 1)
                hidden_hi(0)
                with act.Fori(0, FF_CHUNKS // 2 - 1) as it:
                    for j in range(4):
                        n = s + 1 + j
                        if j % 2 == 0:
                            par = (1, 0)[j // 2]
                            act.wait_ge(slab_used, 4 * it + (n + 1))
                            act.wait_ge(q["chunk"], 2 * it + (1 + j // 2))
                            relu(0, par)
                        round_slab_at(n + RING, 4 * it)
                        if j % 2 == 0:
                            act.wait_ge(q["squared"], 2 * it + (2 + j // 2))
                            hidden_hi(par)
                n = s + N_FF - 3
                act.wait_ge(slab_used, n + 1)
                act.wait_ge(q["chunk"], FF_CHUNKS - 1)
                relu(0, 1)
                round_slab(n + RING)
                act.wait_ge(q["squared"], FF_CHUNKS)
                hidden_hi(1)
                round_slab(n + 1 + RING)
                round_slab(n + 2 + RING)

            def glu_part(i):
                s, q = S_SG[i], glu[i]

                def gate(par):
                    nc.scalar.activation(tmp_a[:, :], up[2 * par][:, :], ACT.Silu).then_inc(q["gate"], 1)

                def hidden_hi(par):
                    copy(hh[:, CT * par:CT * par + CT, :], tmp_b[:, :].rearrange("p (f n) -> p f n", f=CT))\
                        .then_inc(q["hidden_hi"], 1)

                act.wait_ge(slab_used, s + 1)
                gate(0)
                round_slab(s + RING)
                round_slab(s + 1 + RING)
                act.wait_ge(q["hidden"], 1)
                hidden_hi(0)
                def two_chunks(off, chunk, rounded):
                    for j in range(8):
                        n = s + 2 + j
                        par = (1, 0)[j // 4]
                        if j % 4 == 0:
                            act.wait_ge(slab_used, off + (n + 1))
                            act.wait_ge(q["chunk"], chunk + (1 + j // 4))
                            gate(par)
                        rounded(n + RING)
                        if j % 4 == 1:
                            act.wait_ge(q["hidden"], chunk + (2 + j // 4))
                            hidden_hi(par)

                with act.Fori(0, GLU_PASSES) as it:
                    two_chunks(8 * it, 2 * it, lambda m: round_slab_at(m, 8 * it))
                two_chunks(8 * GLU_PASSES, 2 * GLU_PASSES, lambda m: round_slab(m + 8 * GLU_PASSES))
                for j in range(2):
                    round_slab(s + N_SG - 2 + j + RING)

            operand_hi(1)
            mlp_part(0)
            operand_hi(2)

            for m in (DQ, DQ + 1, KV, KV + 1):
                round_slab(m + RING)
            act.wait_ge(slab_used, KV + 2)
            copy(pe_raw[:, 0, :], up[0][:, 0:TOKENS]).then_inc(mla["pe"], 1)
            for tile in range(TILES):
                if tile:
                    act.wait_ge(mla["sumsq"], 1)
                nc.scalar.activation(tmp_a[:, 0:Q_LORA], acc[:, 2 * tile, 0:Q_LORA], ACT.Square,
                                     accum_out=sumsq[:, tile:tile + 1]).then_inc(mla["sumsq"], 1)
                if tile:
                    act.wait_ge(mla["sumsq"], 2)
                nc.scalar.activation(tmp_b[:, tile * KV_LORA:(tile + 1) * KV_LORA], acc[:, 2 * tile + 1, 0:KV_LORA],
                                     ACT.Square, accum_out=sumsq[:, 2 + tile:3 + tile]).then_inc(mla["sumsq"], 1)
            for g, (k, n) in enumerate(((0, 2), (2, 1), (3, 2))):
                act.wait_ge(mla["turned"], g + 1)
                copy(xh[:, k:k + n, :], acc[:, g, 0:n * TOKENS].rearrange("p (k n) -> p k n", k=n))\
                    .then_inc(mla["t_hi"], 1)
            for j in range(4):
                act.wait_ge(slab_used, UQ + j + 1)
                if j:
                    act.wait_ge(mla["rotated"], j)
                copy(pe_raw[:, (j + 1) % 2, :], up[2 + j % 2][:, 0:TOKENS]).then_inc(mla["pe"], 1)
                copy(q_nope[:, 2 * j:2 * j + 2, :], up[j % 2][:, :].rearrange("p (h n) -> p h n", h=2))\
                    .then_inc(mla["q_out"], 1)
                round_slab(UQ + j + RING)
            for j in range(4):
                if j < 3:
                    act.wait_ge(mla["k_ps"], j + 1)
                else:
                    act.wait_ge(slab_used, UK + 1)
                copy(k_nope[:, 2 * j:2 * j + 2, :], up[j][:, :].rearrange("p (h n) -> p h n", h=2))\
                    .then_inc(mla["k_out"], 1)
            round_slab(UK + RING)
            act.wait_ge(slab_used, UV + 1)
            copy(v_a[:, 0, :].rearrange("p (h n) -> p h n", h=2), acc[:, 0:2, :]).then_inc(mla["v0"], 1)
            round_slab(UV + RING)

            def attention_part(i, scale, prob, prob_t, o_hi, o_tiles):
                q = att[i]
                for h in range(HEADS + 2):
                    if h < HEADS:
                        act.wait_ge(q["negmax"], h + 1)
                        if h >= 2:
                            act.wait_ge(q["turned"], h - 1)
                        S = up[h % 4]
                        nc.scalar.activation(prob[:, h % 2, 0:P], S[:, 0:P], ACT.Exp, scale=scale,
                                             bias=head_max[:, 1, h, 0:1], accum_out=head_sum[:, 0, h, 0:1])\
                            .then_inc(q["probs"], 1)
                        nc.scalar.activation(prob[:, h % 2, P:384], S[:, P:384], ACT.Exp, scale=scale,
                                             bias=head_max[:, 1, h, 1:2], accum_out=head_sum[:, 0, h, 1:2])\
                            .then_inc(q["probs"], 1)
                    if 1 <= h <= HEADS:
                        g = h - 1
                        act.wait_ge(q["turned"], g + 1)
                        if g >= 2:
                            act.wait_ge(q["o_ps"], g - 1)
                        copy(prob_t[:, g % 2, :], acc[:, g % 2, 0:384]).then_inc(q["t_out"], 1)
                    if h >= 2:
                        g = h - 2
                        act.wait_ge(q["o_ps"], g + 1)
                        dst, src = o_tiles(g)
                        copy(o_hi(dst), src).then_inc(q["o_hi"], 1)

            def mla_out(g):
                return (slice(0, P), g), acc[:, 2 + g % 2, 0:TOKENS]

            attention_part(0, QK_SCALE, prob_a, prob_t_a, lambda d: xh[d[0], d[1], :], mla_out)
            for j in range(4):
                round_slab(WO + j + RING)
            operand_hi(3)

            mlp_part(1)
            square_sums(4)
            operand_hi(4)
            glu_part(0)
            square_sums(5)
            operand_hi(5)

            for j in range(6):
                act.wait_ge(slab_used, HX + j + 1)
                cy = (tmp_a, tmp_b)[j % 2]
                if j >= 2:
                    act.wait_ge(hy["xbc"], j - 1)
                for f in range(CT):
                    ft = CT * j + f
                    nc.scalar.activation(
                        cy[:, f * TOKENS:(f + 1) * TOKENS], up[j % 2][:, f * TOKENS:(f + 1) * TOKENS], ACT.Identity,
                        scale=cols[:, ROW_XBC + (XBC_TAPS - 1) * XT + ft:][:, 0:1],
                        bias=cols[:, ROW_XBC_B + ft:][:, 0:1]).then_inc(hy["tap0"], 1)
                round_slab(HX + j + RING)
                act.wait_ge(hy["conv"], j + 1)
                dst = xs_t[:, CT * j:CT * j + CT, :] if j < 4 else bc_t[:, CT * (j - 4):CT * (j - 4) + CT, :]
                nc.scalar.activation(dst, cy[:, :].rearrange("p (f n) -> p f n", f=CT), ACT.Silu)\
                    .then_inc(hy["xbc"], 1)
            round_slab(HDT + RING)
            act.wait_ge(hy["dt_abs"], 1)
            nc.scalar.activation(dt_work[:, 2, :], dt_work[:, 1, :], ACT.Exp).then_inc(hy["dt_exp"], 1)
            act.wait_ge(hy["rows"], 64)
            nc.scalar.activation(dt_work[:, 9, 0:SSD_HEADS], a_row, ACT.Exp).then_inc(hy["dt_exp"], 1)
            for j in range(4):
                act.wait_ge(slab_used, HQK + j + 1)
                dst = (q_b, k_b)[j // 2][:, CT * (j % 2):CT * (j % 2) + CT, :]
                copy(dst, up[j % 2][:, :].rearrange("p (f n) -> p f n", f=CT),
                     scale=(float(ATT_HD) ** -0.5 if j < 2 else 1.0)).then_inc(hy["qk_out"], 1)
                round_slab(HQK + j + RING)
            for tile in range(TILES):
                act.wait_ge(slab_used, HV + 2)
                copy(v_b[:, tile, :], acc[:, tile, :]).then_inc(hy["v_out"], 1)
            for j in range(2):
                round_slab(HV + j + RING)
            act.wait_ge(hy["cum_ps"], 1)
            nc.scalar.activation(dt_work[:, 7, :], acc[:, 2, 0:32], ACT.Exp).then_inc(hy["decays"], 1)
            for g in range(SSD_GROUPS):
                act.wait_ge(hy["cb_ps"], g + 1)
                copy(cb_off[:, g, :], acc[:, g, P:2 * P]).then_inc(hy["cb_act"], 1)
            for n in range(8):
                act.wait_ge(hy["seg"], n + 1)
                if n >= 2:
                    act.wait_ge(hy["y_ps"], n - 1)
                nc.scalar.activation((tmp_c, tmp_d)[n % 2][:, :], (tmp_a, tmp_b)[n % 2][:, :], ACT.Exp)\
                    .then_inc(hy["exp"], 1)
            for j in range(4):
                act.wait_ge(slab_used, HZ + j + 1)
                if j % 2:
                    for tile in range(TILES):
                        n = j // 2 * TILES + tile
                        if n >= 2:
                            act.wait_ge(hy["y_gated"], n - 1)
                        nc.scalar.activation((tmp_a, tmp_b)[n % 2][:, :], acc[:, 2 * tile + j // 2, :], ACT.Silu)\
                            .then_inc(hy["z_gate"], 1)
                round_slab(HZ + j + RING)
            for tile in range(TILES):
                act.wait_ge(hy["y_gated"], 3 + tile)
                if tile:
                    act.wait_ge(hy["sumsq"], 1)
                nc.scalar.activation(xdt_end, y_tok[:, tile, :], ACT.Square,
                                     accum_out=sumsq[:, 2 + tile:3 + tile]).then_inc(hy["sumsq"], 1)

            def hybrid_out(g):
                o = ATT_HD * (g % 2)
                return (slice(o, o + ATT_HD), g // 2), acc[o:o + ATT_HD, 2 + g % 2, 0:TOKENS]

            attention_part(1, 1.0, prob_b, prob_t_b, lambda d: hh[d[0], d[1], :], hybrid_out)
            for g in range(4):
                act.wait_ge(hy["y_ps_t"], g + 1)
                copy(xh[:, 4 * (g % 2):4 * (g % 2) + 4, (g // 2) * P:(g // 2 + 1) * P],
                     up[g][:, :].rearrange("p (k n) -> p k n", k=4)).then_inc(hy["y_hi"], 1)
            for j in range(6):
                round_slab(HWO + j + RING)
            square_sums(6)
            operand_hi(6)
            glu_part(1)
            square_sums(7)

        @block.vector
        def _(dve):
            steps = [0]
            vec = nc.vector

            def then(ins):
                steps[0] += 1
                ins.then_inc(dve_step, 1)
                dve.wait_ge(dve_step, steps[0])

            def rest(dst, whole, high):
                return vec.tensor_tensor(dst, whole, high.bitcast(F32), ALU.subtract)

            def split_slab(m):
                if m >= N_SLABS:
                    return
                dve.wait_ge(hi_done, m + 1)
                w = width[m]
                rest(weight_lo[:, m % RING, 0:w], raw[:, m % RING, 0:w], weight_hi[:, m % RING, 0:w])\
                    .then_inc(lo_done, 1)

            def split_slab_at(m, off):
                dve.wait_ge(hi_done, off + (m + 1))
                w = width[m]
                rest(weight_lo[:, m % RING, 0:w], raw[:, m % RING, 0:w], weight_hi[:, m % RING, 0:w])\
                    .then_inc(lo_done, 1)

            def halves(a):
                return a.rearrange("p (h n) -> p h n", h=2)

            def operand_lo(b):
                for g in range(4):
                    tile, h = g // 2, g % 2
                    dve.wait_ge(operand_high, 4 * b + g + 1)
                    rest(xl[:, 4 * h:4 * h + 4, tile * P:(tile + 1) * P],
                         up[g][:, :].rearrange("p (k n) -> p k n", k=4),
                         xh[:, 4 * h:4 * h + 4, tile * P:(tile + 1) * P]).then_inc(operand_low, 1)

            def product_done(b, tile, last):
                if tile == 0:
                    dve.wait_ge(tile0, b)
                else:
                    dve.wait_ge(slab_used, last + 1)

            def layer_norm(b, last, rows_landed, ready):
                for tile in range(TILES):
                    product_done(b, tile, last)
                    x = x_tok[:, tile, :]
                    then(vec.scalar_tensor_tensor(halves(x), halves(x), ALPHA, acc[:, 2 * tile:2 * tile + 2, :],
                                                  ALU.mult, ALU.add))
                    vec.bn_stats(stat[:, tile, 0, :], x[:, 0:HALF])
                    then(vec.bn_stats(stat[:, tile, 1, :], x[:, HALF:D]))
                    vec.bn_aggr(mean_var[:, tile, :], stat[:, tile, :, :].rearrange("p a b -> p (a b)"))\
                        .then_inc(norm[b]["stat"], 1)
                for tile in range(TILES):
                    x = x_tok[:, tile, :]
                    dve.wait_ge(norm[b]["rstd"], tile + 1)
                    then(vec.tensor_scalar(x, x, mean_var[:, tile, 0:1], rstd[:, tile:tile + 1],
                                           ALU.subtract, ALU.mult))
                    dve.wait_ge(norm[b]["rows"], rows_landed)
                    then(vec.tensor_tensor(x, x, gain[:, :], ALU.mult))
                    vec.tensor_tensor(x, x, bias[:, :], ALU.add).then_inc(norm[b][ready], 1)

            def add_product(b, last, factor):
                for tile in range(TILES):
                    product_done(b, tile, last)
                    x = halves(x_tok[:, tile, :])
                    vec.scalar_tensor_tensor(x, acc[:, 2 * tile:2 * tile + 2, :], factor, x, ALU.mult, ALU.add)\
                        .then_inc(norm[b]["resid"], 1)

            def rms_norm(b, row, roots_before, rows_landed):
                for tile in range(TILES):
                    dve.wait_ge(norm[b]["rstd"], roots_before + tile + 1)
                    dve.wait_ge(norm[b]["rows"], rows_landed)
                    vec.scalar_tensor_tensor(normed[:, tile, :], x_tok[:, tile, :], rstd[:, 2 + tile:3 + tile], row,
                                             ALU.mult, ALU.mult).then_inc(norm[b]["tok"], 1)

            for m in range(RING):
                split_slab(m)
            operand_lo(0)

            dve.wait_ge(cols_ready, 1)
            m = S_SC
            for c in range(SC_CHUNKS + 1):
                if c < SC_CHUNKS:
                    split_slab(m + RING)
                    split_slab(m + 1 + RING)
                    dve.wait_ge(slab_used, m + 3)
                    dve.wait_ge(sc["c_copied"], c + 1)
                    vec.tensor_tensor(tmp_b[:, :], up[2][:, :], tmp_a[:, :], ALU.mult).then_inc(sc["ch_made"], 1)
                    split_slab(m + 2 + RING)
                    dve.wait_ge(sc["conv0"], CT * (c + 1))
                    for back in (1, 2):
                        for f in range(CT):
                            o = f * TOKENS
                            row = ROW_SC + (SC_TAPS - 1 - back) * KD + CT * c + f
                            ins = vec.scalar_tensor_tensor(
                                tmp_c[:, o + back:o + TOKENS], tmp_b[:, o:o + TOKENS - back], cols[:, row:row + 1],
                                tmp_c[:, o + back:o + TOKENS], ALU.mult, ALU.add)
                        then(ins)
                    b_bank = up[3 if c % 2 else 0]
                    vec.tensor_tensor(tmp_d[:, :], b_bank[:, :], tmp_c[:, :], ALU.mult).then_inc(sc["y_made"], 1)
                    dve.wait_ge(sc["y_hi"], c + 1)
                    rest(hl[:, CT * (c % 2):CT * (c % 2) + CT, :], tmp_d[:, :].rearrange("p (f n) -> p f n", f=CT),
                         hh[:, CT * (c % 2):CT * (c % 2) + CT, :]).then_inc(sc["chunk"], 1)
                    m += 3
                if c:
                    split_slab(m + RING)
                    m += 1
            layer_norm(1, S_SC + N_SC - 1, 32, "tok")
            operand_lo(1)

            def hidden_lo(par):
                return rest(hl[:, CT * par:CT * par + CT, :], tmp_b[:, :].rearrange("p (f n) -> p f n", f=CT),
                            hh[:, CT * par:CT * par + CT, :])

            def mlp_part(i):
                s, q = S_FF[i], mlp[i]

                def square():
                    vec.tensor_tensor(tmp_b[:, :], tmp_a[:, :], tmp_a[:, :], ALU.mult).then_inc(q["squared"], 1)

                dve.wait_ge(q["relu"], 1)
                square()
                split_slab(s + RING)
                dve.wait_ge(q["hidden_hi"], 1)
                hidden_lo(0).then_inc(q["chunk"], 1)
                with dve.Fori(0, FF_CHUNKS // 2 - 1) as it:
                    for j in range(4):
                        n = s + 1 + j
                        par = (1, 0)[j // 2]
                        if j % 2 == 0:
                            dve.wait_ge(q["relu"], 2 * it + (2 + j // 2))
                            square()
                        split_slab_at(n + RING, 4 * it)
                        if j % 2 == 0:
                            dve.wait_ge(q["hidden_hi"], 2 * it + (2 + j // 2))
                            hidden_lo(par).then_inc(q["chunk"], 1)
                n = s + N_FF - 3
                dve.wait_ge(q["relu"], FF_CHUNKS)
                square()
                split_slab(n + RING)
                dve.wait_ge(q["hidden_hi"], FF_CHUNKS)
                hidden_lo(1).then_inc(q["chunk"], 1)
                split_slab(n + 1 + RING)
                split_slab(n + 2 + RING)

            def glu_part(i):
                s, q = S_SG[i], glu[i]

                def gated(par):
                    vec.tensor_tensor(tmp_b[:, :], up[2 * par + 1][:, :], tmp_a[:, :], ALU.mult)\
                        .then_inc(q["hidden"], 1)

                split_slab(s + RING)
                dve.wait_ge(slab_used, s + 2)
                dve.wait_ge(q["gate"], 1)
                gated(0)
                split_slab(s + 1 + RING)
                dve.wait_ge(q["hidden_hi"], 1)
                hidden_lo(0).then_inc(q["chunk"], 1)

                def two_chunks(off, chunk, split):
                    for j in range(8):
                        n = s + 2 + j
                        par = (1, 0)[j // 4]
                        if j % 4 == 1:
                            dve.wait_ge(slab_used, off + (n + 1))
                            dve.wait_ge(q["gate"], chunk + (2 + j // 4))
                            gated(par)
                        split(n + RING)
                        if j % 4 == 1:
                            dve.wait_ge(q["hidden_hi"], chunk + (2 + j // 4))
                            hidden_lo(par).then_inc(q["chunk"], 1)

                with dve.Fori(0, GLU_PASSES) as it:
                    two_chunks(8 * it, 2 * it, lambda m: split_slab_at(m, 8 * it))
                two_chunks(8 * GLU_PASSES, 2 * GLU_PASSES, lambda m: split_slab(m + 8 * GLU_PASSES))
                for j in range(2):
                    split_slab(s + N_SG - 2 + j + RING)

            mlp_part(0)
            layer_norm(2, S_FF[0] + N_FF - 1, 32, "tok")
            operand_lo(2)

            for m in (DQ, DQ + 1, KV, KV + 1):
                split_slab(m + RING)
            dve.wait_ge(mla["rows"], 32)
            dve.wait_ge(mla["rstd"], 2)
            for tile in range(TILES):
                vec.scalar_tensor_tensor(latent_q[:, tile, :], acc[:, 2 * tile, 0:Q_LORA], rstd[:, tile:tile + 1], g_q,
                                         ALU.mult, ALU.mult).then_inc(mla["latent"], 1)
                vec.scalar_tensor_tensor(latent_kv[:, tile, :], acc[:, 2 * tile + 1, 0:KV_LORA],
                                         rstd[:, 2 + tile:3 + tile], g_kv, ALU.mult, ALU.mult)\
                    .then_inc(mla["latent"], 1)

            def rotate(r, dst):
                dve.wait_ge(mla["swapped"], r + 1)
                if r >= 1:
                    dve.wait_ge(mla["rotated"], r)
                vec.tensor_tensor(tmp_c[:, 0:TOKENS], pe_raw[:, r % 2, :], cos, ALU.mult)
                then(vec.tensor_tensor(tmp_d[:, 0:TOKENS], acc[:, 3, 0:TOKENS], sin, ALU.mult))
                vec.tensor_tensor(dst, tmp_c[:, 0:TOKENS], tmp_d[:, 0:TOKENS], ALU.add).then_inc(mla["rotated"], 1)

            for g, (k, n) in enumerate(((0, 2), (2, 1), (3, 2))):
                dve.wait_ge(mla["t_hi"], g + 1)
                rest(xl[:, k:k + n, :], acc[:, g, 0:n * TOKENS].rearrange("p (k n) -> p k n", k=n), xh[:, k:k + n, :])\
                    .then_inc(mla["t_lo"], 1)
            rotate(0, k_rot)
            for j in range(4):
                split_slab(UQ + j + RING)
                rotate(j + 1, q_rot[:, j, :])
            split_slab(UK + RING)
            dve.wait_ge(slab_used, UV + 1)
            vec.tensor_copy(halves(v_a[:, 1, :]), acc[:, 2:4, :]).then_inc(mla["v1"], 1)
            split_slab(UV + RING)

            def attention_part(i, scale, prob, o_part, o_lo, o_hi):
                q = att[i]
                for h in range(HEADS + 2):
                    if h < HEADS:
                        dve.wait_ge(q["scores"], h + 1)
                        S = up[h % 4]
                        vec.reduce_max(head_max[:, 0, h, 0:1], S[:, 0:P], axis=AX_X)
                        then(vec.reduce_max(head_max[:, 0, h, 1:2], S[:, P:384], axis=AX_X))
                        vec.tensor_scalar(head_max[:, 1, h, :], head_max[:, 0, h, :], -scale, None, ALU.mult)\
                            .then_inc(q["negmax"], 1)
                    if 1 <= h <= HEADS:
                        g = h - 1
                        dve.wait_ge(q["probs"], 2 * g + 2)
                        then(vec.reciprocal(head_sum[:, 1, g, :], head_sum[:, 0, g, :]))
                        for a, b, n in ((0, P, 0), (P, 384, 1)):
                            vec.tensor_scalar(prob[:, g % 2, a:b], prob[:, g % 2, a:b], head_sum[:, 1, g, n:n + 1], None,
                                              ALU.mult).then_inc(q["normed"], 1)
                    if h >= 2:
                        g = h - 2
                        dve.wait_ge(q["o_hi"], g + 1)
                        dst, src = o_part(g)
                        rest(o_lo(dst), src, o_hi(dst)).then_inc(q["o_lo"], 1)

            attention_part(0, QK_SCALE, prob_a, lambda g: ((slice(0, P), g), acc[:, 2 + g % 2, 0:TOKENS]),
                           lambda d: xl[d[0], d[1], :], lambda d: xh[d[0], d[1], :])
            for j in range(4):
                split_slab(WO + j + RING)
            layer_norm(3, WO + 3, 32, "tok")
            operand_lo(3)

            mlp_part(1)
            layer_norm(4, S_FF[1] + N_FF - 1, 48, "resid")
            rms_norm(4, gain2[:, :], TILES, 48)
            operand_lo(4)
            glu_part(0)
            add_product(5, S_SG[0] + N_SG - 1, 0.5)
            rms_norm(5, gain[:, :], 0, 16)
            operand_lo(5)

            for j in range(6):
                split_slab(HX + j + RING)
                cy, ps = (tmp_a, tmp_b)[j % 2], up[j % 2]
                dve.wait_ge(hy["tap0"], CT * (j + 1))
                for back in (1, 2, 3):
                    for f in range(CT):
                        o = f * TOKENS
                        row = ROW_XBC + (XBC_TAPS - 1 - back) * XT + CT * j + f
                        ins = vec.scalar_tensor_tensor(
                            cy[:, o + back:o + TOKENS], ps[:, o:o + TOKENS - back], cols[:, row:row + 1],
                            cy[:, o + back:o + TOKENS], ALU.mult, ALU.add)
                    if back < 3:
                        then(ins)
                ins.then_inc(hy["conv"], 1)

            x_dt, neg_abs, e_dt, z_dt, z2_dt, series, dt, _, adt, exp_a = [dt_work[:, i, :] for i in range(10)]
            nadt = z_dt
            dve.wait_ge(slab_used, HDT + 1)
            dve.wait_ge(hy["rows"], 64)
            for tile in range(TILES):
                sl = slice(tile * SSD_HEADS, (tile + 1) * SSD_HEADS)
                ins = vec.tensor_tensor(x_dt[:, sl], up[2 + tile][:, 0:SSD_HEADS], dtb_row, ALU.add)
            then(ins)
            then(vec.tensor_scalar(neg_abs, x_dt, -1.0, None, ALU.mult))
            vec.tensor_tensor(neg_abs, neg_abs, x_dt, ALU.min).then_inc(hy["dt_abs"], 1)
            split_slab(HDT + RING)
            dve.wait_ge(hy["dt_exp"], 2)
            then(vec.tensor_scalar(z_dt, e_dt, 2.0, None, ALU.add))
            then(vec.reciprocal(z_dt, z_dt))
            then(vec.tensor_tensor(z_dt, z_dt, e_dt, ALU.mult))
            then(vec.tensor_tensor(z2_dt, z_dt, z_dt, ALU.mult))
            then(vec.tensor_scalar(series, z2_dt, 1.0 / 19, None, ALU.mult))
            for k in (17, 15, 13, 11, 9, 7, 5, 3):
                then(vec.scalar_tensor_tensor(series, series, 1.0 / k, z2_dt, ALU.add, ALU.mult))
            then(vec.scalar_tensor_tensor(series, series, 1.0, z_dt, ALU.add, ALU.mult))
            then(vec.tensor_scalar(dt, x_dt, 0.0, None, ALU.max))
            then(vec.scalar_tensor_tensor(dt, series, 2.0, dt, ALU.mult, ALU.add))
            for tile in range(TILES):
                sl = slice(tile * SSD_HEADS, (tile + 1) * SSD_HEADS)
                ins = vec.tensor_tensor(nadt[:, sl], dt[:, sl], exp_a[:, 0:SSD_HEADS], ALU.mult)
            then(ins)
            vec.tensor_scalar(adt, nadt, -1.0, None, ALU.mult).then_inc(hy["adt"], 1)
            for j in range(4):
                split_slab(HQK + j + RING)
            for j in range(2):
                split_slab(HV + j + RING)

            def heads(a, n=8):
                return a.rearrange("p (h d) -> p h d", h=n)

            def per_head(a, n=8):
                return a.unsqueeze(2).to_broadcast([P, n, SSD_HD])

            for g in range(4):
                tile, h = g // 2, g % 2
                dve.wait_ge(hy["xs_ps"], g + 1)
                src = heads(up[2 + g % 2][:, :])
                cols_h = slice(h * HALF, (h + 1) * HALF)
                vec.tensor_tensor(heads(y_tok[:, tile, cols_h]), src, per_head(dskip_row[:, 8 * h:8 * h + 8]), ALU.mult)\
                    .then_inc(hy["y_sum"], 1)
                hd = tile * SSD_HEADS + 8 * h
                vec.tensor_tensor(heads(xdt[:, tile, cols_h]), src, per_head(dt[:, hd:hd + 8]), ALU.mult)\
                    .then_inc(hy["xdt"], 1)
            for g in range(SSD_GROUPS):
                dve.wait_ge(hy["cb_act"], g + 1)
                for tile in range(TILES):
                    vec.tensor_tensor(cb_diag[:, 2 * g + tile, :], acc[:, g, 2 * P * tile:2 * P * tile + P], tri, ALU.mult)\
                        .then_inc(hy["cb"], 1)
            dve.wait_ge(hy["decays"], 1)
            dve.wait_ge(hy["xdt"], 2)
            vec.tensor_tensor(heads(xdt_end, SSD_HEADS), heads(xdt[:, 0, :], SSD_HEADS),
                              per_head(dt_work[:, 7, 0:SSD_HEADS], SSD_HEADS), ALU.mult).then_inc(hy["cb"], 1)
            dve.wait_ge(hy["cb"], 4)
            for n in range(8 + 1):
                if n < 8:
                    dve.wait_ge(hy["seg_ps"], n + 1)
                    if n >= 2:
                        dve.wait_ge(hy["exp"], n - 1)
                    vec.tensor_scalar((tmp_a, tmp_b)[n % 2][:, :], up[n % 2][:, :], 0.0, None, ALU.min)\
                        .then_inc(hy["seg"], 1)
                if n >= 1:
                    k = n - 1
                    g, tile = (k % 4) // 2, k // 4
                    dve.wait_ge(hy["exp"], k + 1)
                    w = (tmp_c, tmp_d)[k % 2][:, :].rearrange("p (h l) -> p h l", h=4)
                    cb = cb_diag[:, 2 * g + tile:2 * g + tile + 1, :].to_broadcast([P, 4, P])
                    vec.tensor_tensor(w, w, cb, ALU.mult).then_inc(hy["seg_w"], 1)
            dve.wait_ge(hy["y_sum"], 4)
            for tile in range(TILES):
                for g in range(SSD_GROUPS):
                    y = y_tok[:, tile, g * HALF:(g + 1) * HALF]
                    dve.wait_ge(hy["y_ps"], 4 * tile + 2 * g + 2)
                    then(vec.tensor_tensor(y, acc[:, 2 * tile + g, :], y, ALU.add))
                    if tile == 1:
                        dve.wait_ge(hy["off_ps"], g + 1)
                        part = (tmp_a, tmp_b)[g][:, :]
                        then(vec.tensor_tensor(heads(part), heads(up[2 + g][:, :]),
                                               per_head(dt_work[:, 7, SSD_HEADS + 8 * g:SSD_HEADS + 8 * g + 8]),
                                               ALU.mult))
                        vec.tensor_tensor(y, y, part, ALU.add).then_inc(hy["y_sum"], 1)
            for j in range(2):
                split_slab(HZ + j + RING)
            dve.wait_ge(hy["y_sum"], 6)
            for n in range(2 * TILES):
                hf, tile = n // TILES, n % TILES
                dve.wait_ge(hy["z_gate"], n + 1)
                y = y_tok[:, tile, hf * HALF:(hf + 1) * HALF]
                vec.tensor_tensor(y, y, (tmp_a, tmp_b)[n % 2][:, :], ALU.mult).then_inc(hy["y_gated"], 1)
                if n == 1:
                    split_slab(HZ + 2 + RING)
                    split_slab(HZ + 3 + RING)
            for tile in range(TILES):
                y = y_tok[:, tile, :]
                dve.wait_ge(hy["rstd"], tile + 1)
                vec.scalar_tensor_tensor(y, y, rstd[:, tile:tile + 1], gain2[:, :], ALU.mult, ALU.mult)\
                    .then_inc(hy["y_n"], 1)

            def hybrid_out(g):
                o = ATT_HD * (g % 2)
                return (slice(o, o + ATT_HD), g // 2), acc[o:o + ATT_HD, 2 + g % 2, 0:TOKENS]

            attention_part(1, 1.0, prob_b, hybrid_out, lambda d: hl[d[0], d[1], :], lambda d: hh[d[0], d[1], :])
            for g in range(4):
                tile, h = g // 2, g % 2
                dve.wait_ge(hy["y_hi"], g + 1)
                rest(xl[:, 4 * h:4 * h + 4, tile * P:(tile + 1) * P], up[g][:, :].rearrange("p (k n) -> p k n", k=4),
                     xh[:, 4 * h:4 * h + 4, tile * P:(tile + 1) * P]).then_inc(hy["y_lo"], 1)
            for j in range(6):
                split_slab(HWO + j + RING)
            add_product(6, HWO + 5, 1.0)
            rms_norm(6, gain[:, :], 0, 16)
            operand_lo(6)
            glu_part(1)
            add_product(7, S_SG[1] + N_SG - 1, 0.5)
            rms_norm(7, gain[:, :], 0, 16)

        @block.tensor
        def _(pe):
            mm = nc.tensor.matmul

            def weights(m, off=0):
                pe.wait_ge(lo_done, off + (m + 1))

            def up_block(dst, m, col, step, k_tiles, x_tile=0, w_tile=0, first=True, last=True):
                for k in range(k_tiles):
                    c = (w_tile + k) * step + col
                    w_h = weight_hi[:, m % RING, c:c + P]
                    w_l = weight_lo[:, m % RING, c:c + P]
                    mm(dst, w_h, xh[:, x_tile + k, :], start=first and k == 0, stop=False)
                    mm(dst, w_h, xl[:, x_tile + k, :], start=False, stop=False)
                    ins = mm(dst, w_l, xh[:, x_tile + k, :], start=False, stop=last and k == k_tiles - 1)
                return ins

            def up_product(m, bank):
                for f in range(CT):
                    ins = up_block(bank[:, f * TOKENS:(f + 1) * TOKENS], m, f * P, CHUNK_F, KD)
                ins.then_inc(slab_used, 1)

            def token_block(dst, s_h, s_l, w_h, w_l, first, last):
                open_group = dict(skip_group_check=True)
                for d, h, l in zip(dst, w_h, w_l):
                    mm(d, s_h, h, start=first, stop=False, **open_group)
                    mm(d, s_h, l, start=False, stop=False, **open_group)
                for d, h in zip(dst, w_h):
                    ins = mm(d, s_l, h, start=False, stop=last, **open_group)
                return ins

            def down_product(m, s_h, s_l, k_tiles, first=False, last=None):
                def one(j, tile):
                    cut = slice(tile * P, (tile + 1) * P)
                    c = [slice(j * D + h * HALF, j * D + (h + 1) * HALF) for h in range(2)]
                    return token_block([acc[:, 2 * tile + h, :] for h in range(2)], s_h(j)[:, cut], s_l(j)[:, cut],
                                       [weight_hi[:, m % RING, x] for x in c], [weight_lo[:, m % RING, x] for x in c],
                                       first and j == 0, last is not None and j == k_tiles - 1)

                if last is None:
                    for j in range(k_tiles):
                        for tile in range(TILES):
                            ins = one(j, tile)
                else:
                    for tile in range(TILES):
                        for j in range(k_tiles):
                            ins = one(j, tile)
                        if tile == 0:
                            ins.then_inc(tile0, 1)
                ins.then_inc(slab_used, 1)

            def hidden(par, j0=0):
                return (lambda j: hh[:, CT * par + j0 + j, :]), (lambda j: hl[:, CT * par + j0 + j, :])

            def turn(b, src):
                for tile in range(TILES):
                    if b == 0:
                        pe.wait_ge(x_landed, 16 * TILES)
                    else:
                        pe.wait_ge(norm[b]["tok"], tile + 1)
                    for h in range(2):
                        for j in range(4):
                            f = (4 * h + j) * P
                            ins = nc.tensor.transpose(up[2 * tile + h][:, j * P:(j + 1) * P], src[:, tile, f:f + P],
                                                      ident)
                        ins.then_inc(turned, 1)
                if b in (1, 3, 4, 6):
                    clear_acc()
                pe.wait_ge(operand_low, 4 * b + 4)

            def clear_acc():
                for n in range(4):
                    mm(acc[:, n, :], zeros[0:1, 0:P], zeros[0:1, :], start=True, stop=False, skip_group_check=True)

            pe.wait_ge(const_landed, 64)
            pe.wait_ge(zeros_ready, 1)
            turn(0, x_tok)
            nc.tensor.transpose(up[3][:, 0:ROWS], rows[:, :], ident[0:ROWS, 0:ROWS]).then_inc(cols_turned, 1)

            m = S_SC
            for c in range(SC_CHUNKS + 1):
                if c < SC_CHUNKS:
                    weights(m)
                    if c == 1:
                        pe.wait_ge(cols_ready, 1)
                    up_product(m, up[3 if c % 2 else 0])
                    weights(m + 1)
                    if c:
                        pe.wait_ge(sc["c_copied"], c)
                    up_product(m + 1, up[1])
                    weights(m + 2)
                    if c:
                        pe.wait_ge(sc["ch_made"], c)
                    up_product(m + 2, up[2])
                    m += 3
                if c:
                    weights(m)
                    pe.wait_ge(sc["chunk"], c)
                    down_product(m, *hidden((c - 1) % 2), CT, first=(c == 1), last=1 if c == SC_CHUNKS else None)
                    m += 1

            def mlp_part(i, b):
                s, q = S_FF[i], mlp[i]
                weights(s)
                up_product(s, up[0])
                with pe.Fori(0, FF_CHUNKS // 2 - 1) as it:
                    for j in range(4):
                        m = s + 1 + j
                        weights(m, 4 * it)
                        if j % 2 == 0:
                            up_product(m, up[(1, 0)[j // 2]])
                        else:
                            pe.wait_ge(q["chunk"], 2 * it + (1 + j // 2))
                            down_product(m, *hidden(j // 2), CT)
                m = s + N_FF - 3
                weights(m)
                up_product(m, up[1])
                weights(m + 1)
                pe.wait_ge(q["chunk"], FF_CHUNKS - 1)
                down_product(m + 1, *hidden(0), CT)
                weights(m + 2)
                pe.wait_ge(q["chunk"], FF_CHUNKS)
                down_product(m + 2, *hidden(1), CT, last=b)

            def glu_part(i, b):
                s, q = S_SG[i], glu[i]
                for j in range(2):
                    weights(s + j)
                    up_product(s + j, up[j])
                with pe.Fori(0, (SG_CHUNKS - 1) // 2) as it:
                    for j in range(8):
                        m = s + 2 + j
                        weights(m, 8 * it)
                        par = (1, 0)[j // 4]
                        if j % 4 < 2:
                            up_product(m, up[2 * par + j % 4])
                        else:
                            if j % 4 == 2:
                                pe.wait_ge(q["chunk"], 2 * it + (1 + j // 4))
                            down_product(m, *hidden(1 - par, j % 4 - 2), 1)
                for j in range(2):
                    m = s + N_SG - 2 + j
                    weights(m)
                    if j == 0:
                        pe.wait_ge(q["chunk"], SG_CHUNKS)
                    down_product(m, *hidden(0, j), 1, last=b if j else None)

            turn(1, x_tok)
            mlp_part(0, 2)
            turn(2, x_tok)

            def token_product(m, dst, n, step, w_tile, k_tiles, x_tile, first, last, col=0):
                for k in range(k_tiles):
                    for tile in range(TILES):
                        c = (w_tile + k) * step + col
                        cut = slice(tile * P, (tile + 1) * P)
                        ins = token_block([dst(tile)], xh[:, x_tile + k, cut], xl[:, x_tile + k, cut],
                                          [weight_hi[:, m % RING, c:c + n]], [weight_lo[:, m % RING, c:c + n]],
                                          first and k == 0, last and k == k_tiles - 1)
                return ins

            for j in range(2):
                weights(DQ + j)
                token_product(DQ + j, lambda tile: acc[:, 2 * tile, 0:Q_LORA], Q_LORA, Q_LORA, 0, 4, 4 * j, j == 0, j == 1)\
                    .then_inc(slab_used, 1)
            for j in range(2):
                weights(KV + j)
                token_product(KV + j, lambda tile: acc[:, 2 * tile + 1, 0:KV_LORA], KV_LORA, KV_COLS, 0, 4, 4 * j,
                              j == 0, j == 1)
                up_block(up[0][:, 0:TOKENS], KV + j, KV_LORA, KV_COLS, 4, 4 * j, 0, j == 0, j == 1)\
                    .then_inc(slab_used, 1)

            def partner(r):
                pe.wait_ge(mla["pe"], r + 1)
                if r:
                    pe.wait_ge(mla["rotated"], r)
                mm(acc[:, 3, 0:TOKENS], swap, pe_raw[:, r % 2, :], start=True, stop=True).then_inc(mla["swapped"], 1)

            pe.wait_ge(mla["latent"], 2 * TILES)
            for g in range(3):
                blocks = (((0, 0), (0, 1), (1, 0), (1, 1)), ((2, 0), (2, 1)), ((0, 0), (0, 1), (1, 0), (1, 1)))[g]
                src = latent_kv if g == 2 else latent_q
                for n, (k, tile) in enumerate(blocks):
                    ins = nc.tensor.transpose(acc[:, g, n * P:(n + 1) * P], src[:, tile, k * P:(k + 1) * P], ident)
                ins.then_inc(mla["turned"], 1)
            partner(0)
            pe.wait_ge(mla["t_lo"], 3)
            for j in range(4):
                weights(UQ + j)
                if j >= 2:
                    pe.wait_ge(mla["q_out"], j - 1)
                for f in range(2):
                    up_block(up[j % 2][:, f * TOKENS:(f + 1) * TOKENS], UQ + j, f * NOPE, UQ_COLS, KQ)
                up_block(up[2 + j % 2][:, 0:TOKENS], UQ + j, 2 * NOPE, UQ_COLS, KQ).then_inc(slab_used, 1)
                if j:
                    partner(j)
            weights(UK)
            pe.wait_ge(mla["q_out"], 4)
            for j in range(4):
                for f in range(2):
                    ins = up_block(up[j][:, f * TOKENS:(f + 1) * TOKENS], UK, (2 * j + f) * NOPE, D, KKV, KQ)
                ins.then_inc(mla["k_ps"] if j < 3 else slab_used, 1)
            partner(4)
            weights(UV)
            pe.wait_ge(mla["rotated"], 5)
            for k in range(KKV):
                for tile in range(TILES):
                    cut = slice(tile * P, (tile + 1) * P)
                    c = [slice(k * D + h * HALF, k * D + (h + 1) * HALF) for h in range(2)]
                    ins = token_block([acc[:, 2 * tile + h, :] for h in range(2)],
                                      xh[:, KQ + k, cut], xl[:, KQ + k, cut],
                                      [weight_hi[:, UV % RING, x] for x in c], [weight_lo[:, UV % RING, x] for x in c],
                                      k == 0, k == KKV - 1)
            ins.then_inc(slab_used, 1)

            def attention_part(i, score, prob, prob_t, v, o_dst, banks_free):
                q = att[i]

                def scores(h):
                    if h >= 4:
                        pe.wait_ge(q["probs"], 2 * (h - 4) + 2)
                    S = up[h % 4]
                    score(h, 0, S[:, 0:P])
                    mm(S[:, P - ATTN_CHUNK:P], mask_row, mask_ones, start=False, stop=True, skip_group_check=True)
                    score(h, 1, S[:, P:384])
                    mm(S[:, 384 - ATTN_CHUNK:384], mask_row, mask_ones, start=False, stop=True, skip_group_check=True)\
                        .then_inc(q["scores"], 1)

                scores(0)
                scores(1)
                for g in range(HEADS):
                    if g + 2 < HEADS:
                        scores(g + 2)
                    if g == 0:
                        banks_free()
                    pe.wait_ge(q["normed"], 2 * g + 2)
                    if g >= 2:
                        pe.wait_ge(q["t_out"], g - 1)
                    for n in range(3):
                        ins = nc.tensor.transpose(acc[:, g % 2, n * P:(n + 1) * P], prob[:, g % 2, n * P:(n + 1) * P],
                                                  ident)
                    ins.then_inc(q["turned"], 1)
                    pe.wait_ge(q["t_out"], g + 1)
                    if g >= 2:
                        pe.wait_ge(q["o_lo"], g - 1)
                    o = o_dst(g)
                    mm(o, v(0, g), prob_t[:, g % 2, 0:TOKENS], start=True, stop=False, skip_group_check=True)
                    mm(o[:, P:TOKENS], v(1, g), prob_t[:, g % 2, TOKENS:384], start=False, stop=True,
                       skip_group_check=True).then_inc(q["o_ps"], 1)

            def mla_score(h, tile, dst):
                queries, keys = slice(tile * P, (tile + 1) * P), slice(0, (tile + 1) * P)
                r = slice(ROPE * (h % 2), ROPE * (h % 2) + ROPE)
                mm(dst, q_nope[:, h, queries], k_nope[:, h, keys], start=True, stop=False, skip_group_check=True)
                mm(dst, q_rot[r, h // 2, queries], k_rot[r, keys], start=False, stop=False, skip_group_check=True)

            def values_copied():
                pe.wait_ge(mla["v0"], 1)
                pe.wait_ge(mla["v1"], 1)

            pe.wait_ge(mla["k_out"], 4)
            attention_part(0, mla_score, prob_a, prob_t_a, lambda kt, h: v_a[:, kt, h * P:(h + 1) * P],
                           lambda h: acc[:, 2 + h % 2, 0:TOKENS], values_copied)
            pe.wait_ge(att[0]["o_lo"], HEADS)
            for c in range(4):
                weights(WO + c)
                down_product(WO + c, lambda j: xh[:, CT * c + j, :], lambda j: xl[:, CT * c + j, :], CT,
                             first=(c == 0), last=3 if c == 3 else None)

            turn(3, x_tok)
            mlp_part(1, 4)
            turn(4, normed)
            glu_part(0, 5)
            turn(5, normed)

            for j in range(6):
                weights(HX + j)
                if j >= 2:
                    pe.wait_ge(hy["conv"], j - 1)
                up_product(HX + j, up[j % 2])
            weights(HDT)
            token_product(HDT, lambda tile: up[2 + tile][:, 0:SSD_HEADS], SSD_HEADS, SSD_HEADS, 0, KD, 0, True, True)\
                .then_inc(slab_used, 1)
            for j in range(4):
                weights(HQK + j)
                if j == 0:
                    pe.wait_ge(hy["conv"], 6)
                if j >= 2:
                    pe.wait_ge(hy["qk_out"], j - 1)
                up_product(HQK + j, up[j % 2])
            for j in range(2):
                weights(HV + j)
                token_product(HV + j, lambda tile: acc[:, tile, :], HALF, HALF, 0, 4, 4 * j, j == 0, j == 1)\
                    .then_inc(slab_used, 1)

            pe.wait_ge(hy["xbc"], 6)
            pe.wait_ge(hy["adt"], 1)
            mm(acc[:, 2, 0:SSD_HEADS], after, adt_tile(0), start=True, stop=True)
            mm(acc[:, 2, SSD_HEADS:2 * SSD_HEADS], tri, adt_tile(1), start=True, stop=True).then_inc(hy["cum_ps"], 1)
            for g in range(4):
                tile, h = g // 2, g % 2
                if g >= 2:
                    pe.wait_ge(hy["xdt"], g - 1)
                for j in range(4):
                    ins = nc.tensor.transpose(up[2 + g % 2][:, j * P:(j + 1) * P],
                                              xs_t[:, 4 * h + j, tile * P:(tile + 1) * P], ident)
                ins.then_inc(hy["xs_ps"], 1)
            pe.wait_ge(hy["v_out"], TILES)
            for g in range(SSD_GROUPS):
                mm(acc[:, g, 0:TOKENS], bc_t[:, g, 0:P], bc_t[:, 2 + g, :], start=True, stop=True)
                mm(acc[:, g, TOKENS:384], bc_t[:, g, P:TOKENS], bc_t[:, 2 + g, P:TOKENS], start=True, stop=True)\
                    .then_inc(hy["cb_ps"], 1)
            pe.wait_ge(hy["qk_out"], 4)
            for n in range(8 + 1):
                if n < 8:
                    tile, h0 = n // 4, 4 * (n % 4)
                    if n >= 2:
                        pe.wait_ge(hy["seg"], n - 1)
                    bank = up[n % 2]
                    mm(bank[:, :].rearrange("p (h l) -> p h l", h=4), tri,
                       nadt_tile(tile)[:, h0:h0 + 4].unsqueeze(2).to_broadcast([P, 4, P]), start=True, stop=False,
                       skip_group_check=True)
                    for q in range(4):
                        ins = mm(bank[:, q * P:(q + 1) * P], adt_tile(tile)[:, h0 + q:h0 + q + 1].to_broadcast([P, P]),
                                 tri, start=False, stop=True, skip_group_check=True)
                    ins.then_inc(hy["seg_ps"], 1)
                if n == 1:
                    pe.wait_ge(hy["xdt"], 4)
                    pe.wait_ge(hy["cb"], 5)
                    pe.wait_ge(hy["decays"], 1)
                    pe.wait_ge(hy["cb_act"], 2)
                    for g in range(SSD_GROUPS):
                        mm(up[2 + g][:, :], cb_off[:, g, :], xdt_end[:, g * HALF:(g + 1) * HALF], start=True, stop=True)\
                            .then_inc(hy["off_ps"], 1)
                if n >= 1:
                    k = n - 1
                    tile, h0 = k // 4, 4 * (k % 4)
                    pe.wait_ge(hy["seg_w"], k + 1)
                    for q in range(4):
                        h = h0 + q
                        ins = mm(acc[:, 2 * tile + h // 8, h % 8 * SSD_HD:(h % 8 + 1) * SSD_HD],
                                 (tmp_c, tmp_d)[k % 2][:, q * P:(q + 1) * P], xdt[:, tile, h * SSD_HD:(h + 1) * SSD_HD],
                                 start=True, stop=True)
                    ins.then_inc(hy["y_ps"], 1)
            pe.wait_ge(hy["y_sum"], 6)
            for j in range(4):
                weights(HZ + j)
                token_product(HZ + j, lambda tile: acc[:, 2 * tile + j // 2, :], HALF, HALF, 0, 4, 4 * (j % 2),
                              j % 2 == 0, j % 2 == 1).then_inc(slab_used, 1)

            def hybrid_score(h, tile, dst):
                queries, keys = slice(tile * P, (tile + 1) * P), slice(0, (tile + 1) * P)
                r = slice(ATT_HD * (h % 2), ATT_HD * (h % 2) + ATT_HD)
                mm(dst, q_b[r, h // 2, queries], k_b[r, h // 2, keys], start=True, stop=False, skip_group_check=True)
                for kt in range(tile + 1):
                    w0 = (tile - kt) * P
                    mm(dst[:, kt * P:(kt + 1) * P], hankel[:, h, w0:w0 + P], anti, start=False, stop=False,
                       skip_group_check=True)

            def gates_taken():
                pe.wait_ge(hy["z_gate"], 2 * TILES)

            pe.wait_ge(hy["hank"], 16 * HEADS)
            attention_part(1, hybrid_score, prob_b, prob_t_b, lambda kt, h: v_b[:, kt, h * ATT_HD:(h + 1) * ATT_HD],
                           lambda h: acc[ATT_HD * (h % 2):ATT_HD * (h % 2) + ATT_HD, 2 + h % 2, 0:TOKENS], gates_taken)
            for tile in range(TILES):
                pe.wait_ge(hy["y_n"], tile + 1)
                for h in range(2):
                    for j in range(4):
                        f = (4 * h + j) * P
                        ins = nc.tensor.transpose(up[2 * tile + h][:, j * P:(j + 1) * P], y_tok[:, tile, f:f + P], ident)
                    ins.then_inc(hy["y_ps_t"], 1)
            pe.wait_ge(att[1]["o_lo"], HEADS)
            for c in range(6):
                weights(HWO + c)
                if c < 2:
                    down_product(HWO + c, lambda j: hh[:, CT * c + j, :], lambda j: hl[:, CT * c + j, :], CT,
                                 first=(c == 0))
                else:
                    if c == 2:
                        pe.wait_ge(hy["y_lo"], 4)
                    down_product(HWO + c, lambda j: xh[:, CT * (c - 2) + j, :], lambda j: xl[:, CT * (c - 2) + j, :], CT,
                                 last=6 if c == 5 else None)
            turn(6, normed)
            glu_part(1, 7)


_NAMES = [
    "x", "sc_w_in", "sc_conv_w", "sc_w_out", "mla_w_dq", "mla_g_q", "mla_w_uq", "mla_w_dkv", "mla_g_kv",
    "mla_w_uk", "mla_w_uv", "mla_w_o", "ff_w1", "ff_w2", "ln_mix_g", "ln_mix_b", "ln_ff_g", "ln_ff_b",
    "ffn1_norm_2", "ffn1_w_gate_2", "ffn1_w_up_2", "ffn1_w_down_2", "mix_norm_2", "w_in_2", "conv_w_2",
    "conv_b_2", "dt_bias_2", "a_log_2", "d_skip_2", "ssd_norm_2", "rel_bias_2", "w_out_2", "ffn2_norm_2",
    "ffn2_w_gate_2", "ffn2_w_up_2", "ffn2_w_down_2", "final_norm_2",
]


def kernel(**inputs):
    import concourse.bacc as bacc
    from concourse.bass_utils import run_bass_kernel_spmd

    nc = bacc.Bacc("TRN2", target_bir_lowering=False, num_devices=1)
    arrays = {name: np.ascontiguousarray(inputs[name]) for name in _NAMES}
    arrays["shape_consts"] = shape_constants()
    aps = {n: nc.dram_tensor(f"in_{n}", a.shape, mybir.dt.from_np(a.dtype), kind="ExternalInput").ap()
           for n, a in arrays.items()}
    out = nc.dram_tensor("out", (1, TOKENS, D), F32, kind="ExternalOutput").ap()
    two_blocks(nc, aps, aps["shape_consts"], out)
    r = run_bass_kernel_spmd(nc, [{f"in_{n}": a for n, a in arrays.items()}], core_ids=[0])
    return r.results[0]["out"]
```

```python
from contextlib import ExitStack

import numpy as np

import concourse.bass as bass
from concourse import mybir

F32 = mybir.dt.float32
F32R = mybir.dt.float32r
BF16 = mybir.dt.bfloat16
ACT = mybir.ActivationFunctionType
ALU = mybir.AluOpType
AX_X = mybir.AxisListType.X

P = 128
TOKENS = 256
TILES = TOKENS // P
D = 1024
KD = D // P
HALF = 512
CHUNK_F = 256
CT = CHUNK_F // P
RING = 4
SLAB = 2048
ATTN_CHUNK = 64

DEPTH = 2
ALPHA = (2.0 * DEPTH) ** 0.25
LN_EPS = 1e-5
MLA_EPS = 1e-6
RMS_EPS = 1e-5
D_FF = 4096
D_FF_2 = 2816
HEADS = 8
NOPE, ROPE, Q_LORA, KV_LORA = 128, 64, 384, 256
KQ, KKV = Q_LORA // P, KV_LORA // P
QK_SCALE = float(NOPE + ROPE) ** -0.5
SSD_HEADS, SSD_HD, SSD_GROUPS = 16, 64, 2
SSD_INNER = SSD_HEADS * SSD_HD
XBC = SSD_INNER + 2 * SSD_GROUPS * P
ATT_HD = 64
ATT_INNER = HEADS * ATT_HD
REL = 513
MIX = SSD_INNER + ATT_INNER
Z0, XBC0, DT0 = 0, SSD_INNER, SSD_INNER + XBC
Q0 = DT0 + SSD_HEADS
K0, V0 = Q0 + ATT_INNER, Q0 + 2 * ATT_INNER
MASKED = -1.0e30

SC_TAPS, XBC_TAPS = 3, 4
XT = XBC // P
ROW_SC, ROW_XBC, ROW_XBC_B = 0, SC_TAPS * KD, SC_TAPS * KD + XBC_TAPS * XT
ROWS = ROW_XBC_B + XT

C_ID, C_ANTI, C_TRI, C_AFTER, C_SWAP, C_COS, C_SIN, C_MROW = 0, 128, 256, 384, 512, 640, 896, 1152
C_ALL = 1280 + 64


def shape_constants():
    c = np.zeros((P, C_ALL), np.float32)
    i = np.arange(P)
    c[:, C_ID:C_ID + P] = np.eye(P)
    c[:, C_ANTI:C_ANTI + P] = np.eye(P)[::-1]
    c[:, C_TRI:C_TRI + P] = i[:, None] <= i[None, :]
    c[:, C_AFTER:C_AFTER + P] = i[:, None] > i[None, :]
    h = ROPE // 2
    for d in range(P):
        src, sign = (d + h, -1.0) if d % ROPE < h else (d - h, 1.0)
        c[src, C_SWAP + d] = sign
    inv = np.float32(10000.0) ** (-np.arange(0, ROPE, 2, dtype=np.float32) / np.float32(ROPE))
    ang = np.arange(TOKENS, dtype=np.float32)[None, :] * inv[i % h][:, None]
    c[:, C_COS:C_COS + TOKENS] = np.cos(ang)
    c[:, C_SIN:C_SIN + TOKENS] = np.sin(ang)
    c[0, C_MROW:C_MROW + ATTN_CHUNK] = MASKED
    c[0, C_MROW + P:C_MROW + P + ATTN_CHUNK] = 1.0
    return c


def two_blocks(nc, t, consts, out):
    FF_CHUNKS = D_FF // CHUNK_F
    SG_CHUNKS = D_FF_2 // CHUNK_F
    SC_CHUNKS = D // CHUNK_F
    N_SC = 4 * SC_CHUNKS
    N_FF = 2 * FF_CHUNKS
    N_MLA = 4 + 4 + 2 + 4
    N_SG = 4 * SG_CHUNKS
    GLU_PASSES = (SG_CHUNKS - 1) // 2 - 1
    N_HY = 2 + 1 + 6 + 4 + 4 + 6
    S_SC = 0
    S_FF = [S_SC + N_SC, S_SC + N_SC + N_FF + N_MLA]
    S_MLA = S_FF[0] + N_FF
    S_SG = [S_FF[1] + N_FF, S_FF[1] + N_FF + N_SG + N_HY]
    S_HY = S_SG[0] + N_SG
    N_SLABS = S_SG[1] + N_SG

    width = [SLAB] * N_SLABS
    loads = [1] * N_SLABS
    for s in S_SG:
        for i in range(SG_CHUNKS):
            d0 = s + 4 * i + 4 if i < SG_CHUNKS - 1 else s + 4 * i + 2
            width[d0] = width[d0 + 1] = D
    DQ, KV, UQ, UK, UV, WO = S_MLA, S_MLA + 2, S_MLA + 4, S_MLA + 8, S_MLA + 9, S_MLA + 10
    UQ_COLS = 2 * (NOPE + ROPE)
    KV_COLS = KV_LORA + 2 * ROPE
    for m in (DQ, DQ + 1):
        width[m] = 4 * Q_LORA
    for m in (KV, KV + 1):
        width[m], loads[m] = 4 * KV_COLS, 2
    for m in range(UQ, UQ + 4):
        width[m], loads[m] = KQ * UQ_COLS, 4
    HV, HDT, HX, HQK, HZ, HWO = S_HY, S_HY + 2, S_HY + 3, S_HY + 9, S_HY + 13, S_HY + 17
    width[HDT] = KD * SSD_HEADS
    landed_at, used_dmas = [], [0] * RING
    for m in range(N_SLABS):
        used_dmas[m % RING] += loads[m]
        landed_at.append(16 * used_dmas[m % RING])

    with ExitStack() as ctx:
        def sb(name, shape, dt=F32):
            return ctx.enter_context(nc.sbuf_tensor(name, shape, dt))

        def sem(name):
            return ctx.enter_context(nc.semaphore(name))

        raw = sb("raw", [P, RING, SLAB])
        weight_hi = sb("weight_hi", [P, RING, SLAB], F32R)
        weight_lo = sb("weight_lo", [P, RING, SLAB], F32R)
        x_tok = sb("x_tok", [P, TILES, D])
        normed = sb("normed", [P, TILES, D])
        xh = sb("xh", [P, KD, TOKENS], F32R)
        xl = sb("xl", [P, KD, TOKENS], F32R)
        hh = sb("hh", [P, 2 * CT, TOKENS], F32R)
        hl = sb("hl", [P, 2 * CT, TOKENS], F32R)
        tmp_a = sb("tmp_a", [P, HALF])
        tmp_b = sb("tmp_b", [P, HALF])
        tmp_c = sb("tmp_c", [P, HALF])
        tmp_d = sb("tmp_d", [P, HALF])
        gain = sb("gain", [P, D])
        bias = sb("bias", [P, D])
        gain2 = sb("gain2", [P, D])
        cst = sb("cst", [P, C_ALL])
        rows = sb("rows", [ROWS, P])
        cols = sb("cols", [P, ROWS])
        zeros = sb("zeros", [1, HALF], BF16)
        stat = sb("stat", [P, TILES, 2, 6])
        mean_var = sb("mean_var", [P, TILES, 2])
        rstd = sb("rstd", [P, 4])
        sumsq = sb("sumsq", [P, 4])
        half_neg = sb("half_neg", [P, 1])
        mean_sq = sb("mean_sq", [P, TILES, 2])
        arena = sb("arena", [P, 10368])

        acc = ctx.enter_context(nc.psum_tensor("acc", [P, 4, HALF], F32))
        up = [ctx.enter_context(nc.psum_tensor(f"up{i}", [P, HALF], F32)) for i in range(4)]

        ident = cst[:, C_ID:C_ID + P]
        anti = cst[:, C_ANTI:C_ANTI + P]
        tri = cst[:, C_TRI:C_TRI + P]
        after = cst[:, C_AFTER:C_AFTER + P]
        swap = cst[:, C_SWAP:C_SWAP + P]
        cos = cst[:, C_COS:C_COS + TOKENS]
        sin = cst[:, C_SIN:C_SIN + TOKENS]
        mask_row = cst[0:1, C_MROW:C_MROW + P]
        mask_ones = cst[0:1, C_MROW + P:C_MROW + P + ATTN_CHUNK]

        at = [0]

        def take(n, *dims):
            a = arena[:, at[0]:at[0] + n]
            at[0] += n
            if len(dims) == 2:
                a = a.rearrange("p (a b) -> p a b", a=dims[0])
            return a

        q_nope = take(HEADS * TOKENS, HEADS, TOKENS)
        k_nope = take(HEADS * TOKENS, HEADS, TOKENS)
        q_rot = take(4 * TOKENS, 4, TOKENS)
        k_rot = take(TOKENS)
        pe_raw = take(2 * TOKENS, 2, TOKENS)
        g_q = take(Q_LORA)
        g_kv = take(KV_LORA)
        prob_a = take(2 * 384, 2, 384)
        prob_t_a = take(2 * 384, 2, 384)
        v_a = normed
        latent_q = normed[:, 0, 0:2 * Q_LORA].rearrange("p (t n) -> p t n", t=TILES)
        latent_kv = normed[:, 1, 0:2 * KV_LORA].rearrange("p (t n) -> p t n", t=TILES)
        at[0] = 0
        bc_t = take(4 * TOKENS, 4, TOKENS)
        xs_t = take(8 * TOKENS, 8, TOKENS)
        hankel = xs_t
        q_b = take(4 * TOKENS, 4, TOKENS)
        k_b = take(4 * TOKENS, 4, TOKENS)
        v_b = take(TILES * HALF, TILES, HALF)
        xdt = take(TILES * D, TILES, D)
        xdt_end = take(D)
        cb_diag = take(4 * P, 4, P)
        cb_off = take(2 * P, 2, P)
        prob_b = xdt[:, 0, 0:2 * 384].rearrange("p (a b) -> p a b", a=2)
        prob_t_b = xdt[:, 1, 0:2 * 384].rearrange("p (a b) -> p a b", a=2)
        dt_work = take(10 * 32, 10, 32)
        a_row = take(SSD_HEADS)
        dtb_row = take(SSD_HEADS)
        dskip_row = take(SSD_HEADS)
        y_tok = normed
        z_gate = (bias, xdt_end)

        def adt_tile(tile):
            return dt_work[:, 8, tile * SSD_HEADS:(tile + 1) * SSD_HEADS]

        def nadt_tile(tile):
            return dt_work[:, 3, tile * SSD_HEADS:(tile + 1) * SSD_HEADS]

        head_max = sb("head_max", [P, 2, HEADS, 2])
        head_sum = sb("head_sum", [P, 2, HEADS, 2])

        ident_landed, const_landed, out_landed = sem("ident_landed"), sem("const_landed"), sem("out_landed")
        x_landed = [sem(f"x_landed{i}") for i in range(TILES)]
        landed = [sem(f"landed{i}") for i in range(RING)]
        hi_done, lo_done, slab_used = sem("hi_done"), sem("lo_done"), sem("slab_used")
        act_step, dve_step, pool_step = sem("act_step"), sem("dve_step"), sem("pool_step")
        cols_turned, cols_ready, zeros_ready, pool_ready = (
            sem("cols_turned"), sem("cols_ready"), sem("zeros_ready"), sem("pool_ready"))

        class Sems:

            def __init__(self, part, names):
                self.s = {n: sem(f"{part}_{n}") for n in names.split()}

            def __getitem__(self, n):
                return self.s[n]

        NORMS = 8
        norm = [Sems(f"norm{b}", "rows rstd tok" + " stat" * (b <= 4) + " resid squares" * (b >= 4)) if b else None for b in range(NORMS)]
        turned, operand_high, operand_low, acc_part = (
            sem("turned"), sem("operand_high"), sem("operand_low"), sem("acc_part"))
        sc = Sems("sc", "c_copied ch_made conv0 y_made y_hi chunk")
        mlp = [Sems(f"mlp{i}", "relu squared hidden_hi chunk") for i in range(2)]
        glu = [Sems(f"glu{i}", "gate hidden hidden_hi chunk") for i in range(2)]
        mla = Sems("mla", "rows latent_ps sumsq rstd latent turned t_hi t_lo pe q_out swapped rotated k_ps k_out v0 v1")
        att = [Sems(f"att{i}", "scores negmax probs normed turned t_out o_ps o_hi o_lo") for i in range(2)]
        hy = Sems("hy", "rows tap0 conv xbc dt_abs dt_exp adt qk_out v_out cum_ps decays xs_ps xs_out y_skip xdt "
                        "hank cb_ps cb_act cb seg_ps seg exp seg_w y_ps off_ps off_taken y_sum z_gate y_gated sumsq "
                        "rstd y_n y_ps_t y_hi y_lo")

        def up_view(w):
            return w.rearrange("(k p) n -> p k n", p=P)

        def up_chunks(w):
            return w.rearrange("(k p) (c f) -> p k c f", p=P, f=CHUNK_F)

        def down_chunks(w):
            return w.rearrange("(c j p) n -> p c j n", p=P, j=CT)

        def spread(v, n):
            return v.rearrange("(a n) -> a n", a=1).to_broadcast([P, n])

        def raw3(m, a, b):
            return raw[:, m % RING, 0:a * b].rearrange("p (a b) -> p a b", a=a)

        def heads(a, n=8):
            return a.rearrange("p (h d) -> p h d", h=n)

        def per_head(a, n=8):
            return a.unsqueeze(2).to_broadcast([P, n, SSD_HD])

        block = ctx.enter_context(nc.Block())

        @block.sync
        def _(sp):
            def load(m, dst, src):
                sp.dma_start(dst, src).then_inc(landed[m % RING], 16)

            def place_free(m):
                if m >= RING:
                    sp.wait_ge(lo_done, m - RING + 1)

            sp.dma_start(ident, consts[:, C_ID:C_ID + P]).then_inc(ident_landed, 16)
            for tile in range(TILES):
                sp.dma_start(x_tok[:, tile, :], t["x"][0, tile * P:(tile + 1) * P, :]).then_inc(x_landed[tile], 16)

            w_in = up_view(t["sc_w_in"][0])
            w_out = down_chunks(t["sc_w_out"][0])
            m = S_SC
            for c in range(SC_CHUNKS + 1):
                for part in range(3 if c < SC_CHUNKS else 0):
                    place_free(m)
                    f0 = part * D + c * CHUNK_F
                    load(m, raw3(m, KD, CHUNK_F), w_in[:, :, f0:f0 + CHUNK_F])
                    m += 1
                if c:
                    place_free(m)
                    load(m, raw3(m, CT, D), w_out[:, c - 1, :, :])
                    m += 1

            def mlp_weights(i):
                w1, w2 = up_chunks(t["ff_w1"][i]), down_chunks(t["ff_w2"][i])
                s = S_FF[i]

                def up_slab(m, c):
                    load(m, raw3(m, KD, CHUNK_F), w1[:, :, c, :])

                def down_slab(m, c):
                    load(m, raw3(m, CT, D), w2[:, c, :, :])

                place_free(s)
                up_slab(s, 0)
                with sp.Fori(0, FF_CHUNKS // 2 - 1) as it:
                    for j in range(4):
                        sp.wait_ge(lo_done, 4 * it + (s + 1 + j - RING + 1))
                        chunk = 2 * it + (1, 0, 2, 1)[j]
                        slot = (s + 1 + j) % RING
                        if j % 2 == 0:
                            sp.dma_start(raw3(slot, KD, CHUNK_F), w1[:, :, bass.ds(chunk, 1), :])\
                              .then_inc(landed[slot], 16)
                        else:
                            sp.dma_start(raw3(slot, CT, D), w2[:, bass.ds(chunk, 1), :, :])\
                              .then_inc(landed[slot], 16)
                e = s + N_FF - 3
                place_free(e)
                up_slab(e, FF_CHUNKS - 1)
                place_free(e + 1)
                down_slab(e + 1, FF_CHUNKS - 2)
                place_free(e + 2)
                down_slab(e + 2, FF_CHUNKS - 1)

            def glu_weights(i):
                name = ("ffn1", "ffn2")[i]
                wg, wu = up_chunks(t[f"{name}_w_gate_2"][0]), up_chunks(t[f"{name}_w_up_2"][0])
                wd = down_chunks(t[f"{name}_w_down_2"][0])
                s = S_SG[i]
                for j, w in enumerate((wg, wu)):
                    place_free(s + j)
                    load(s + j, raw3(s + j, KD, CHUNK_F), w[:, :, 0, :])
                with sp.Fori(0, (SG_CHUNKS - 1) // 2) as it:
                    for j in range(8):
                        sp.wait_ge(lo_done, 8 * it + (s + 2 + j - RING + 1))
                        slot = (s + 2 + j) % RING
                        c = 2 * it + j // 4
                        if j % 4 < 2:
                            sp.dma_start(raw3(slot, KD, CHUNK_F), (wg, wu)[j % 4][:, :, bass.ds(c + 1, 1), :])\
                              .then_inc(landed[slot], 16)
                        else:
                            sp.dma_start(raw3(slot, 1, D), wd[:, bass.ds(c, 1), j % 4 - 2, :])\
                              .then_inc(landed[slot], 16)
                for j in range(2):
                    e = s + N_SG - 2 + j
                    place_free(e)
                    load(e, raw3(e, 1, D), wd[:, SG_CHUNKS - 1, j:j + 1, :])

            mlp_weights(0)

            w = up_view(t["mla_w_dq"][0])
            for j in range(2):
                place_free(DQ + j)
                load(DQ + j, raw3(DQ + j, 4, Q_LORA), w[:, 4 * j:4 * j + 4, :])
            w = up_view(t["mla_w_dkv"][0])
            for j in range(2):
                place_free(KV + j)
                dst = raw3(KV + j, 4, KV_COLS)
                load(KV + j, dst[:, :, 0:KV_LORA + ROPE], w[:, 4 * j:4 * j + 4, :])
                load(KV + j, dst[:, :, KV_LORA + ROPE:], w[:, 4 * j:4 * j + 4, KV_LORA:])
            w = up_view(t["mla_w_uq"][0]).rearrange("p k (h c) -> p k h c", h=HEADS)
            for j in range(4):
                place_free(UQ + j)
                dst = raw3(UQ + j, KQ, UQ_COLS)
                for h in range(2):
                    load(UQ + j, dst[:, :, h * NOPE:(h + 1) * NOPE], w[:, :, 2 * j + h, 0:NOPE])
                    r0 = 2 * NOPE + h * ROPE
                    load(UQ + j, dst[:, :, r0:r0 + ROPE], w[:, :, 2 * j + h, NOPE:])
            for m, name in ((UK, "mla_w_uk"), (UV, "mla_w_uv")):
                place_free(m)
                load(m, raw3(m, KKV, D), t[name][0].rearrange("(k p) h d -> p k (h d)", p=P))
            w = down_chunks(t["mla_w_o"][0])
            for j in range(4):
                place_free(WO + j)
                load(WO + j, raw3(WO + j, CT, D), w[:, j, :, :])

            mlp_weights(1)
            glu_weights(0)

            w = up_view(t["w_in_2"][0])
            for j in range(2):
                place_free(HV + j)
                load(HV + j, raw3(HV + j, 4, HALF), w[:, 4 * j:4 * j + 4, V0:V0 + HALF])
            place_free(HDT)
            load(HDT, raw3(HDT, KD, SSD_HEADS), w[:, :, DT0:DT0 + SSD_HEADS])
            for s, f0, n in ((HX, XBC0, 6), (HQK, Q0, 4), (HZ, Z0, 4)):
                for j in range(n):
                    place_free(s + j)
                    load(s + j, raw3(s + j, KD, CHUNK_F), w[:, :, f0 + j * CHUNK_F:f0 + (j + 1) * CHUNK_F])
            w = down_chunks(t["w_out_2"][0])
            for j in range(6):
                place_free(HWO + j)
                load(HWO + j, raw3(HWO + j, CT, D), w[:, j, :, :])

            glu_weights(1)

            for n in range(2 * TILES):
                tile, c = n // 2, slice(n % 2 * HALF, (n % 2 + 1) * HALF)
                sp.wait_ge(norm[7]["tok"], n + 1)
                sp.dma_start(out[0, tile * P:(tile + 1) * P, c], normed[:, tile, c]).then_inc(out_landed, 16)
            sp.wait_ge(out_landed, 32 * TILES)

        @block.gpsimd
        def _(pool):
            steps = [0]

            def then(ins):
                steps[0] += 1
                ins.then_inc(pool_step, 1)
                pool.wait_ge(pool_step, steps[0])

            nc.gpsimd.memset(zeros[:, :], 0.0).then_inc(zeros_ready, 1)
            then(nc.gpsimd.memset(half_neg[:, :], -0.5))
            pool.wait_ge(landed[0], 16)
            pool.dma_start(cst[:, P:], consts[:, P:]).then_inc(const_landed, 16)
            pool.dma_start(rows[ROW_SC:ROW_XBC, :], t["sc_conv_w"][0].rearrange("k (f p) -> (k f) p", p=P))\
                .then_inc(const_landed, 16)
            pool.dma_start(rows[ROW_XBC:ROW_XBC_B, :], t["conv_w_2"][0].rearrange("k (f p) -> (k f) p", p=P))\
                .then_inc(const_landed, 16)
            pool.dma_start(rows[ROW_XBC_B:ROWS, :], t["conv_b_2"][0].rearrange("(f p) -> f p", p=P))\
                .then_inc(const_landed, 16)

            def norm_rows(b, *pairs):
                for dst, v, n in pairs:
                    pool.dma_start(dst, spread(v, n)).then_inc(norm[b]["rows"], 16)

            def root(dst, src, eps):
                n = dst.shape[-1]
                then(nc.gpsimd.tensor_scalar(dst, src, eps, None, ALU.add))
                return nc.gpsimd.tensor_tensor(dst, dst, half_neg[:, :].to_broadcast([P, n]), ALU.pow)

            def layer_norm_root(b):
                for tile in range(TILES):
                    pool.wait_ge(norm[b]["stat"], tile + 1)
                    root(rstd[:, tile:tile + 1], mean_var[:, tile, 1:2], LN_EPS).then_inc(norm[b]["rstd"], 1)

            norm_rows(1, (gain[:, :], t["ln_mix_g"][0], D), (bias[:, :], t["ln_mix_b"][0], D))
            layer_norm_root(1)
            pool.wait_ge(norm[1]["tok"], 2 * TILES)
            norm_rows(2, (gain[:, :], t["ln_ff_g"][0], D), (bias[:, :], t["ln_ff_b"][0], D))
            layer_norm_root(2)

            pool.dma_start(g_q, spread(t["mla_g_q"][0], Q_LORA)).then_inc(mla["rows"], 16)
            pool.dma_start(g_kv, spread(t["mla_g_kv"][0], KV_LORA)).then_inc(mla["rows"], 16)
            pool.wait_ge(norm[2]["tok"], 2 * TILES)
            norm_rows(3, (gain[:, :], t["ln_mix_g"][1], D), (bias[:, :], t["ln_mix_b"][1], D))
            for n, (c, k) in enumerate(((slice(0, 2), 2), (slice(2, 3), 3), (slice(3, 4), 4))):
                pool.wait_ge(mla["sumsq"], k)
                root(rstd[:, c], sumsq[:, c], MLA_EPS).then_inc(mla["rstd"], 1)
            layer_norm_root(3)

            pool.wait_ge(norm[3]["tok"], 2 * TILES)
            norm_rows(4, (gain[:, :], t["ln_ff_g"][1], D), (bias[:, :], t["ln_ff_b"][1], D),
                      (gain2[:, :], t["ffn1_norm_2"][0], D))
            layer_norm_root(4)

            def rms_root(b):
                for tile in range(TILES):
                    pool.wait_ge(norm[b]["squares"], 2 * tile + 2)
                    r = rstd[:, 2 + tile:3 + tile]
                    then(nc.gpsimd.tensor_tensor(r, mean_sq[:, tile, 0:1], mean_sq[:, tile, 1:2], ALU.add))
                    root(r, r, RMS_EPS).then_inc(norm[b]["rstd"], 1)

            rms_root(4)
            pool.wait_ge(norm[4]["tok"], 2 * TILES)
            norm_rows(5, (gain[:, :], t["mix_norm_2"][0], D))
            pool.dma_start(gain2[:, :], spread(t["ssd_norm_2"][0], D)).then_inc(hy["rows"], 16)
            rms_root(5)

            pool.dma_start(a_row, spread(t["a_log_2"][0], SSD_HEADS)).then_inc(hy["rows"], 16)
            pool.dma_start(dtb_row, spread(t["dt_bias_2"][0], SSD_HEADS)).then_inc(hy["rows"], 16)
            pool.dma_start(dskip_row, spread(t["d_skip_2"][0], SSD_HEADS)).then_inc(hy["rows"], 16)
            pool.wait_ge(norm[5]["tok"], 2 * TILES)
            norm_rows(6, (gain[:, :], t["ffn2_norm_2"][0], D))
            pool.wait_ge(hy["rows"], 64)
            for g in range(4):
                tile, h = g // 2, g % 2
                y = heads(y_tok[:, tile, h * HALF:(h + 1) * HALF])
                pool.wait_ge(hy["xs_out"], g + 1)
                nc.gpsimd.tensor_tensor(y, y, per_head(dskip_row[:, 8 * h:8 * h + 8]), ALU.mult).then_inc(hy["y_skip"], 1)
            rel = t["rel_bias_2"][0]
            for h in range(HEADS):
                window = bass.AP(rel.tensor, rel.offset + h * REL + P + 1, [[1, P], [1, TOKENS]])
                pool.dma_start(hankel[:, h, :], window).then_inc(hy["hank"], 16)
            for tile in range(TILES):
                pool.wait_ge(hy["sumsq"], tile + 1)
                root(rstd[:, tile:tile + 1], sumsq[:, 2 + tile:3 + tile], RMS_EPS).then_inc(hy["rstd"], 1)
            rms_root(6)
            pool.wait_ge(norm[6]["tok"], 2 * TILES)
            norm_rows(7, (gain[:, :], t["final_norm_2"], D))
            rms_root(7)

        @block.scalar
        def _(act):
            steps = [0]

            def then(ins):
                steps[0] += 1
                ins.then_inc(act_step, 1)
                act.wait_ge(act_step, steps[0])

            def copy(dst, src, **kw):
                return nc.scalar.activation(dst, src, ACT.Copy, **kw)

            def round_slab(m):
                if m >= N_SLABS:
                    return
                act.wait_ge(landed[m % RING], landed_at[m])
                if m >= RING:
                    act.wait_ge(slab_used, m - RING + 1)
                copy(weight_hi[:, m % RING, 0:width[m]], raw[:, m % RING, 0:width[m]]).then_inc(hi_done, 1)

            def round_slab_at(m, off):
                act.wait_ge(landed[m % RING], off * (16 // RING) + landed_at[m])
                act.wait_ge(slab_used, off + (m - RING + 1))
                copy(weight_hi[:, m % RING, 0:width[m]], raw[:, m % RING, 0:width[m]]).then_inc(hi_done, 1)

            def operand_hi(b, last=None, between=False):
                def followers():
                    round_slab(last - 1 + RING)
                    round_slab(last + RING)

                for g in range(4):
                    tile, h = g // 2, g % 2
                    act.wait_ge(turned, 4 * b + g + 1)
                    copy(xh[:, 4 * h:4 * h + 4, tile * P:(tile + 1) * P],
                         up[g][:, :].rearrange("p (k n) -> p k n", k=4)).then_inc(operand_high, 1)
                    if between and g == 1:
                        followers()
                if last is not None and not between:
                    followers()

            def mean_squares(b):
                for n in range(2 * TILES):
                    tile, h = n // 2, n % 2
                    c = slice(h * HALF, (h + 1) * HALF)
                    act.wait_ge(norm[b]["resid"], n + 1)
                    nc.scalar.activation(normed[:, tile, c], x_tok[:, tile, c], ACT.Square, scale=float(D) ** -0.5,
                                         accum_out=mean_sq[:, tile, h:h + 1]).then_inc(norm[b]["squares"], 1)

            operand_hi(0)
            for m in range(RING):
                round_slab(m)
            m = S_SC
            for c in range(SC_CHUNKS + 1):
                if c < SC_CHUNKS:
                    round_slab(m + RING)
                    act.wait_ge(slab_used, m + 2)
                    if c:
                        act.wait_ge(sc["ch_made"], c)
                    copy(tmp_a[:, :], up[1][:, :]).then_inc(sc["c_copied"], 1)
                    round_slab(m + 1 + RING)
                    if c == 0:
                        act.wait_ge(cols_turned, 1)
                        copy(cols[:, :], up[3][:, 0:ROWS]).then_inc(cols_ready, 1)
                        act.wait_ge(cols_ready, 1)
                    act.wait_ge(sc["ch_made"], c + 1)
                    if c:
                        act.wait_ge(sc["y_made"], c)
                    for f in range(CT):
                        tap = cols[:, ROW_SC + (SC_TAPS - 1) * KD + CT * c + f:][:, 0:1]
                        nc.scalar.activation(tmp_c[:, f * TOKENS:(f + 1) * TOKENS],
                                             tmp_b[:, f * TOKENS:(f + 1) * TOKENS], ACT.Copy, scale=tap)\
                            .then_inc(sc["conv0"], 1)
                    act.wait_ge(sc["y_made"], c + 1)
                    copy(hh[:, CT * (c % 2):CT * (c % 2) + CT, :],
                         tmp_d[:, :].rearrange("p (f n) -> p f n", f=CT)).then_inc(sc["y_hi"], 1)
                    round_slab(m + 2 + RING)
                    m += 3
                if 0 < c < SC_CHUNKS:
                    round_slab(m + RING)
                    m += 1

            def mlp_part(i):
                s, q = S_FF[i], mlp[i]

                def relu(c, par):
                    nc.scalar.activation(tmp_a[:, :], up[par][:, :], ACT.Relu).then_inc(q["relu"], 1)

                def hidden_hi(par):
                    copy(hh[:, CT * par:CT * par + CT, :], tmp_b[:, :].rearrange("p (f n) -> p f n", f=CT))\
                        .then_inc(q["hidden_hi"], 1)

                act.wait_ge(slab_used, s + 1)
                relu(0, 0)
                round_slab(s + RING)
                act.wait_ge(q["squared"], 1)
                hidden_hi(0)
                with act.Fori(0, FF_CHUNKS // 2 - 1) as it:
                    for j in range(4):
                        n = s + 1 + j
                        if j % 2 == 0:
                            par = (1, 0)[j // 2]
                            act.wait_ge(slab_used, 4 * it + (n + 1))
                            act.wait_ge(q["chunk"], 2 * it + (1 + j // 2))
                            relu(0, par)
                        round_slab_at(n + RING, 4 * it)
                        if j % 2 == 0:
                            act.wait_ge(q["squared"], 2 * it + (2 + j // 2))
                            hidden_hi(par)
                n = s + N_FF - 3
                act.wait_ge(slab_used, n + 1)
                act.wait_ge(q["chunk"], FF_CHUNKS - 1)
                relu(0, 1)
                act.wait_ge(q["squared"], FF_CHUNKS)
                hidden_hi(1)
                round_slab(n + RING)

            def glu_part(i):
                s, q = S_SG[i], glu[i]

                def gate(par):
                    nc.scalar.activation(tmp_a[:, :], up[2 * par][:, :], ACT.Silu).then_inc(q["gate"], 1)

                def hidden_hi(par):
                    copy(hh[:, CT * par:CT * par + CT, :], tmp_b[:, :].rearrange("p (f n) -> p f n", f=CT))\
                        .then_inc(q["hidden_hi"], 1)

                act.wait_ge(slab_used, s + 1)
                gate(0)
                round_slab(s + RING)
                round_slab(s + 1 + RING)
                act.wait_ge(q["hidden"], 1)
                hidden_hi(0)
                def two_chunks(off, chunk, rounded):
                    for j in range(8):
                        n = s + 2 + j
                        par = (1, 0)[j // 4]
                        if j % 4 == 0:
                            act.wait_ge(slab_used, off + (n + 1))
                            act.wait_ge(q["chunk"], chunk + (1 + j // 4))
                            gate(par)
                        rounded(n + RING)
                        if j % 4 == 1:
                            act.wait_ge(q["hidden"], chunk + (2 + j // 4))
                            hidden_hi(par)

                with act.Fori(0, GLU_PASSES) as it:
                    two_chunks(8 * it, 2 * it, lambda m: round_slab_at(m, 8 * it))
                two_chunks(8 * GLU_PASSES, 2 * GLU_PASSES, lambda m: round_slab(m + 8 * GLU_PASSES))

            operand_hi(1)
            round_slab(S_FF[0] - 1 + RING)
            mlp_part(0)
            operand_hi(2, S_MLA - 1, between=True)

            act.wait_ge(slab_used, DQ + 2)
            for tile in range(TILES):
                nc.scalar.activation((tmp_a, tmp_b)[tile][:, 0:Q_LORA],
                                     acc[:, 2 * tile, 0:Q_LORA], ACT.Square, scale=float(Q_LORA) ** -0.5,
                                     accum_out=sumsq[:, tile:tile + 1]).then_inc(mla["sumsq"], 1)
            round_slab(DQ + RING)
            round_slab(DQ + 1 + RING)
            for tile in range(TILES):
                act.wait_ge(mla["latent_ps"], 1 + tile)
                nc.scalar.activation((tmp_c, tmp_d)[tile][:, 0:KV_LORA], acc[:, 2 * tile + 1, 0:KV_LORA], ACT.Square,
                                     scale=float(KV_LORA) ** -0.5, accum_out=sumsq[:, 2 + tile:3 + tile])\
                    .then_inc(mla["sumsq"], 1)

            def latent_hi(g, k, n):
                act.wait_ge(mla["turned"], g + 1)
                copy(xh[:, k:k + n, :], up[1 + g][:, 0:n * TOKENS].rearrange("p (k n) -> p k n", k=n))\
                    .then_inc(mla["t_hi"], 1)

            latent_hi(0, 0, 2)
            latent_hi(1, 2, 1)
            act.wait_ge(slab_used, KV + 2)
            copy(pe_raw[:, 0, :], up[0][:, 0:TOKENS]).then_inc(mla["pe"], 1)
            latent_hi(2, 3, 2)
            round_slab(KV + RING)
            round_slab(KV + 1 + RING)
            for j in range(4):
                act.wait_ge(slab_used, UQ + j + 1)
                if j:
                    act.wait_ge(mla["rotated"], j)
                copy(pe_raw[:, (j + 1) % 2, :], up[2 + j % 2][:, 0:TOKENS]).then_inc(mla["pe"], 1)
                copy(q_nope[:, 2 * j:2 * j + 2, :], up[j % 2][:, :].rearrange("p (h n) -> p h n", h=2))\
                    .then_inc(mla["q_out"], 1)
                round_slab(UQ + j + RING)
            for j in range(4):
                if j < 3:
                    act.wait_ge(mla["k_ps"], j + 1)
                else:
                    act.wait_ge(slab_used, UK + 1)
                copy(k_nope[:, 2 * j:2 * j + 2, :], up[j][:, :].rearrange("p (h n) -> p h n", h=2))\
                    .then_inc(mla["k_out"], 1)
            act.wait_ge(slab_used, UV + 1)
            copy(v_a[:, 0, :].rearrange("p (h n) -> p h n", h=2), acc[:, 0:2, :]).then_inc(mla["v0"], 1)

            def attention_part(i, scale, prob, prob_t, o_hi, o_tiles, beside=None):
                q = att[i]
                for h in range(HEADS + 3):
                    if h < HEADS:
                        act.wait_ge(q["negmax"], h + 1)
                        if h >= 2:
                            act.wait_ge(q["turned"], h - 1)
                        S = up[h % 3]
                        nc.scalar.activation(prob[:, h % 2, 0:P], S[:, 0:P], ACT.Exp, scale=scale,
                                             bias=head_max[:, 1, h, 0:1], accum_out=head_sum[:, 0, h, 0:1])\
                            .then_inc(q["probs"], 1)
                        nc.scalar.activation(prob[:, h % 2, P:384], S[:, P:384], ACT.Exp, scale=scale,
                                             bias=head_max[:, 1, h, 1:2], accum_out=head_sum[:, 0, h, 1:2])\
                            .then_inc(q["probs"], 1)
                    if 1 <= h <= HEADS:
                        g = h - 1
                        act.wait_ge(q["turned"], g + 1)
                        if g >= 2:
                            act.wait_ge(q["o_ps"], g - 1)
                        copy(prob_t[:, g % 2, :], acc[:, g % 2, 0:384]).then_inc(q["t_out"], 1)
                    if h >= 3:
                        g = h - 3
                        act.wait_ge(q["o_ps"], g + 1)
                        dst, src = o_tiles(g)
                        copy(o_hi(dst), src).then_inc(q["o_hi"], 1)
                    if beside:
                        beside(h)

            def mla_out(g):
                return (slice(0, P), g), acc[:, 2 + g % 2, 0:TOKENS]

            attention_part(0, QK_SCALE, prob_a, prob_t_a, lambda d: xh[d[0], d[1], :], mla_out)
            for m in (UK, UV, WO, WO + 1):
                round_slab(m + RING)
            operand_hi(3, WO + 3)

            mlp_part(1)
            mean_squares(4)
            operand_hi(4, S_SG[0] - 1)
            glu_part(0)
            mean_squares(5)
            operand_hi(5, S_HY - 1)

            for tile in range(TILES):
                act.wait_ge(slab_used, HV + 2)
                copy(v_b[:, tile, :], acc[:, tile, :]).then_inc(hy["v_out"], 1)
            round_slab(HV + RING)
            round_slab(HV + 1 + RING)
            act.wait_ge(hy["dt_abs"], 1)
            nc.scalar.activation(dt_work[:, 2, :], dt_work[:, 1, :], ACT.Exp).then_inc(hy["dt_exp"], 1)
            act.wait_ge(hy["rows"], 64)
            nc.scalar.activation(dt_work[:, 9, 0:SSD_HEADS], a_row, ACT.Exp).then_inc(hy["dt_exp"], 1)
            round_slab(HDT + RING)

            def conv_out(j):
                act.wait_ge(hy["conv"], j + 1)
                dst = xs_t[:, CT * j:CT * j + CT, :] if j < 4 else bc_t[:, CT * (j - 4):CT * (j - 4) + CT, :]
                nc.scalar.activation(dst, (tmp_a, tmp_b)[j % 2][:, :].rearrange("p (f n) -> p f n", f=CT), ACT.Silu)\
                    .then_inc(hy["xbc"], 1)

            for j in range(6):
                act.wait_ge(slab_used, HX + j + 1)
                cy = (tmp_a, tmp_b)[j % 2]
                if j >= 2:
                    act.wait_ge(hy["xbc"], j - 1)
                for f in range(CT):
                    ft = CT * j + f
                    nc.scalar.activation(
                        cy[:, f * TOKENS:(f + 1) * TOKENS], up[j % 4][:, f * TOKENS:(f + 1) * TOKENS], ACT.Identity,
                        scale=cols[:, ROW_XBC + (XBC_TAPS - 1) * XT + ft:][:, 0:1],
                        bias=cols[:, ROW_XBC_B + ft:][:, 0:1]).then_inc(hy["tap0"], 1)
                round_slab(HX + j + RING)
                if j:
                    conv_out(j - 1)
            conv_out(5)

            def keys_queries(j):
                act.wait_ge(slab_used, HQK + j + 1)
                dst = (q_b, k_b)[j // 2][:, CT * (j % 2):CT * (j % 2) + CT, :]
                copy(dst, up[2 + j % 2][:, :].rearrange("p (f n) -> p f n", f=CT),
                     scale=(float(ATT_HD) ** -0.5 if j < 2 else 1.0)).then_inc(hy["qk_out"], 1)
                round_slab(HQK + j + RING)

            act.wait_ge(hy["cum_ps"], 1)
            nc.scalar.activation(dt_work[:, 7, :], acc[:, 2, 32:64], ACT.Exp).then_inc(hy["decays"], 1)
            keys_queries(0)
            for g in range(4):
                act.wait_ge(hy["xs_ps"], g + 1)
                copy(y_tok[:, g // 2, g % 2 * HALF:(g % 2 + 1) * HALF], acc[:, g, :]).then_inc(hy["xs_out"], 1)
            keys_queries(1)
            for g in range(SSD_GROUPS):
                act.wait_ge(hy["cb_ps"], g + 1)
                copy(cb_off[:, g, :], up[g][:, P:2 * P]).then_inc(hy["cb_act"], 1)
            keys_queries(2)
            keys_queries(3)
            for p in range(4):
                for n in (2 * p, 2 * p + 1):
                    act.wait_ge(hy["seg"], n + 1)
                    if n >= 2:
                        act.wait_ge(hy["y_ps"], n - 1)
                    nc.scalar.activation((tmp_c, tmp_d)[n % 2][:, :], (tmp_a, tmp_b)[n % 2][:, :], ACT.Exp)\
                        .then_inc(hy["exp"], 1)
                act.wait_ge(slab_used, HZ + p + 1)
                if p == 0:
                    act.wait_ge(hy["off_ps"], SSD_GROUPS)
                for tile in range(TILES):
                    nc.scalar.activation(z_gate[tile][:, p * TOKENS:(p + 1) * TOKENS],
                                         up[2 + p % 2][:, tile * TOKENS:(tile + 1) * TOKENS], ACT.Silu)\
                        .then_inc(hy["z_gate"], 1)
                if p < 3:
                    round_slab(HZ + p + RING)

            def y_beside(h):
                if h in (3, 4):
                    tile = h - 3
                    act.wait_ge(hy["y_gated"], 1 + tile)
                    nc.scalar.activation(z_gate[tile][:, :], y_tok[:, tile, :], ACT.Square, scale=float(D) ** -0.5,
                                         accum_out=sumsq[:, 2 + tile:3 + tile]).then_inc(hy["sumsq"], 1)
                if 5 <= h < 9:
                    g = h - 5
                    act.wait_ge(hy["y_ps_t"], g + 1)
                    copy(xh[:, 4 * (g % 2):4 * (g % 2) + 4, (g // 2) * P:(g // 2 + 1) * P],
                         up[3][:, :].rearrange("p (k n) -> p k n", k=4)).then_inc(hy["y_hi"], 1)

            def hybrid_out(g):
                o = ATT_HD * (g % 2)
                return (slice(o, o + ATT_HD), g // 2), acc[o:o + ATT_HD, 2 + g % 2, 0:TOKENS]

            attention_part(1, 1.0, prob_b, prob_t_b, lambda d: hh[d[0], d[1], :], hybrid_out, y_beside)
            for m in [HZ + 3] + [HWO + j for j in range(4)]:
                round_slab(m + RING)
            mean_squares(6)
            operand_hi(6, HWO + 5)
            glu_part(1)
            mean_squares(7)

        @block.vector
        def _(dve):
            steps = [0]
            vec = nc.vector

            def then(ins):
                steps[0] += 1
                ins.then_inc(dve_step, 1)
                dve.wait_ge(dve_step, steps[0])

            def rest(dst, whole, high):
                return vec.tensor_tensor(dst, whole, high.bitcast(F32), ALU.subtract)

            def split_slab(m):
                if m >= N_SLABS:
                    return
                dve.wait_ge(hi_done, m + 1)
                w = width[m]
                rest(weight_lo[:, m % RING, 0:w], raw[:, m % RING, 0:w], weight_hi[:, m % RING, 0:w])\
                    .then_inc(lo_done, 1)

            def split_slab_at(m, off):
                dve.wait_ge(hi_done, off + (m + 1))
                w = width[m]
                rest(weight_lo[:, m % RING, 0:w], raw[:, m % RING, 0:w], weight_hi[:, m % RING, 0:w])\
                    .then_inc(lo_done, 1)

            def halves(a):
                return a.rearrange("p (h n) -> p h n", h=2)

            def operand_lo(b, tiles=range(TILES)):
                for tile in tiles:
                    for h in range(2):
                        g = 2 * tile + h
                        dve.wait_ge(operand_high, 4 * b + g + 1)
                        rest(xl[:, 4 * h:4 * h + 4, tile * P:(tile + 1) * P],
                             up[g][:, :].rearrange("p (k n) -> p k n", k=4),
                             xh[:, 4 * h:4 * h + 4, tile * P:(tile + 1) * P]).then_inc(operand_low, 1)

            def product_done(b, tile, h, last):
                if tile == 0:
                    dve.wait_ge(acc_part, 2 * (b - 1) + 1)
                elif h == 0:
                    dve.wait_ge(acc_part, 2 * (b - 1) + 2)
                else:
                    dve.wait_ge(slab_used, last + 1)

            HALVES = (slice(0, HALF), slice(HALF, D))

            def layer_norm(b, last, rows_landed, ready, middle=None, hurry=False):
                for tile in range(TILES):
                    x = x_tok[:, tile, :]
                    for h, c in enumerate(HALVES):
                        product_done(b, tile, h, last)
                        then(vec.scalar_tensor_tensor(x[:, c], x[:, c], ALPHA, acc[:, 2 * tile + h, :],
                                                      ALU.mult, ALU.add))
                        ins = vec.bn_stats(stat[:, tile, h, :], x[:, c])
                    then(ins)
                    vec.bn_aggr(mean_var[:, tile, :], stat[:, tile, :, :].rearrange("p a b -> p (a b)"))\
                        .then_inc(norm[b]["stat"], 1)
                    if tile and hurry:
                        middle()
                    dve.wait_ge(norm[b]["rows"], rows_landed)
                    dve.wait_ge(norm[b]["stat"], tile + 1)
                    for c in HALVES:
                        ins = vec.scalar_tensor_tensor(x[:, c], x[:, c], mean_var[:, tile, 0:1], gain[:, c],
                                                       ALU.subtract, ALU.mult)
                    then(ins)
                    if tile and middle and not hurry:
                        middle()
                    dve.wait_ge(norm[b]["rstd"], tile + 1)
                    for c in HALVES:
                        vec.scalar_tensor_tensor(x[:, c], x[:, c], rstd[:, tile:tile + 1], bias[:, c],
                                                 ALU.mult, ALU.add).then_inc(norm[b][ready], 1)

            def add_product(b, last, factor, parts=range(2 * TILES)):
                for n in parts:
                    tile, h = n // 2, n % 2
                    x = x_tok[:, tile, HALVES[h]]
                    product_done(b, tile, h, last)
                    vec.scalar_tensor_tensor(x, acc[:, n, :], factor, x, ALU.mult, ALU.add)\
                        .then_inc(norm[b]["resid"], 1)

            def rms_norm(b, row, roots_before, rows_landed, tiles=range(TILES)):
                for tile in tiles:
                    dve.wait_ge(norm[b]["rstd"], roots_before + tile + 1)
                    dve.wait_ge(norm[b]["rows"], rows_landed)
                    for c in HALVES:
                        vec.scalar_tensor_tensor(normed[:, tile, c], x_tok[:, tile, c], rstd[:, 2 + tile:3 + tile],
                                                 row[:, c], ALU.mult, ALU.mult).then_inc(norm[b]["tok"], 1)

            operand_lo(0)
            for m in range(RING):
                split_slab(m)

            m = S_SC
            for c in range(SC_CHUNKS):
                split_slab(m + RING)
                split_slab(m + 1 + RING)
                dve.wait_ge(slab_used, m + 3)
                dve.wait_ge(sc["c_copied"], c + 1)
                vec.tensor_tensor(tmp_b[:, :], up[2][:, :], tmp_a[:, :], ALU.mult).then_inc(sc["ch_made"], 1)
                if c == 0:
                    dve.wait_ge(cols_ready, 1)
                dve.wait_ge(sc["conv0"], CT * (c + 1))
                for back in (1, 2):
                    for f in range(CT):
                        o = f * TOKENS
                        row = ROW_SC + (SC_TAPS - 1 - back) * KD + CT * c + f
                        ins = vec.scalar_tensor_tensor(
                            tmp_c[:, o + back:o + TOKENS], tmp_b[:, o:o + TOKENS - back], cols[:, row:row + 1],
                            tmp_c[:, o + back:o + TOKENS], ALU.mult, ALU.add)
                    then(ins)
                b_bank = up[3 if c % 2 else 0]
                vec.tensor_tensor(tmp_d[:, :], b_bank[:, :], tmp_c[:, :], ALU.mult).then_inc(sc["y_made"], 1)
                dve.wait_ge(sc["y_hi"], c + 1)
                rest(hl[:, CT * (c % 2):CT * (c % 2) + CT, :], tmp_d[:, :].rearrange("p (f n) -> p f n", f=CT),
                     hh[:, CT * (c % 2):CT * (c % 2) + CT, :]).then_inc(sc["chunk"], 1)
                split_slab(m + 2 + RING)
                m += 3
                if c:
                    split_slab(m + RING)
                    m += 1
            layer_norm(1, S_SC + N_SC - 1, 32, "tok", lambda: operand_lo(1, [0]))
            operand_lo(1, [1])
            split_slab(S_FF[0] - 1 + RING)

            def followers(last):
                split_slab(last - 1 + RING)
                split_slab(last + RING)

            def hidden_lo(par):
                return rest(hl[:, CT * par:CT * par + CT, :], tmp_b[:, :].rearrange("p (f n) -> p f n", f=CT),
                            hh[:, CT * par:CT * par + CT, :])

            def mlp_part(i):
                s, q = S_FF[i], mlp[i]

                def square():
                    vec.tensor_tensor(tmp_b[:, :], tmp_a[:, :], tmp_a[:, :], ALU.mult).then_inc(q["squared"], 1)

                dve.wait_ge(q["relu"], 1)
                square()
                split_slab(s + RING)
                dve.wait_ge(q["hidden_hi"], 1)
                hidden_lo(0).then_inc(q["chunk"], 1)
                with dve.Fori(0, FF_CHUNKS // 2 - 1) as it:
                    for j in range(4):
                        n = s + 1 + j
                        par = (1, 0)[j // 2]
                        if j % 2 == 0:
                            dve.wait_ge(q["relu"], 2 * it + (2 + j // 2))
                            square()
                        split_slab_at(n + RING, 4 * it)
                        if j % 2 == 0:
                            dve.wait_ge(q["hidden_hi"], 2 * it + (2 + j // 2))
                            hidden_lo(par).then_inc(q["chunk"], 1)
                n = s + N_FF - 3
                dve.wait_ge(q["relu"], FF_CHUNKS)
                square()
                dve.wait_ge(q["hidden_hi"], FF_CHUNKS)
                hidden_lo(1).then_inc(q["chunk"], 1)
                split_slab(n + RING)

            def glu_part(i):
                s, q = S_SG[i], glu[i]

                def gated(par):
                    vec.tensor_tensor(tmp_b[:, :], up[2 * par + 1][:, :], tmp_a[:, :], ALU.mult)\
                        .then_inc(q["hidden"], 1)

                split_slab(s + RING)
                dve.wait_ge(slab_used, s + 2)
                dve.wait_ge(q["gate"], 1)
                gated(0)
                split_slab(s + 1 + RING)
                dve.wait_ge(q["hidden_hi"], 1)
                hidden_lo(0).then_inc(q["chunk"], 1)

                def two_chunks(off, chunk, split):
                    for j in range(8):
                        n = s + 2 + j
                        par = (1, 0)[j // 4]
                        if j % 4 == 1:
                            dve.wait_ge(slab_used, off + (n + 1))
                            dve.wait_ge(q["gate"], chunk + (2 + j // 4))
                            gated(par)
                        split(n + RING)
                        if j % 4 == 1:
                            dve.wait_ge(q["hidden_hi"], chunk + (2 + j // 4))
                            hidden_lo(par).then_inc(q["chunk"], 1)

                with dve.Fori(0, GLU_PASSES) as it:
                    two_chunks(8 * it, 2 * it, lambda m: split_slab_at(m, 8 * it))
                two_chunks(8 * GLU_PASSES, 2 * GLU_PASSES, lambda m: split_slab(m + 8 * GLU_PASSES))

            mlp_part(0)
            layer_norm(2, S_MLA - 1, 32, "tok", lambda: operand_lo(2, [0]), hurry=True)
            operand_lo(2, [1])
            followers(S_MLA - 1)

            dve.wait_ge(mla["rows"], 32)
            dve.wait_ge(mla["rstd"], 1)
            for tile in range(TILES):
                vec.scalar_tensor_tensor(latent_q[:, tile, :], acc[:, 2 * tile, 0:Q_LORA], rstd[:, tile:tile + 1], g_q,
                                         ALU.mult, ALU.mult).then_inc(mla["latent"], 1)
            split_slab(DQ + RING)
            split_slab(DQ + 1 + RING)
            for tile in range(TILES):
                dve.wait_ge(mla["rstd"], 2 + tile)
                vec.scalar_tensor_tensor(latent_kv[:, tile, :], acc[:, 2 * tile + 1, 0:KV_LORA],
                                         rstd[:, 2 + tile:3 + tile], g_kv, ALU.mult, ALU.mult)\
                    .then_inc(mla["latent"], 1)

            def rotate(r, dst):
                dve.wait_ge(mla["swapped"], r + 1)
                if r >= 1:
                    dve.wait_ge(mla["rotated"], r)
                vec.tensor_tensor(tmp_c[:, 0:TOKENS], pe_raw[:, r % 2, :], cos, ALU.mult)
                then(vec.tensor_tensor(tmp_d[:, 0:TOKENS], acc[:, 3, 0:TOKENS], sin, ALU.mult))
                vec.tensor_tensor(dst, tmp_c[:, 0:TOKENS], tmp_d[:, 0:TOKENS], ALU.add).then_inc(mla["rotated"], 1)

            for g, (k, n) in enumerate(((0, 2), (2, 1), (3, 2))):
                dve.wait_ge(mla["t_hi"], g + 1)
                rest(xl[:, k:k + n, :], up[1 + g][:, 0:n * TOKENS].rearrange("p (k n) -> p k n", k=n),
                     xh[:, k:k + n, :]).then_inc(mla["t_lo"], 1)
            split_slab(KV + RING)
            split_slab(KV + 1 + RING)
            rotate(0, k_rot)
            for j in range(4):
                split_slab(UQ + j + RING)
                rotate(j + 1, q_rot[:, j, :])
            dve.wait_ge(slab_used, UV + 1)
            vec.tensor_copy(halves(v_a[:, 1, :]), acc[:, 2:4, :]).then_inc(mla["v1"], 1)

            def attention_part(i, scale, prob, o_part, o_lo, o_hi, beside=None):
                q = att[i]
                for h in range(HEADS + 3):
                    if h < HEADS:
                        dve.wait_ge(q["scores"], h + 1)
                        S = up[h % 3]
                        vec.reduce_max(head_max[:, 0, h, 0:1], S[:, 0:P], axis=AX_X)
                        then(vec.reduce_max(head_max[:, 0, h, 1:2], S[:, P:384], axis=AX_X))
                        vec.tensor_scalar(head_max[:, 1, h, :], head_max[:, 0, h, :], -scale, None, ALU.mult)\
                            .then_inc(q["negmax"], 1)
                    if 1 <= h <= HEADS:
                        g = h - 1
                        dve.wait_ge(q["probs"], 2 * g + 2)
                        then(vec.reciprocal(head_sum[:, 1, g, :], head_sum[:, 0, g, :]))
                        for a, b, n in ((0, P, 0), (P, 384, 1)):
                            vec.tensor_scalar(prob[:, g % 2, a:b], prob[:, g % 2, a:b], head_sum[:, 1, g, n:n + 1], None,
                                              ALU.mult).then_inc(q["normed"], 1)
                    if h >= 3:
                        g = h - 3
                        dve.wait_ge(q["o_hi"], g + 1)
                        dst, src = o_part(g)
                        rest(o_lo(dst), src, o_hi(dst)).then_inc(q["o_lo"], 1)
                    if beside:
                        beside(h)

            attention_part(0, QK_SCALE, prob_a, lambda g: ((slice(0, P), g), acc[:, 2 + g % 2, 0:TOKENS]),
                           lambda d: xl[d[0], d[1], :], lambda d: xh[d[0], d[1], :])
            for m in (UK, UV, WO, WO + 1):
                split_slab(m + RING)
            layer_norm(3, WO + 3, 32, "tok", lambda: operand_lo(3, [0]))
            operand_lo(3, [1])
            followers(WO + 3)

            mlp_part(1)
            layer_norm(4, S_SG[0] - 1, 48, "resid", lambda: rms_norm(4, gain2[:, :], TILES, 48, [0]))
            rms_norm(4, gain2[:, :], TILES, 48, [1])
            operand_lo(4)
            followers(S_SG[0] - 1)
            glu_part(0)
            add_product(5, S_HY - 1, 0.5, range(3))
            rms_norm(5, gain[:, :], 0, 16, [0])
            add_product(5, S_HY - 1, 0.5, [3])
            operand_lo(5, [0])
            rms_norm(5, gain[:, :], 0, 16, [1])
            operand_lo(5, [1])
            followers(S_HY - 1)

            split_slab(HV + RING)
            split_slab(HV + 1 + RING)
            x_dt, neg_abs, e_dt, z_dt, z2_dt, series, dt, _, adt, exp_a = [dt_work[:, i, :] for i in range(10)]
            nadt = z_dt
            dve.wait_ge(slab_used, HDT + 1)
            dve.wait_ge(hy["rows"], 64)
            for tile in range(TILES):
                sl = slice(tile * SSD_HEADS, (tile + 1) * SSD_HEADS)
                ins = vec.tensor_tensor(x_dt[:, sl], acc[:, 2, sl], dtb_row, ALU.add)
            then(ins)
            then(vec.tensor_scalar(neg_abs, x_dt, -1.0, None, ALU.mult))
            vec.tensor_tensor(neg_abs, neg_abs, x_dt, ALU.min).then_inc(hy["dt_abs"], 1)
            split_slab(HDT + RING)
            dve.wait_ge(hy["dt_exp"], 2)
            then(vec.tensor_scalar(z_dt, e_dt, 2.0, None, ALU.add))
            then(vec.reciprocal(z_dt, z_dt))
            then(vec.tensor_tensor(z_dt, z_dt, e_dt, ALU.mult))
            then(vec.tensor_tensor(z2_dt, z_dt, z_dt, ALU.mult))
            then(vec.tensor_scalar(series, z2_dt, 1.0 / 19, None, ALU.mult))
            for k in (17, 15, 13, 11, 9, 7, 5, 3):
                then(vec.scalar_tensor_tensor(series, series, 1.0 / k, z2_dt, ALU.add, ALU.mult))
            then(vec.scalar_tensor_tensor(series, series, 1.0, z_dt, ALU.add, ALU.mult))
            then(vec.tensor_scalar(dt, x_dt, 0.0, None, ALU.max))
            then(vec.scalar_tensor_tensor(dt, series, 2.0, dt, ALU.mult, ALU.add))
            for tile in range(TILES):
                sl = slice(tile * SSD_HEADS, (tile + 1) * SSD_HEADS)
                ins = vec.tensor_tensor(nadt[:, sl], dt[:, sl], exp_a[:, 0:SSD_HEADS], ALU.mult)
            then(ins)
            vec.tensor_scalar(adt, nadt, -1.0, None, ALU.mult).then_inc(hy["adt"], 1)
            for j in range(6):
                cy, ps = (tmp_a, tmp_b)[j % 2], up[j % 4]
                dve.wait_ge(hy["tap0"], CT * (j + 1))
                for back in (1, 2, 3):
                    for f in range(CT):
                        o = f * TOKENS
                        row = ROW_XBC + (XBC_TAPS - 1 - back) * XT + CT * j + f
                        ins = vec.scalar_tensor_tensor(
                            cy[:, o + back:o + TOKENS], ps[:, o:o + TOKENS - back], cols[:, row:row + 1],
                            cy[:, o + back:o + TOKENS], ALU.mult, ALU.add)
                    if back < 3:
                        then(ins)
                ins.then_inc(hy["conv"], 1)
                split_slab(HX + j + RING)

            split_slab(HQK + RING)
            for g in range(4):
                tile, h = g // 2, g % 2
                dve.wait_ge(hy["xs_out"], g + 1)
                hd = tile * SSD_HEADS + 8 * h
                vec.tensor_tensor(heads(xdt[:, tile, h * HALF:(h + 1) * HALF]), heads(acc[:, g, :]),
                                  per_head(dt[:, hd:hd + 8]), ALU.mult).then_inc(hy["xdt"], 1)
                if g == 1:
                    dve.wait_ge(hy["decays"], 1)
                    dve.wait_ge(hy["xdt"], 2)
                    vec.tensor_tensor(heads(xdt_end, SSD_HEADS), heads(xdt[:, 0, :], SSD_HEADS),
                                      per_head(dt_work[:, 7, 0:SSD_HEADS], SSD_HEADS), ALU.mult).then_inc(hy["cb"], 1)
            split_slab(HQK + 1 + RING)
            for g in range(SSD_GROUPS):
                dve.wait_ge(hy["cb_act"], g + 1)
                for tile in range(TILES):
                    vec.tensor_tensor(cb_diag[:, 2 * g + tile, :], up[g][:, 2 * P * tile:2 * P * tile + P], tri, ALU.mult)\
                        .then_inc(hy["cb"], 1)
            split_slab(HQK + 2 + RING)
            dve.wait_ge(hy["y_skip"], 4)
            for g in range(SSD_GROUPS):
                dve.wait_ge(hy["off_ps"], g + 1)
                part = (tmp_a, tmp_b)[g][:, :]
                vec.tensor_tensor(heads(part), heads(up[g][:, :]),
                                  per_head(dt_work[:, 7, SSD_HEADS + 8 * g:SSD_HEADS + 8 * g + 8]), ALU.mult)\
                    .then_inc(hy["off_taken"], 1)
            dve.wait_ge(hy["off_taken"], SSD_GROUPS)
            for g in range(SSD_GROUPS):
                y = y_tok[:, 1, g * HALF:(g + 1) * HALF]
                vec.tensor_tensor(y, y, (tmp_a, tmp_b)[g][:, :], ALU.add).then_inc(hy["y_sum"], 1)
            dve.wait_ge(hy["y_sum"], SSD_GROUPS)
            split_slab(HQK + 3 + RING)
            dve.wait_ge(hy["cb"], 5)
            for p in range(4 + 1):
                if p < 4:
                    for n in (2 * p, 2 * p + 1):
                        dve.wait_ge(hy["seg_ps"], n + 1)
                        if n >= 2:
                            dve.wait_ge(hy["exp"], n - 1)
                        vec.tensor_scalar((tmp_a, tmp_b)[n % 2][:, :], up[n % 2][:, :], 0.0, None, ALU.min)\
                            .then_inc(hy["seg"], 1)
                    for n in (2 * p, 2 * p + 1):
                        g, tile = p % 2, p // 2
                        dve.wait_ge(hy["exp"], n + 1)
                        w = (tmp_c, tmp_d)[n % 2][:, :].rearrange("p (h l) -> p h l", h=4)
                        cb = cb_diag[:, 2 * g + tile:2 * g + tile + 1, :].to_broadcast([P, 4, P])
                        vec.tensor_tensor(w, w, cb, ALU.mult).then_inc(hy["seg_w"], 1)
                if p >= 1:
                    g, tile = (p - 1) % 2, (p - 1) // 2
                    y = y_tok[:, tile, g * HALF:(g + 1) * HALF]
                    dve.wait_ge(hy["y_ps"], 2 * p)
                    vec.tensor_tensor(y, acc[:, 2 * tile + g, :], y, ALU.add).then_inc(hy["y_sum"], 1)
                    if p < 4:
                        split_slab(HZ + p - 1 + RING)

            def y_beside(h):
                if h < 2:
                    y = y_tok[:, h, :]
                    dve.wait_ge(hy["y_sum"], 4 + 2 * h)
                    dve.wait_ge(hy["z_gate"], 4 * TILES)
                    vec.tensor_tensor(y, y, z_gate[h][:, :], ALU.mult).then_inc(hy["y_gated"], 1)
                if h in (4, 5):
                    tile = h - 4
                    y = y_tok[:, tile, :]
                    dve.wait_ge(hy["rstd"], tile + 1)
                    vec.scalar_tensor_tensor(y, y, rstd[:, tile:tile + 1], gain2[:, :], ALU.mult, ALU.mult)\
                        .then_inc(hy["y_n"], 1)
                if 5 <= h < 9:
                    g = h - 5
                    tile, f = g // 2, g % 2
                    dve.wait_ge(hy["y_hi"], g + 1)
                    rest(xl[:, 4 * f:4 * f + 4, tile * P:(tile + 1) * P], up[3][:, :].rearrange("p (k n) -> p k n", k=4),
                         xh[:, 4 * f:4 * f + 4, tile * P:(tile + 1) * P]).then_inc(hy["y_lo"], 1)

            def hybrid_out(g):
                o = ATT_HD * (g % 2)
                return (slice(o, o + ATT_HD), g // 2), acc[o:o + ATT_HD, 2 + g % 2, 0:TOKENS]

            attention_part(1, 1.0, prob_b, hybrid_out, lambda d: hl[d[0], d[1], :], lambda d: hh[d[0], d[1], :], y_beside)
            for m in [HZ + 3] + [HWO + j for j in range(4)]:
                split_slab(m + RING)
            add_product(6, HWO + 5, 1.0)
            rms_norm(6, gain[:, :], 0, 16)
            operand_lo(6)
            followers(HWO + 5)
            glu_part(1)
            add_product(7, S_SG[1] + N_SG - 1, 0.5)
            rms_norm(7, gain[:, :], 0, 16)

        @block.tensor
        def _(pe):
            mm = nc.tensor.matmul

            def weights(m, off=0):
                pe.wait_ge(lo_done, off + (m + 1))

            def up_block(dst, m, col, step, k_tiles, x_tile=0, w_tile=0, first=True, last=True):
                for k in range(k_tiles):
                    c = (w_tile + k) * step + col
                    w_h = weight_hi[:, m % RING, c:c + P]
                    w_l = weight_lo[:, m % RING, c:c + P]
                    mm(dst, w_h, xh[:, x_tile + k, :], start=first and k == 0, stop=False)
                    mm(dst, w_h, xl[:, x_tile + k, :], start=False, stop=False)
                    ins = mm(dst, w_l, xh[:, x_tile + k, :], start=False, stop=last and k == k_tiles - 1)
                return ins

            def up_product(m, bank, b=None):
                for f in range(CT):
                    dst = bank[:, f * TOKENS:(f + 1) * TOKENS]
                    if b is None:
                        ins = up_block(dst, m, f * P, CHUNK_F, KD)
                        continue
                    w_h, w_l = [[w[:, m % RING, k * CHUNK_F + f * P:k * CHUNK_F + f * P + P] for k in range(KD)]
                                for w in (weight_hi, weight_lo)]
                    for k in range(KD):
                        if (f, k) == (0, 0):
                            pe.wait_ge(operand_low, 4 * b + 1)
                        if f == 0 and k in (0, KD // 2):
                            pe.wait_ge(operand_high, 4 * b + 3 + k // 4)
                        mm(dst, w_h[k], xh[:, k, :], start=k == 0, stop=False)
                        mm(dst, w_l[k], xh[:, k, :], start=False, stop=False)
                    pe.wait_ge(operand_low, 4 * b + 4)
                    for k in range(KD):
                        ins = mm(dst, w_h[k], xl[:, k, :], start=False, stop=k == KD - 1)
                ins.then_inc(slab_used, 1)

            def token_block(dst, s_h, s_l, w_h, w_l, first, last):
                open_group = dict(skip_group_check=True)
                for d, h, l in zip(dst, w_h, w_l):
                    mm(d, s_h, h, start=first, stop=False, **open_group)
                    mm(d, s_h, l, start=False, stop=False, **open_group)
                for d, h in zip(dst, w_h):
                    ins = mm(d, s_l, h, start=False, stop=last, **open_group)
                return ins

            def down_block(m, s_h, s_l, j, tile, halves, first, last):
                cut = slice(tile * P, (tile + 1) * P)
                c = [slice(j * D + h * HALF, j * D + (h + 1) * HALF) for h in halves]
                return token_block([acc[:, 2 * tile + h, :] for h in halves], s_h(j)[:, cut], s_l(j)[:, cut],
                                   [weight_hi[:, m % RING, x] for x in c], [weight_lo[:, m % RING, x] for x in c],
                                   first, last)

            def down_product(m, s_h, s_l, k_tiles, first=False):
                for j in range(k_tiles):
                    for tile in range(TILES):
                        ins = down_block(m, s_h, s_l, j, tile, (0, 1), first and j == 0, False)
                ins.then_inc(slab_used, 1)

            def last_products(b, k_tiles, slabs):
                for tile, halves in ((0, (0, 1)), (1, (0,)), (1, (1,))):
                    for n, (m, s_h, s_l, ready) in enumerate(slabs):
                        if tile == 0:
                            weights(m)
                            ready()
                        for j in range(k_tiles):
                            ins = down_block(m, s_h, s_l, j, tile, halves, False, (n, j) == (len(slabs) - 1, k_tiles - 1))
                        if tile and halves == (1,):
                            ins.then_inc(slab_used, 1)
                    if halves != (1,):
                        ins.then_inc(acc_part, 1)

            def hidden(par, j0=0):
                return (lambda j: hh[:, CT * par + j0 + j, :]), (lambda j: hl[:, CT * par + j0 + j, :])

            def keep_warm(n):
                for _ in range(n):
                    mm(up[3][:, :], zeros[0:1, 0:P], zeros[0:1, :], start=True, stop=True)

            def turn_tile(b, src, tile):
                if b == 0:
                    pe.wait_ge(x_landed[tile], 16)
                for h in range(2):
                    if b:
                        pe.wait_ge(norm[b]["tok"], 2 * tile + h + 1)
                    for j in range(4):
                        f = (4 * h + j) * P
                        ins = nc.tensor.transpose(up[2 * tile + h][:, j * P:(j + 1) * P], src[:, tile, f:f + P], ident)
                    ins.then_inc(turned, 1)

            def turn(b, src):
                if b:
                    keep_warm(WARM[b][0])
                turn_tile(b, src, 0)
                if b:
                    keep_warm(WARM[b][1])
                turn_tile(b, src, 1)
                if b in (1, 3, 4, 6):
                    clear_acc()

            def clear_acc():
                for n in range(4):
                    mm(acc[:, n, :], zeros[0:1, 0:P], zeros[0:1, :], start=True, stop=False, skip_group_check=True)

            WARM = {1: (8, 12), 3: (4, 12), 4: (16, 12), 6: (6, 4)}

            pe.wait_ge(ident_landed, 16)
            turn(0, x_tok)

            m = S_SC
            for c in range(SC_CHUNKS):
                weights(m)
                if c == 1:
                    pe.wait_ge(cols_ready, 1)
                up_product(m, up[3 if c % 2 else 0], 0 if c == 0 else None)
                weights(m + 1)
                if c:
                    pe.wait_ge(sc["c_copied"], c)
                up_product(m + 1, up[1])
                if c == 0:
                    pe.wait_ge(const_landed, 64)
                    nc.tensor.transpose(up[3][:, 0:ROWS], rows[:, :], ident[0:ROWS, 0:ROWS]).then_inc(cols_turned, 1)
                weights(m + 2)
                if c:
                    pe.wait_ge(sc["ch_made"], c)
                up_product(m + 2, up[2])
                m += 3
                if c:
                    weights(m)
                    pe.wait_ge(sc["chunk"], c)
                    down_product(m, *hidden((c - 1) % 2), CT, first=(c == 1))
                    m += 1
            last_products(1, CT, [(m, *hidden((SC_CHUNKS - 1) % 2), lambda: pe.wait_ge(sc["chunk"], SC_CHUNKS))])

            def mlp_part(i, b):
                s, q = S_FF[i], mlp[i]
                weights(s)
                up_product(s, up[0], b - 1)
                with pe.Fori(0, FF_CHUNKS // 2 - 1) as it:
                    for j in range(4):
                        m = s + 1 + j
                        weights(m, 4 * it)
                        if j % 2 == 0:
                            up_product(m, up[(1, 0)[j // 2]])
                        else:
                            pe.wait_ge(q["chunk"], 2 * it + (1 + j // 2))
                            down_product(m, *hidden(j // 2), CT)
                m = s + N_FF - 3
                weights(m)
                up_product(m, up[1])
                last_products(b, CT, [(m + 1, *hidden(0), lambda: pe.wait_ge(q["chunk"], FF_CHUNKS - 1)),
                                      (m + 2, *hidden(1), lambda: pe.wait_ge(q["chunk"], FF_CHUNKS))])

            def glu_part(i, b):
                s, q = S_SG[i], glu[i]
                for j in range(2):
                    weights(s + j)
                    up_product(s + j, up[j], None if j else b - 1)
                with pe.Fori(0, (SG_CHUNKS - 1) // 2) as it:
                    for j in range(8):
                        m = s + 2 + j
                        weights(m, 8 * it)
                        par = (1, 0)[j // 4]
                        if j % 4 < 2:
                            up_product(m, up[2 * par + j % 4])
                        else:
                            if j % 4 == 2:
                                pe.wait_ge(q["chunk"], 2 * it + (1 + j // 4))
                            down_product(m, *hidden(1 - par, j % 4 - 2), 1)
                m = s + N_SG - 2
                last_products(b, 1, [(m + j, *hidden(0, j), lambda: pe.wait_ge(q["chunk"], SG_CHUNKS)) for j in range(2)])

            turn(1, x_tok)
            mlp_part(0, 2)
            turn_tile(2, x_tok, 0)

            def token_product(m, dst, n, step, k_tiles, x_tile, first, last, tiles=range(TILES)):
                for tile in tiles:
                    for k in range(k_tiles):
                        c = k * step
                        cut = slice(tile * P, (tile + 1) * P)
                        ins = token_block([dst(tile)], xh[:, x_tile + k, cut], xl[:, x_tile + k, cut],
                                          [weight_hi[:, m % RING, c:c + n]], [weight_lo[:, m % RING, c:c + n]],
                                          first and k == 0, last and k == k_tiles - 1)
                return ins

            def query_latent(j, tile):
                return token_product(DQ + j, lambda t: acc[:, 2 * t, 0:Q_LORA], Q_LORA, Q_LORA, 4, 4 * j, j == 0, j == 1,
                                     [tile])

            def key_latent(j, tile):
                return token_product(KV + j, lambda t: acc[:, 2 * t + 1, 0:KV_LORA], KV_LORA, KV_COLS, 4, 4 * j,
                                     j == 0, j == 1, [tile])

            pe.wait_ge(operand_low, 4 * 2 + 2)
            for j in range(2):
                weights(DQ + j)
                query_latent(j, 0)
            turn_tile(2, x_tok, 1)
            pe.wait_ge(operand_low, 4 * 2 + 4)
            for j in range(2):
                query_latent(j, 1).then_inc(slab_used, 1)
            for tile in range(TILES):
                for j in range(2):
                    weights(KV + j)
                    ins = key_latent(j, tile)
                ins.then_inc(mla["latent_ps"], 1)
            for j in range(2):
                up_block(up[0][:, 0:TOKENS], KV + j, KV_LORA, KV_COLS, 4, 4 * j, 0, j == 0, j == 1)\
                    .then_inc(slab_used, 1)

            def partner(r):
                pe.wait_ge(mla["pe"], r + 1)
                if r:
                    pe.wait_ge(mla["rotated"], r)
                mm(acc[:, 3, 0:TOKENS], swap, pe_raw[:, r % 2, :], start=True, stop=True).then_inc(mla["swapped"], 1)

            for g in range(3):
                pe.wait_ge(mla["latent"], TILES if g < 2 else 2 * TILES)
                blocks = (((0, 0), (0, 1), (1, 0), (1, 1)), ((2, 0), (2, 1)), ((0, 0), (0, 1), (1, 0), (1, 1)))[g]
                src = latent_kv if g == 2 else latent_q
                for n, (k, tile) in enumerate(blocks):
                    ins = nc.tensor.transpose(up[1 + g][:, n * P:(n + 1) * P], src[:, tile, k * P:(k + 1) * P], ident)
                ins.then_inc(mla["turned"], 1)
            partner(0)
            pe.wait_ge(mla["t_lo"], 3)
            for j in range(4):
                weights(UQ + j)
                if j >= 2:
                    pe.wait_ge(mla["q_out"], j - 1)
                for f in range(2):
                    up_block(up[j % 2][:, f * TOKENS:(f + 1) * TOKENS], UQ + j, f * NOPE, UQ_COLS, KQ)
                up_block(up[2 + j % 2][:, 0:TOKENS], UQ + j, 2 * NOPE, UQ_COLS, KQ).then_inc(slab_used, 1)
                if j:
                    partner(j)
            weights(UK)
            pe.wait_ge(mla["q_out"], 4)
            for j in range(4):
                for f in range(2):
                    ins = up_block(up[j][:, f * TOKENS:(f + 1) * TOKENS], UK, (2 * j + f) * NOPE, D, KKV, KQ)
                ins.then_inc(mla["k_ps"] if j < 3 else slab_used, 1)
            partner(4)
            weights(UV)
            pe.wait_ge(mla["rotated"], 5)
            for k in range(KKV):
                for tile in range(TILES):
                    cut = slice(tile * P, (tile + 1) * P)
                    c = [slice(k * D + h * HALF, k * D + (h + 1) * HALF) for h in range(2)]
                    ins = token_block([acc[:, 2 * tile + h, :] for h in range(2)],
                                      xh[:, KQ + k, cut], xl[:, KQ + k, cut],
                                      [weight_hi[:, UV % RING, x] for x in c], [weight_lo[:, UV % RING, x] for x in c],
                                      k == 0, k == KKV - 1)
            ins.then_inc(slab_used, 1)

            def attention_part(i, score, prob, prob_t, v, o_dst, banks_free, beside=None):
                q = att[i]

                def scores(h):
                    if h >= 3:
                        pe.wait_ge(q["probs"], 2 * (h - 3) + 2)
                    S = up[h % 3]
                    score(h, 0, S[:, 0:P])
                    mm(S[:, P - ATTN_CHUNK:P], mask_row, mask_ones, start=False, stop=True, skip_group_check=True)
                    score(h, 1, S[:, P:384])
                    mm(S[:, 384 - ATTN_CHUNK:384], mask_row, mask_ones, start=False, stop=True, skip_group_check=True)\
                        .then_inc(q["scores"], 1)

                def turn_probs(g):
                    pe.wait_ge(q["normed"], 2 * g + 2)
                    if g >= 2:
                        pe.wait_ge(q["t_out"], g - 1)
                    for n in range(3):
                        ins = nc.tensor.transpose(acc[:, g % 2, n * P:(n + 1) * P], prob[:, g % 2, n * P:(n + 1) * P],
                                                  ident)
                    ins.then_inc(q["turned"], 1)

                def outputs(g):
                    pe.wait_ge(q["t_out"], g + 1)
                    if g >= 2:
                        pe.wait_ge(q["o_lo"], g - 1)
                    o = o_dst(g)
                    mm(o, v(0, g), prob_t[:, g % 2, 0:TOKENS], start=True, stop=False, skip_group_check=True)
                    mm(o[:, P:TOKENS], v(1, g), prob_t[:, g % 2, TOKENS:384], start=False, stop=True,
                       skip_group_check=True).then_inc(q["o_ps"], 1)

                scores(0)
                scores(1)
                for g in range(HEADS + 1):
                    if g + 2 < HEADS:
                        scores(g + 2)
                    if g == 0:
                        banks_free()
                    if g < HEADS:
                        turn_probs(g)
                        if beside:
                            beside(g)
                    if g:
                        outputs(g - 1)

            def mla_score(h, tile, dst):
                queries, keys = slice(tile * P, (tile + 1) * P), slice(0, (tile + 1) * P)
                r = slice(ROPE * (h % 2), ROPE * (h % 2) + ROPE)
                mm(dst, q_nope[:, h, queries], k_nope[:, h, keys], start=True, stop=False, skip_group_check=True)
                mm(dst, q_rot[r, h // 2, queries], k_rot[r, keys], start=False, stop=False, skip_group_check=True)

            def values_copied():
                pe.wait_ge(mla["v0"], 1)
                pe.wait_ge(mla["v1"], 1)

            pe.wait_ge(mla["k_out"], 4)
            attention_part(0, mla_score, prob_a, prob_t_a, lambda kt, h: v_a[:, kt, h * P:(h + 1) * P],
                           lambda h: acc[:, 2 + h % 2, 0:TOKENS], values_copied)
            def heads_out(c):
                return lambda: pe.wait_ge(att[0]["o_lo"], CT * c + 2)

            def latent_rows(c):
                return (lambda j: xh[:, CT * c + j, :]), (lambda j: xl[:, CT * c + j, :])

            for c in range(2):
                weights(WO + c)
                heads_out(c)()
                if c == 0:
                    pe.wait_ge(att[0]["t_out"], HEADS)
                    pe.wait_ge(att[0]["o_lo"], HEADS)
                down_product(WO + c, *latent_rows(c), CT, first=(c == 0))
            last_products(3, CT, [(WO + c, *latent_rows(c), heads_out(c)) for c in (2, 3)])

            turn(3, x_tok)
            mlp_part(1, 4)
            turn(4, normed)
            glu_part(0, 5)
            turn_tile(5, normed, 0)

            def values(j, tile):
                return token_product(HV + j, lambda t: acc[:, t, :], HALF, HALF, 4, 4 * j, j == 0, j == 1, [tile])

            pe.wait_ge(operand_low, 4 * 5 + 2)
            for j in range(2):
                weights(HV + j)
                values(j, 0)
            turn_tile(5, normed, 1)
            pe.wait_ge(operand_low, 4 * 5 + 4)
            for j in range(2):
                values(j, 1).then_inc(slab_used, 1)
            weights(HDT)
            token_product(HDT, lambda t: acc[:, 2, t * SSD_HEADS:(t + 1) * SSD_HEADS], SSD_HEADS, SSD_HEADS, KD, 0, True, True)\
                .then_inc(slab_used, 1)
            for j in range(6):
                weights(HX + j)
                if j >= 4:
                    pe.wait_ge(hy["conv"], j - 3)
                up_product(HX + j, up[j % 4])
                if j == 3:
                    pe.wait_ge(hy["adt"], 1)
                    mm(acc[:, 2, 32:32 + SSD_HEADS], after, adt_tile(0), start=True, stop=True)
                    mm(acc[:, 2, 32 + SSD_HEADS:64], tri, adt_tile(1), start=True, stop=True).then_inc(hy["cum_ps"], 1)

            def keys_queries(j):
                weights(HQK + j)
                if j < 2:
                    pe.wait_ge(hy["conv"], 3 + j)
                else:
                    pe.wait_ge(hy["qk_out"], j - 1)
                up_product(HQK + j, up[2 + j % 2])

            keys_queries(0)
            pe.wait_ge(hy["xbc"], 4)
            pe.wait_ge(hy["v_out"], TILES)
            pe.wait_ge(hy["decays"], 1)
            for g in range(4):
                tile, h = g // 2, g % 2
                for j in range(4):
                    ins = nc.tensor.transpose(acc[:, g, j * P:(j + 1) * P], xs_t[:, 4 * h + j, tile * P:(tile + 1) * P],
                                              ident)
                ins.then_inc(hy["xs_ps"], 1)
            keys_queries(1)
            pe.wait_ge(hy["xbc"], 6)
            for g in range(SSD_GROUPS):
                mm(up[g][:, 0:TOKENS], bc_t[:, g, 0:P], bc_t[:, 2 + g, :], start=True, stop=True)
                mm(up[g][:, TOKENS:384], bc_t[:, g, P:TOKENS], bc_t[:, 2 + g, P:TOKENS], start=True, stop=True)\
                    .then_inc(hy["cb_ps"], 1)
            keys_queries(2)
            pe.wait_ge(hy["cb"], 5)
            pe.wait_ge(hy["cb_act"], 2)
            for g in range(SSD_GROUPS):
                mm(up[g][:, :], cb_off[:, g, :], xdt_end[:, g * HALF:(g + 1) * HALF], start=True, stop=True)\
                    .then_inc(hy["off_ps"], 1)
            keys_queries(3)

            def decay_sums(n):
                tile, h0 = n // 4, 4 * (n % 4)
                bank = up[n % 2]
                if n >= 2:
                    pe.wait_ge(hy["seg"], n - 1)
                else:
                    pe.wait_ge(hy["off_taken"], n + 1)
                mm(bank[:, :].rearrange("p (h l) -> p h l", h=4), tri,
                   nadt_tile(tile)[:, h0:h0 + 4].unsqueeze(2).to_broadcast([P, 4, P]), start=True, stop=False,
                   skip_group_check=True)
                for q in range(4):
                    ins = mm(bank[:, q * P:(q + 1) * P], adt_tile(tile)[:, h0 + q:h0 + q + 1].to_broadcast([P, P]),
                             tri, start=False, stop=True, skip_group_check=True)
                ins.then_inc(hy["seg_ps"], 1)

            def scan_outputs(n):
                tile, h0 = n // 4, 4 * (n % 4)
                if n == 0:
                    pe.wait_ge(hy["xdt"], 4)
                    pe.wait_ge(hy["xs_out"], 4)
                pe.wait_ge(hy["seg_w"], n + 1)
                for q in range(4):
                    h = h0 + q
                    ins = mm(acc[:, 2 * tile + h // 8, h % 8 * SSD_HD:(h % 8 + 1) * SSD_HD],
                             (tmp_c, tmp_d)[n % 2][:, q * P:(q + 1) * P], xdt[:, tile, h * SSD_HD:(h + 1) * SSD_HD],
                             start=True, stop=True)
                ins.then_inc(hy["y_ps"], 1)

            for p in range(4):
                decay_sums(2 * p)
                decay_sums(2 * p + 1)
                weights(HZ + p)
                if p < 2:
                    pe.wait_ge(hy["qk_out"], 3 + p)
                else:
                    pe.wait_ge(hy["z_gate"], 2 * (p - 1))
                token_product(HZ + p, lambda t: up[2 + p % 2][:, t * TOKENS:(t + 1) * TOKENS], CHUNK_F, CHUNK_F, KD, 0,
                              True, True).then_inc(slab_used, 1)
                scan_outputs(2 * p)
                scan_outputs(2 * p + 1)

            def hybrid_score(h, tile, dst):
                queries, keys = slice(tile * P, (tile + 1) * P), slice(0, (tile + 1) * P)
                r = slice(ATT_HD * (h % 2), ATT_HD * (h % 2) + ATT_HD)
                mm(dst, q_b[r, h // 2, queries], k_b[r, h // 2, keys], start=True, stop=False, skip_group_check=True)
                for kt in range(tile + 1):
                    w0 = (tile - kt) * P
                    mm(dst[:, kt * P:(kt + 1) * P], hankel[:, h, w0:w0 + P], anti, start=False, stop=False,
                       skip_group_check=True)

            def banks_free():
                pe.wait_ge(hy["y_sum"], 2 + 4)

            def turn_y(g):
                if g < 4:
                    return
                tile, h = (g - 4) // 2, g % 2
                if g == 4:
                    pe.wait_ge(hy["z_gate"], 4 * TILES)
                else:
                    pe.wait_ge(hy["y_lo"], g - 4)
                pe.wait_ge(hy["y_n"], tile + 1)
                for j in range(4):
                    f = (4 * h + j) * P
                    ins = nc.tensor.transpose(up[3][:, j * P:(j + 1) * P], y_tok[:, tile, f:f + P], ident)
                ins.then_inc(hy["y_ps_t"], 1)

            pe.wait_ge(hy["hank"], 16 * HEADS)
            pe.wait_ge(hy["z_gate"], 3 * TILES)
            attention_part(1, hybrid_score, prob_b, prob_t_b, lambda kt, h: v_b[:, kt, h * ATT_HD:(h + 1) * ATT_HD],
                           lambda h: acc[ATT_HD * (h % 2):ATT_HD * (h % 2) + ATT_HD, 2 + h % 2, 0:TOKENS], banks_free, turn_y)
            pe.wait_ge(hy["y_lo"], 4)
            pe.wait_ge(att[1]["o_lo"], HEADS)
            for c in range(4):
                weights(HWO + c)
                down_product(HWO + c, *latent_rows(c), CT, first=(c == 0))

            def head_rows(c):
                return (lambda j: hh[:, CT * c + j, :]), (lambda j: hl[:, CT * c + j, :])

            last_products(6, CT, [(HWO + 4 + c, *head_rows(c), lambda: None) for c in range(2)])
            turn(6, normed)
            glu_part(1, 7)


_NAMES = [
    "x", "sc_w_in", "sc_conv_w", "sc_w_out", "mla_w_dq", "mla_g_q", "mla_w_uq", "mla_w_dkv", "mla_g_kv",
    "mla_w_uk", "mla_w_uv", "mla_w_o", "ff_w1", "ff_w2", "ln_mix_g", "ln_mix_b", "ln_ff_g", "ln_ff_b",
    "ffn1_norm_2", "ffn1_w_gate_2", "ffn1_w_up_2", "ffn1_w_down_2", "mix_norm_2", "w_in_2", "conv_w_2",
    "conv_b_2", "dt_bias_2", "a_log_2", "d_skip_2", "ssd_norm_2", "rel_bias_2", "w_out_2", "ffn2_norm_2",
    "ffn2_w_gate_2", "ffn2_w_up_2", "ffn2_w_down_2", "final_norm_2",
]


def kernel(**inputs):
    import concourse.bacc as bacc
    from concourse.bass_utils import run_bass_kernel_spmd

    nc = bacc.Bacc("TRN2", target_bir_lowering=False, num_devices=1)
    arrays = {name: np.ascontiguousarray(inputs[name]) for name in _NAMES}
    arrays["shape_consts"] = shape_constants()
    aps = {n: nc.dram_tensor(f"in_{n}", a.shape, mybir.dt.from_np(a.dtype), kind="ExternalInput").ap()
           for n, a in arrays.items()}
    out = nc.dram_tensor("out", (1, TOKENS, D), F32, kind="ExternalOutput").ap()
    two_blocks(nc, aps, aps["shape_consts"], out)
    r = run_bass_kernel_spmd(nc, [{f"in_{n}": a for n, a in arrays.items()}], core_ids=[0])
    return r.results[0]["out"]
```

```python
from contextlib import ExitStack

import numpy as np

import concourse.bass as bass
from concourse import mybir

F32 = mybir.dt.float32
F32R = mybir.dt.float32r
BF16 = mybir.dt.bfloat16
ACT = mybir.ActivationFunctionType
ALU = mybir.AluOpType
AX_X = mybir.AxisListType.X

P = 128
TOKENS = 256
TILES = TOKENS // P
D = 1024
KD = D // P
HALF = 512
CHUNK_F = 256
CT = CHUNK_F // P
RING = 4
SLAB = 2048
ATTN_CHUNK = 64

DEPTH = 2
ALPHA = (2.0 * DEPTH) ** 0.25
LN_EPS = 1e-5
MLA_EPS = 1e-6
RMS_EPS = 1e-5
D_FF = 4096
D_FF_2 = 2816
HEADS = 8
NOPE, ROPE, Q_LORA, KV_LORA = 128, 64, 384, 256
KQ, KKV = Q_LORA // P, KV_LORA // P
QK_SCALE = float(NOPE + ROPE) ** -0.5
SSD_HEADS, SSD_HD, SSD_GROUPS = 16, 64, 2
SSD_INNER = SSD_HEADS * SSD_HD
XBC = SSD_INNER + 2 * SSD_GROUPS * P
ATT_HD = 64
ATT_INNER = HEADS * ATT_HD
REL = 513
MIX = SSD_INNER + ATT_INNER
Z0, XBC0, DT0 = 0, SSD_INNER, SSD_INNER + XBC
Q0 = DT0 + SSD_HEADS
K0, V0 = Q0 + ATT_INNER, Q0 + 2 * ATT_INNER
MASKED = -1.0e30

SC_TAPS, XBC_TAPS = 3, 4
XT = XBC // P
ROW_SC, ROW_XBC, ROW_XBC_B = 0, SC_TAPS * KD, SC_TAPS * KD + XBC_TAPS * XT
ROWS = ROW_XBC_B + XT

C_ID, C_ALPHA, C_ANTI, C_TRI, C_AFTER, C_SWAP, C_COS, C_SIN = 0, 128, 256, 384, 512, 640, 768, 1024
C_ALL = 1280


def shape_constants():
    c = np.zeros((P, C_ALL), np.float32)
    i = np.arange(P)
    c[:, C_ID:C_ID + P] = np.eye(P)
    c[:, C_ALPHA:C_ALPHA + P] = ALPHA * np.eye(P)
    c[:, C_ANTI:C_ANTI + P] = np.eye(P)[::-1]
    c[:, C_TRI:C_TRI + P] = i[:, None] <= i[None, :]
    c[:, C_AFTER:C_AFTER + P] = i[:, None] > i[None, :]
    h = ROPE // 2
    for d in range(P):
        src, sign = (d + h, -1.0) if d % ROPE < h else (d - h, 1.0)
        c[src, C_SWAP + d] = sign
    inv = np.float32(10000.0) ** (-np.arange(0, ROPE, 2, dtype=np.float32) / np.float32(ROPE))
    ang = np.arange(TOKENS, dtype=np.float32)[None, :] * inv[i % h][:, None]
    c[:, C_COS:C_COS + TOKENS] = np.cos(ang)
    c[:, C_SIN:C_SIN + TOKENS] = np.sin(ang)
    return c


def two_blocks(nc, t, consts, out):
    FF_CHUNKS = D_FF // CHUNK_F
    SG_CHUNKS = D_FF_2 // CHUNK_F
    SC_CHUNKS = D // CHUNK_F
    N_SC = 4 * SC_CHUNKS
    N_FF = 2 * FF_CHUNKS
    N_MLA = 4 + 4 + 2 + 4
    N_SG = 4 * SG_CHUNKS
    GLU_PASSES = (SG_CHUNKS - 1) // 2 - 1
    N_HY = 2 + 1 + 6 + 4 + 4 + 6
    S_SC = 0
    S_FF = [S_SC + N_SC, S_SC + N_SC + N_FF + N_MLA]
    S_MLA = S_FF[0] + N_FF
    S_SG = [S_FF[1] + N_FF, S_FF[1] + N_FF + N_SG + N_HY]
    S_HY = S_SG[0] + N_SG
    N_SLABS = S_SG[1] + N_SG

    width = [SLAB] * N_SLABS
    loads = [1] * N_SLABS
    for s in S_SG:
        for i in range(SG_CHUNKS):
            d0 = s + 4 * i + 4 if i < SG_CHUNKS - 1 else s + 4 * i + 2
            width[d0] = width[d0 + 1] = D
    DQ, KV, UQ, UK, UV, WO = S_MLA, S_MLA + 2, S_MLA + 4, S_MLA + 8, S_MLA + 9, S_MLA + 10
    UQ_COLS = 2 * (NOPE + ROPE)
    KV_COLS = KV_LORA + 2 * ROPE
    for m in (DQ, DQ + 1):
        width[m] = 4 * Q_LORA
    for m in (KV, KV + 1):
        width[m], loads[m] = 4 * KV_COLS, 2
    for m in range(UQ, UQ + 4):
        width[m], loads[m] = KQ * UQ_COLS, 4
    HV, HDT, HX, HQK, HZ, HWO = S_HY, S_HY + 2, S_HY + 3, S_HY + 9, S_HY + 13, S_HY + 17
    width[HDT] = KD * SSD_HEADS
    landed_at, used_dmas = [], [0] * RING
    for m in range(N_SLABS):
        used_dmas[m % RING] += loads[m]
        landed_at.append(16 * used_dmas[m % RING])

    with ExitStack() as ctx:
        def sb(name, shape, dt=F32):
            return ctx.enter_context(nc.sbuf_tensor(name, shape, dt))

        def sem(name):
            return ctx.enter_context(nc.semaphore(name))

        raw = sb("raw", [P, RING, SLAB])
        weight_hi = sb("weight_hi", [P, RING, SLAB], F32R)
        weight_lo = sb("weight_lo", [P, RING, SLAB], F32R)
        x_tok = sb("x_tok", [P, TILES, D])
        normed = sb("normed", [P, TILES, D])
        xh = sb("xh", [P, KD, TOKENS], F32R)
        xl = sb("xl", [P, KD, TOKENS], F32R)
        hh = sb("hh", [P, 2 * CT, TOKENS], F32R)
        hl = sb("hl", [P, 2 * CT, TOKENS], F32R)
        tmp_a = sb("tmp_a", [P, HALF])
        tmp_b = sb("tmp_b", [P, HALF])
        tmp_c = sb("tmp_c", [P, HALF])
        tmp_d = sb("tmp_d", [P, HALF])
        gain = sb("gain", [P, D])
        bias = sb("bias", [P, D])
        gain2 = sb("gain2", [P, D])
        cst = sb("cst", [P, C_ALL])
        rows = sb("rows", [ROWS, P])
        cols = sb("cols", [P, ROWS])
        zeros = sb("zeros", [P, HALF], BF16)
        mask_row = sb("mask_row", [1, P], BF16)
        mask_ones = sb("mask_ones", [1, ATTN_CHUNK], BF16)
        prob_t = sb("prob_t", [P, 2, 384])
        stat = sb("stat", [P, TILES, 2, 6])
        mean_var = sb("mean_var", [P, TILES, 2])
        rstd = sb("rstd", [P, 4])
        sumsq = sb("sumsq", [P, 4])
        half_neg = sb("half_neg", [P, 1])
        mean_sq = sb("mean_sq", [P, TILES, 2])
        arena = sb("arena", [P, 10368])

        acc = ctx.enter_context(nc.psum_tensor("acc", [P, 4, HALF], F32))
        up = [ctx.enter_context(nc.psum_tensor(f"up{i}", [P, HALF], F32)) for i in range(4)]

        ident = cst[:, C_ID:C_ID + P]
        alpha_ident = cst[:, C_ALPHA:C_ALPHA + P]
        anti = cst[:, C_ANTI:C_ANTI + P]
        tri = cst[:, C_TRI:C_TRI + P]
        after = cst[:, C_AFTER:C_AFTER + P]
        swap = cst[:, C_SWAP:C_SWAP + P]
        cos = cst[:, C_COS:C_COS + TOKENS]
        sin = cst[:, C_SIN:C_SIN + TOKENS]

        at = [0]

        def take(n, *dims):
            a = arena[:, at[0]:at[0] + n]
            at[0] += n
            if len(dims) == 2:
                a = a.rearrange("p (a b) -> p a b", a=dims[0])
            return a

        q_nope = take(HEADS * TOKENS, HEADS, TOKENS)
        k_nope = take(HEADS * TOKENS, HEADS, TOKENS)
        q_rot = take(4 * TOKENS, 4, TOKENS)
        k_rot = take(TOKENS)
        pe_raw = take(2 * TOKENS, 2, TOKENS)
        g_q = take(Q_LORA)
        g_kv = take(KV_LORA)
        prob_a = take(2 * 384, 2, 384)
        v_a = normed
        latent_q = normed[:, 0, 0:2 * Q_LORA].rearrange("p (t n) -> p t n", t=TILES)
        latent_kv = normed[:, 1, 0:2 * KV_LORA].rearrange("p (t n) -> p t n", t=TILES)
        at[0] = 0
        bc_t = take(4 * TOKENS, 4, TOKENS)
        xs_t = take(8 * TOKENS, 8, TOKENS)
        hankel = xs_t
        q_b = take(4 * TOKENS, 4, TOKENS)
        k_b = take(4 * TOKENS, 4, TOKENS)
        v_b = take(TILES * HALF, TILES, HALF)
        xdt = take(TILES * D, TILES, D)
        xdt_end = take(D)
        cb_diag = take(4 * P, 4, P)
        cb_off = take(2 * P, 2, P)
        prob_b = arena[:, 0:2 * 384].rearrange("p (a b) -> p a b", a=2)
        dt_work = take(10 * 32, 10, 32)
        a_row = take(SSD_HEADS)
        dtb_row = take(SSD_HEADS)
        dskip_row = take(SSD_HEADS)
        y_tok = normed
        z_gate = (bias, xdt_end)

        def adt_tile(tile):
            return dt_work[:, 8, tile * SSD_HEADS:(tile + 1) * SSD_HEADS]

        def cum_head(tile, h):
            return dt_work[:, 4, tile * SSD_HEADS + h:tile * SSD_HEADS + h + 1]

        head_max = sb("head_max", [P, 2, HEADS, 2])
        head_sum = sb("head_sum", [P, 2, HEADS, 2])

        ident_landed, const_landed, out_landed = sem("ident_landed"), sem("const_landed"), sem("out_landed")
        first_landed, first_hi, first_lo = sem("first_landed"), sem("first_hi"), sem("first_lo")
        x_landed = [sem(f"x_landed{i}") for i in range(TILES)]
        landed = [sem(f"landed{i}") for i in range(RING)]
        hi_done, lo_done, slab_used = sem("hi_done"), sem("lo_done"), sem("slab_used")
        act_step, dve_step, pool_step = sem("act_step"), sem("dve_step"), sem("pool_step")
        cols_turned, cols_ready, zeros_ready, pool_ready = (
            sem("cols_turned"), sem("cols_ready"), sem("zeros_ready"), sem("pool_ready"))

        class Sems:

            def __init__(self, part, names):
                self.s = {n: sem(f"{part}_{n}") for n in names.split()}

            def __getitem__(self, n):
                return self.s[n]

        NORMS = 8
        norm = [Sems(f"norm{b}", "rows rstd tok" + " stat" * (b <= 4) + " resid squares" * (b >= 4)) if b else None for b in range(NORMS)]
        turned, operand_high, operand_low, acc_part = (
            sem("turned"), sem("operand_high"), sem("operand_low"), sem("acc_part"))
        sc = Sems("sc", "c_copied ch_made conv0 y_made y_hi chunk")
        mlp = [Sems(f"mlp{i}", "relu squared hidden_hi chunk") for i in range(2)]
        glu = [Sems(f"glu{i}", "gate hidden hidden_hi chunk") for i in range(2)]
        mla = Sems("mla", "rows latent_ps sumsq rstd latent turned t_hi t_lo pe q_out swapped rotated k_ps k_out v0 v1")
        att = [Sems(f"att{i}", "scores negmax probs normed turned t_out o_ps o_hi o_lo") for i in range(2)]
        hy = Sems("hy", "rows tap0 conv xbc dt_abs dt_exp adt qk_out v_out cum_ps cum_out decays xs_ps xs_out y_skip xdt "
                        "hank cb_ps cb_act cb seg_ps seg exp seg_w y_ps off_ps off_taken y_sum z_gate y_gated sumsq "
                        "rstd y_n y_ps_t y_hi y_lo")

        def up_view(w):
            return w.rearrange("(k p) n -> p k n", p=P)

        def up_chunks(w):
            return w.rearrange("(k p) (c f) -> p k c f", p=P, f=CHUNK_F)

        def down_chunks(w):
            return w.rearrange("(c j p) n -> p c j n", p=P, j=CT)

        def spread(v, n):
            return v.rearrange("(a n) -> a n", a=1).to_broadcast([P, n])

        def raw3(m, a, b):
            return raw[:, m % RING, 0:a * b].rearrange("p (a b) -> p a b", a=a)

        def heads(a, n=8):
            return a.rearrange("p (h d) -> p h d", h=n)

        def per_head(a, n=8):
            return a.unsqueeze(2).to_broadcast([P, n, SSD_HD])

        def mla_out(g):
            return (slice(0, P), g), up[3][:, 0:TOKENS]

        def hybrid_out(g):
            o = ATT_HD * (g % 2)
            return (slice(o, o + ATT_HD), g // 2), acc[o:o + ATT_HD, 3, 0:TOKENS]

        block = ctx.enter_context(nc.Block())

        @block.sync
        def _(sp):
            def load(m, dst, src):
                sp.dma_start(dst, src).then_inc(landed[m % RING], 16)

            def place_free(m):
                if m >= RING:
                    sp.wait_ge(lo_done, m - RING + 1)

            sp.dma_start(cst[:, 0:C_ANTI], consts[:, 0:C_ANTI]).then_inc(ident_landed, 16)
            for tile in range(TILES):
                sp.dma_start(x_tok[:, tile, :], t["x"][0, tile * P:(tile + 1) * P, :]).then_inc(x_landed[tile], 16)

            w_in = up_view(t["sc_w_in"][0])
            w_out = down_chunks(t["sc_w_out"][0])
            m = S_SC
            for c in range(SC_CHUNKS + 1):
                for part in range(3 if c < SC_CHUNKS else 0):
                    place_free(m)
                    f0 = part * D + c * CHUNK_F
                    k0 = 0
                    if m == 0:
                        k0 = KD // 2
                        sp.dma_start(raw3(m, KD, CHUNK_F)[:, 0:k0, :], w_in[:, 0:k0, f0:f0 + CHUNK_F])\
                            .then_inc(first_landed, 16)
                    load(m, raw3(m, KD, CHUNK_F)[:, k0:, :], w_in[:, k0:, f0:f0 + CHUNK_F])
                    m += 1
                if c:
                    place_free(m)
                    load(m, raw3(m, CT, D), w_out[:, c - 1, :, :])
                    m += 1

            def mlp_weights(i):
                w1, w2 = up_chunks(t["ff_w1"][i]), down_chunks(t["ff_w2"][i])
                s = S_FF[i]

                def up_slab(m, c):
                    load(m, raw3(m, KD, CHUNK_F), w1[:, :, c, :])

                def down_slab(m, c):
                    load(m, raw3(m, CT, D), w2[:, c, :, :])

                place_free(s)
                up_slab(s, 0)
                with sp.Fori(0, FF_CHUNKS // 2 - 1) as it:
                    for j in range(4):
                        sp.wait_ge(lo_done, 4 * it + (s + 1 + j - RING + 1))
                        chunk = 2 * it + (1, 0, 2, 1)[j]
                        slot = (s + 1 + j) % RING
                        if j % 2 == 0:
                            sp.dma_start(raw3(slot, KD, CHUNK_F), w1[:, :, bass.ds(chunk, 1), :])\
                              .then_inc(landed[slot], 16)
                        else:
                            sp.dma_start(raw3(slot, CT, D), w2[:, bass.ds(chunk, 1), :, :])\
                              .then_inc(landed[slot], 16)
                e = s + N_FF - 3
                place_free(e)
                up_slab(e, FF_CHUNKS - 1)
                place_free(e + 1)
                down_slab(e + 1, FF_CHUNKS - 2)
                place_free(e + 2)
                down_slab(e + 2, FF_CHUNKS - 1)

            def glu_weights(i):
                name = ("ffn1", "ffn2")[i]
                wg, wu = up_chunks(t[f"{name}_w_gate_2"][0]), up_chunks(t[f"{name}_w_up_2"][0])
                wd = down_chunks(t[f"{name}_w_down_2"][0])
                s = S_SG[i]
                for j, w in enumerate((wg, wu)):
                    place_free(s + j)
                    load(s + j, raw3(s + j, KD, CHUNK_F), w[:, :, 0, :])
                with sp.Fori(0, (SG_CHUNKS - 1) // 2) as it:
                    for j in range(8):
                        sp.wait_ge(lo_done, 8 * it + (s + 2 + j - RING + 1))
                        slot = (s + 2 + j) % RING
                        c = 2 * it + j // 4
                        if j % 4 < 2:
                            sp.dma_start(raw3(slot, KD, CHUNK_F), (wg, wu)[j % 4][:, :, bass.ds(c + 1, 1), :])\
                              .then_inc(landed[slot], 16)
                        else:
                            sp.dma_start(raw3(slot, 1, D), wd[:, bass.ds(c, 1), j % 4 - 2, :])\
                              .then_inc(landed[slot], 16)
                for j in range(2):
                    e = s + N_SG - 2 + j
                    place_free(e)
                    load(e, raw3(e, 1, D), wd[:, SG_CHUNKS - 1, j:j + 1, :])

            mlp_weights(0)

            w = up_view(t["mla_w_dq"][0])
            for j in range(2):
                place_free(DQ + j)
                load(DQ + j, raw3(DQ + j, 4, Q_LORA), w[:, 4 * j:4 * j + 4, :])
            w = up_view(t["mla_w_dkv"][0])
            for j in range(2):
                place_free(KV + j)
                dst = raw3(KV + j, 4, KV_COLS)
                load(KV + j, dst[:, :, 0:KV_LORA + ROPE], w[:, 4 * j:4 * j + 4, :])
                load(KV + j, dst[:, :, KV_LORA + ROPE:], w[:, 4 * j:4 * j + 4, KV_LORA:])
            w = up_view(t["mla_w_uq"][0]).rearrange("p k (h c) -> p k h c", h=HEADS)
            for j in range(4):
                place_free(UQ + j)
                dst = raw3(UQ + j, KQ, UQ_COLS)
                for h in range(2):
                    load(UQ + j, dst[:, :, h * NOPE:(h + 1) * NOPE], w[:, :, 2 * j + h, 0:NOPE])
                    r0 = 2 * NOPE + h * ROPE
                    load(UQ + j, dst[:, :, r0:r0 + ROPE], w[:, :, 2 * j + h, NOPE:])
            for m, name in ((UK, "mla_w_uk"), (UV, "mla_w_uv")):
                place_free(m)
                load(m, raw3(m, KKV, D), t[name][0].rearrange("(k p) h d -> p k (h d)", p=P))
            w = down_chunks(t["mla_w_o"][0])
            for j in range(4):
                place_free(WO + j)
                load(WO + j, raw3(WO + j, CT, D), w[:, j, :, :])

            mlp_weights(1)
            glu_weights(0)

            w = up_view(t["w_in_2"][0])
            for j in range(2):
                place_free(HV + j)
                load(HV + j, raw3(HV + j, 4, HALF), w[:, 4 * j:4 * j + 4, V0:V0 + HALF])
            place_free(HDT)
            load(HDT, raw3(HDT, KD, SSD_HEADS), w[:, :, DT0:DT0 + SSD_HEADS])
            for s, f0, n in ((HX, XBC0, 6), (HQK, Q0, 4), (HZ, Z0, 4)):
                for j in range(n):
                    place_free(s + j)
                    load(s + j, raw3(s + j, KD, CHUNK_F), w[:, :, f0 + j * CHUNK_F:f0 + (j + 1) * CHUNK_F])
            w = down_chunks(t["w_out_2"][0])
            for j in range(6):
                place_free(HWO + j)
                load(HWO + j, raw3(HWO + j, CT, D), w[:, (4, 5, 0, 1, 2, 3)[j], :, :])

            glu_weights(1)

            for n in range(2 * TILES):
                tile, c = n // 2, slice(n % 2 * HALF, (n % 2 + 1) * HALF)
                sp.wait_ge(norm[7]["tok"], n + 1)
                sp.dma_start(out[0, tile * P:(tile + 1) * P, c], normed[:, tile, c]).then_inc(out_landed, 16)
            sp.wait_ge(out_landed, 32 * TILES)

        @block.gpsimd
        def _(pool):
            steps = [0]

            def then(ins):
                steps[0] += 1
                ins.then_inc(pool_step, 1)
                pool.wait_ge(pool_step, steps[0])

            nc.gpsimd.memset(zeros[:, :], 0.0).then_inc(zeros_ready, 1)
            nc.gpsimd.memset(mask_row[:, 0:ATTN_CHUNK], MASKED).then_inc(zeros_ready, 1)
            nc.gpsimd.memset(mask_row[:, ATTN_CHUNK:P], 0.0).then_inc(zeros_ready, 1)
            nc.gpsimd.memset(mask_ones[:, :], 1.0).then_inc(zeros_ready, 1)
            then(nc.gpsimd.memset(half_neg[:, :], -0.5))
            pool.wait_ge(landed[0], 16)
            pool.dma_start(cst[:, C_ANTI:], consts[:, C_ANTI:]).then_inc(const_landed, 16)
            pool.dma_start(rows[ROW_SC:ROW_XBC, :], t["sc_conv_w"][0].rearrange("k (f p) -> (k f) p", p=P))\
                .then_inc(const_landed, 16)
            pool.dma_start(rows[ROW_XBC:ROW_XBC_B, :], t["conv_w_2"][0].rearrange("k (f p) -> (k f) p", p=P))\
                .then_inc(const_landed, 16)
            pool.dma_start(rows[ROW_XBC_B:ROWS, :], t["conv_b_2"][0].rearrange("(f p) -> f p", p=P))\
                .then_inc(const_landed, 16)

            def norm_rows(b, *pairs):
                for dst, v, n in pairs:
                    pool.dma_start(dst, spread(v, n)).then_inc(norm[b]["rows"], 16)

            def root(dst, src, eps):
                n = dst.shape[-1]
                then(nc.gpsimd.tensor_scalar(dst, src, eps, None, ALU.add))
                return nc.gpsimd.tensor_tensor(dst, dst, half_neg[:, :].to_broadcast([P, n]), ALU.pow)

            def layer_norm_root(b):
                for tile in range(TILES):
                    pool.wait_ge(norm[b]["stat"], tile + 1)
                    root(rstd[:, tile:tile + 1], mean_var[:, tile, 1:2], LN_EPS).then_inc(norm[b]["rstd"], 1)

            norm_rows(1, (gain[:, :], t["ln_mix_g"][0], D), (bias[:, :], t["ln_mix_b"][0], D))
            layer_norm_root(1)
            pool.wait_ge(norm[1]["tok"], 2 * TILES)
            norm_rows(2, (gain[:, :], t["ln_ff_g"][0], D), (bias[:, :], t["ln_ff_b"][0], D))
            layer_norm_root(2)

            pool.dma_start(g_q, spread(t["mla_g_q"][0], Q_LORA)).then_inc(mla["rows"], 16)
            pool.dma_start(g_kv, spread(t["mla_g_kv"][0], KV_LORA)).then_inc(mla["rows"], 16)
            pool.wait_ge(norm[2]["tok"], 2 * TILES)
            norm_rows(3, (gain[:, :], t["ln_mix_g"][1], D), (bias[:, :], t["ln_mix_b"][1], D))
            for n, (c, k) in enumerate(((slice(0, 2), 2), (slice(2, 3), 3), (slice(3, 4), 4))):
                pool.wait_ge(mla["sumsq"], k)
                root(rstd[:, c], sumsq[:, c], MLA_EPS).then_inc(mla["rstd"], 1)
            layer_norm_root(3)

            pool.wait_ge(norm[3]["tok"], 2 * TILES)
            norm_rows(4, (gain[:, :], t["ln_ff_g"][1], D), (bias[:, :], t["ln_ff_b"][1], D),
                      (gain2[:, :], t["ffn1_norm_2"][0], D))
            layer_norm_root(4)

            def rms_root(b):
                for tile in range(TILES):
                    pool.wait_ge(norm[b]["squares"], 2 * tile + 2)
                    r = rstd[:, 2 + tile:3 + tile]
                    then(nc.gpsimd.tensor_tensor(r, mean_sq[:, tile, 0:1], mean_sq[:, tile, 1:2], ALU.add))
                    root(r, r, RMS_EPS).then_inc(norm[b]["rstd"], 1)

            rms_root(4)
            pool.wait_ge(norm[4]["tok"], 2 * TILES)
            norm_rows(5, (gain[:, :], t["mix_norm_2"][0], D))
            pool.dma_start(gain2[:, :], spread(t["ssd_norm_2"][0], D)).then_inc(hy["rows"], 16)
            rms_root(5)

            pool.dma_start(a_row, spread(t["a_log_2"][0], SSD_HEADS)).then_inc(hy["rows"], 16)
            pool.dma_start(dtb_row, spread(t["dt_bias_2"][0], SSD_HEADS)).then_inc(hy["rows"], 16)
            pool.dma_start(dskip_row, spread(t["d_skip_2"][0], SSD_HEADS)).then_inc(hy["rows"], 16)
            pool.wait_ge(norm[5]["tok"], 2 * TILES)
            norm_rows(6, (gain[:, :], t["ffn2_norm_2"][0], D))
            pool.wait_ge(hy["rows"], 64)
            for g in range(4):
                tile, h = g // 2, g % 2
                y = heads(y_tok[:, tile, h * HALF:(h + 1) * HALF])
                pool.wait_ge(hy["xs_out"], g + 1)
                nc.gpsimd.tensor_tensor(y, y, per_head(dskip_row[:, 8 * h:8 * h + 8]), ALU.mult).then_inc(hy["y_skip"], 1)
            rel = t["rel_bias_2"][0]
            for h in range(HEADS):
                window = bass.AP(rel.tensor, rel.offset + h * REL + P + 1, [[1, P], [1, TOKENS]])
                pool.dma_start(hankel[:, h, :], window).then_inc(hy["hank"], 16)
            for tile in range(TILES):
                pool.wait_ge(hy["sumsq"], tile + 1)
                root(rstd[:, tile:tile + 1], sumsq[:, 2 + tile:3 + tile], RMS_EPS).then_inc(hy["rstd"], 1)
            rms_root(6)
            pool.wait_ge(norm[6]["tok"], 2 * TILES)
            norm_rows(7, (gain[:, :], t["final_norm_2"], D))
            rms_root(7)

        @block.scalar
        def _(act):
            steps = [0]

            def then(ins):
                steps[0] += 1
                ins.then_inc(act_step, 1)
                act.wait_ge(act_step, steps[0])

            def copy(dst, src, **kw):
                return nc.scalar.activation(dst, src, ACT.Copy, **kw)

            def round_slab(m):
                if m >= N_SLABS:
                    return
                act.wait_ge(landed[m % RING], landed_at[m])
                if m >= RING:
                    act.wait_ge(slab_used, m - RING + 1)
                copy(weight_hi[:, m % RING, 0:width[m]], raw[:, m % RING, 0:width[m]]).then_inc(hi_done, 1)

            def round_slab_at(m, off):
                act.wait_ge(landed[m % RING], off * (16 // RING) + landed_at[m])
                act.wait_ge(slab_used, off + (m - RING + 1))
                copy(weight_hi[:, m % RING, 0:width[m]], raw[:, m % RING, 0:width[m]]).then_inc(hi_done, 1)

            def operand_hi(b, last=None, between=False):
                def followers():
                    round_slab(last - 1 + RING)
                    round_slab(last + RING)

                for g in range(4):
                    tile, h = g // 2, g % 2
                    act.wait_ge(turned, 4 * b + g + 1)
                    copy(xh[:, 4 * h:4 * h + 4, tile * P:(tile + 1) * P],
                         up[g][:, :].rearrange("p (k n) -> p k n", k=4)).then_inc(operand_high, 1)
                    if between and g == 1:
                        followers()
                if last is not None and not between:
                    followers()

            def mean_squares(b):
                for n in range(2 * TILES):
                    tile, h = n // 2, n % 2
                    c = slice(h * HALF, (h + 1) * HALF)
                    act.wait_ge(norm[b]["resid"], n + 1)
                    nc.scalar.activation(normed[:, tile, c], x_tok[:, tile, c], ACT.Square, scale=float(D) ** -0.5,
                                         accum_out=mean_sq[:, tile, h:h + 1]).then_inc(norm[b]["squares"], 1)

            operand_hi(0)
            act.wait_ge(first_landed, 16)
            copy(weight_hi[:, 0, 0:SLAB // 2], raw[:, 0, 0:SLAB // 2]).then_inc(first_hi, 1)
            act.wait_ge(landed[0], landed_at[0])
            copy(weight_hi[:, 0, SLAB // 2:], raw[:, 0, SLAB // 2:]).then_inc(hi_done, 1)
            for m in range(1, RING):
                round_slab(m)
            m = S_SC
            for c in range(SC_CHUNKS + 1):
                if c < SC_CHUNKS:
                    round_slab(m + RING)
                    act.wait_ge(slab_used, m + 2)
                    if c:
                        act.wait_ge(sc["ch_made"], c)
                    copy(tmp_a[:, :], up[1][:, :]).then_inc(sc["c_copied"], 1)
                    round_slab(m + 1 + RING)
                    if c == 0:
                        act.wait_ge(cols_turned, 1)
                        copy(cols[:, :], up[3][:, 0:ROWS]).then_inc(cols_ready, 1)
                        act.wait_ge(cols_ready, 1)
                    act.wait_ge(sc["ch_made"], c + 1)
                    if c:
                        act.wait_ge(sc["y_made"], c)
                    for f in range(CT):
                        tap = cols[:, ROW_SC + (SC_TAPS - 1) * KD + CT * c + f:][:, 0:1]
                        nc.scalar.activation(tmp_c[:, f * TOKENS:(f + 1) * TOKENS],
                                             tmp_b[:, f * TOKENS:(f + 1) * TOKENS], ACT.Copy, scale=tap)\
                            .then_inc(sc["conv0"], 1)
                    act.wait_ge(sc["y_made"], c + 1)
                    copy(hh[:, CT * (c % 2):CT * (c % 2) + CT, :],
                         tmp_d[:, :].rearrange("p (f n) -> p f n", f=CT)).then_inc(sc["y_hi"], 1)
                    round_slab(m + 2 + RING)
                    m += 3
                if 0 < c < SC_CHUNKS:
                    if c < SC_CHUNKS - 1:
                        round_slab(m + RING)
                    m += 1

            def mlp_part(i):
                s, q = S_FF[i], mlp[i]

                def relu(c, par):
                    nc.scalar.activation(tmp_a[:, :], up[par][:, :], ACT.Relu).then_inc(q["relu"], 1)

                def hidden_hi(par):
                    copy(hh[:, CT * par:CT * par + CT, :], tmp_b[:, :].rearrange("p (f n) -> p f n", f=CT))\
                        .then_inc(q["hidden_hi"], 1)

                act.wait_ge(slab_used, s + 1)
                relu(0, 0)
                round_slab(s + RING)
                act.wait_ge(q["squared"], 1)
                hidden_hi(0)
                with act.Fori(0, FF_CHUNKS // 2 - 1) as it:
                    for j in range(4):
                        n = s + 1 + j
                        if j % 2 == 0:
                            par = (1, 0)[j // 2]
                            act.wait_ge(slab_used, 4 * it + (n + 1))
                            act.wait_ge(q["chunk"], 2 * it + (1 + j // 2))
                            relu(0, par)
                        round_slab_at(n + RING, 4 * it)
                        if j % 2 == 0:
                            act.wait_ge(q["squared"], 2 * it + (2 + j // 2))
                            hidden_hi(par)
                n = s + N_FF - 3
                act.wait_ge(slab_used, n + 1)
                act.wait_ge(q["chunk"], FF_CHUNKS - 1)
                relu(0, 1)
                act.wait_ge(q["squared"], FF_CHUNKS)
                hidden_hi(1)
                round_slab(n + RING)

            def glu_part(i):
                s, q = S_SG[i], glu[i]

                def gate(par):
                    nc.scalar.activation(tmp_a[:, :], up[2 * par][:, :], ACT.Silu).then_inc(q["gate"], 1)

                def hidden_hi(par):
                    copy(hh[:, CT * par:CT * par + CT, :], tmp_b[:, :].rearrange("p (f n) -> p f n", f=CT))\
                        .then_inc(q["hidden_hi"], 1)

                act.wait_ge(slab_used, s + 1)
                gate(0)
                round_slab(s + RING)
                round_slab(s + 1 + RING)
                act.wait_ge(q["hidden"], 1)
                hidden_hi(0)
                def two_chunks(off, chunk, rounded):
                    for j in range(8):
                        n = s + 2 + j
                        par = (1, 0)[j // 4]
                        if j % 4 == 0:
                            act.wait_ge(slab_used, off + (n + 1))
                            act.wait_ge(q["chunk"], chunk + (1 + j // 4))
                            gate(par)
                        rounded(n + RING)
                        if j % 4 == 1:
                            act.wait_ge(q["hidden"], chunk + (2 + j // 4))
                            hidden_hi(par)

                with act.Fori(0, GLU_PASSES) as it:
                    two_chunks(8 * it, 2 * it, lambda m: round_slab_at(m, 8 * it))
                two_chunks(8 * GLU_PASSES, 2 * GLU_PASSES, lambda m: round_slab(m + 8 * GLU_PASSES))

            operand_hi(1, S_FF[0] - 1)
            mlp_part(0)
            operand_hi(2, S_MLA - 1, between=True)

            act.wait_ge(slab_used, DQ + 2)
            for tile in range(TILES):
                nc.scalar.activation((tmp_a, tmp_b)[tile][:, 0:Q_LORA],
                                     acc[:, 2 * tile, 0:Q_LORA], ACT.Square, scale=float(Q_LORA) ** -0.5,
                                     accum_out=sumsq[:, tile:tile + 1]).then_inc(mla["sumsq"], 1)
            round_slab(DQ + RING)
            round_slab(DQ + 1 + RING)
            for tile in range(TILES):
                act.wait_ge(mla["latent_ps"], 1 + tile)
                nc.scalar.activation((tmp_c, tmp_d)[tile][:, 0:KV_LORA], acc[:, 2 * tile + 1, 0:KV_LORA], ACT.Square,
                                     scale=float(KV_LORA) ** -0.5, accum_out=sumsq[:, 2 + tile:3 + tile])\
                    .then_inc(mla["sumsq"], 1)

            def latent_hi(g, k, n):
                act.wait_ge(mla["turned"], g + 1)
                copy(xh[:, k:k + n, :], up[1 + g][:, 0:n * TOKENS].rearrange("p (k n) -> p k n", k=n))\
                    .then_inc(mla["t_hi"], 1)

            latent_hi(0, 0, 2)
            latent_hi(1, 2, 1)
            act.wait_ge(slab_used, KV + 2)
            copy(pe_raw[:, 0, :], up[0][:, 0:TOKENS]).then_inc(mla["pe"], 1)
            latent_hi(2, 3, 2)
            round_slab(KV + RING)
            round_slab(KV + 1 + RING)
            for j in range(4):
                act.wait_ge(slab_used, UQ + j + 1)
                if j:
                    act.wait_ge(mla["rotated"], j)
                copy(pe_raw[:, (j + 1) % 2, :], up[2 + j % 2][:, 0:TOKENS]).then_inc(mla["pe"], 1)
                copy(q_nope[:, 2 * j:2 * j + 2, :], up[j % 2][:, :].rearrange("p (h n) -> p h n", h=2))\
                    .then_inc(mla["q_out"], 1)
                if j < 2:
                    round_slab(UQ + j + RING)
            for j in range(4):
                if j < 3:
                    act.wait_ge(mla["k_ps"], j + 1)
                else:
                    act.wait_ge(slab_used, UK + 1)
                copy(k_nope[:, 2 * j:2 * j + 2, :], up[j][:, :].rearrange("p (h n) -> p h n", h=2))\
                    .then_inc(mla["k_out"], 1)
            round_slab(UQ + 2 + RING)
            round_slab(UQ + 3 + RING)
            act.wait_ge(slab_used, UV + 1)
            copy(v_a[:, 0, :].rearrange("p (h n) -> p h n", h=2), acc[:, 0:2, :]).then_inc(mla["v0"], 1)

            def attention(i, scale, prob, s_bank, t_bank, o_hi, o_tiles, lag):
                q = att[i]

                def step(h):
                    if h < HEADS:
                        act.wait_ge(q["negmax"], h + 1)
                        if h >= 2:
                            act.wait_ge(q["turned"], h - 1)
                        S = s_bank[h % 2]
                        nc.scalar.activation(prob[:, h % 2, 0:P], S[:, 0:P], ACT.Exp, scale=scale,
                                             bias=head_max[:, 1, h, 0:1], accum_out=head_sum[:, 0, h, 0:1])\
                            .then_inc(q["probs"], 1)
                        nc.scalar.activation(prob[:, h % 2, P:384], S[:, P:384], ACT.Exp, scale=scale,
                                             bias=head_max[:, 1, h, 1:2], accum_out=head_sum[:, 0, h, 1:2])\
                            .then_inc(q["probs"], 1)
                    if 1 <= h <= HEADS:
                        g = h - 1
                        act.wait_ge(q["turned"], g + 1)
                        if g >= 2:
                            act.wait_ge(q["o_ps"], g - 1)
                        copy(prob_t[:, g % 2, :], t_bank[:, 0:384]).then_inc(q["t_out"], 1)
                    if h >= lag:
                        g = h - lag
                        act.wait_ge(q["o_ps"], g + 1)
                        dst, src = o_tiles(g)
                        copy(o_hi(dst), src).then_inc(q["o_hi"], 1)
                return step

            heads_a = attention(0, QK_SCALE, prob_a, up[0:2], up[2], lambda d: xh[d[0], d[1], :], mla_out, 3)
            for h in range(HEADS + 3):
                heads_a(h)
                if h in (6, 7):
                    round_slab((UK, UV)[h - 6] + RING)
            round_slab(WO + RING)
            round_slab(WO + 1 + RING)
            operand_hi(3, WO + 3)

            mlp_part(1)
            mean_squares(4)
            operand_hi(4, S_SG[0] - 1)
            glu_part(0)
            mean_squares(5)
            operand_hi(5, S_HY - 1)

            for tile in range(TILES):
                act.wait_ge(slab_used, HV + 2)
                copy(v_b[:, tile, :], acc[:, tile, :]).then_inc(hy["v_out"], 1)
            round_slab(HV + RING)
            round_slab(HV + 1 + RING)
            act.wait_ge(hy["dt_abs"], 1)
            nc.scalar.activation(dt_work[:, 2, :], dt_work[:, 1, :], ACT.Exp).then_inc(hy["dt_exp"], 1)
            act.wait_ge(hy["rows"], 64)
            nc.scalar.activation(dt_work[:, 9, 0:SSD_HEADS], a_row, ACT.Exp).then_inc(hy["dt_exp"], 1)
            round_slab(HDT + RING)

            def conv_out(j):
                act.wait_ge(hy["conv"], j + 1)
                dst = xs_t[:, CT * j:CT * j + CT, :] if j < 4 else bc_t[:, CT * (j - 4):CT * (j - 4) + CT, :]
                nc.scalar.activation(dst, (tmp_a, tmp_b)[j % 2][:, :].rearrange("p (f n) -> p f n", f=CT), ACT.Silu)\
                    .then_inc(hy["xbc"], 1)

            for j in range(6):
                act.wait_ge(slab_used, HX + j + 1)
                cy = (tmp_a, tmp_b)[j % 2]
                if j >= 2:
                    act.wait_ge(hy["xbc"], j - 1)
                for f in range(CT):
                    ft = CT * j + f
                    nc.scalar.activation(
                        cy[:, f * TOKENS:(f + 1) * TOKENS], up[j % 4][:, f * TOKENS:(f + 1) * TOKENS], ACT.Identity,
                        scale=cols[:, ROW_XBC + (XBC_TAPS - 1) * XT + ft:][:, 0:1],
                        bias=cols[:, ROW_XBC_B + ft:][:, 0:1]).then_inc(hy["tap0"], 1)
                round_slab(HX + j + RING)
                if j:
                    conv_out(j - 1)
            conv_out(5)

            def keys_queries(j):
                act.wait_ge(slab_used, HQK + j + 1)
                dst = (q_b, k_b)[j // 2][:, CT * (j % 2):CT * (j % 2) + CT, :]
                copy(dst, up[2 + j % 2][:, :].rearrange("p (f n) -> p f n", f=CT),
                     scale=(float(ATT_HD) ** -0.5 if j < 2 else 1.0)).then_inc(hy["qk_out"], 1)
                round_slab(HQK + j + RING)

            act.wait_ge(hy["cum_ps"], 1)
            act.wait_ge(hy["cum_out"], TILES)
            nc.scalar.activation(dt_work[:, 7, :], acc[:, 2, 32:64], ACT.Exp).then_inc(hy["decays"], 1)
            keys_queries(0)
            for g in range(4):
                act.wait_ge(hy["xs_ps"], g + 1)
                copy(y_tok[:, g // 2, g % 2 * HALF:(g % 2 + 1) * HALF], acc[:, g, :]).then_inc(hy["xs_out"], 1)
            keys_queries(1)
            for g in range(SSD_GROUPS):
                act.wait_ge(hy["cb_ps"], g + 1)
                copy(cb_off[:, g, :], up[g][:, P:2 * P]).then_inc(hy["cb_act"], 1)
            keys_queries(2)
            keys_queries(3)
            heads_b = attention(1, 1.0, prob_b, up[2:4], acc[:, 2, :], lambda d: hh[d[0], d[1], :], hybrid_out, 3)
            for p in range(4):
                heads_b(2 * p)
                for n in (2 * p, 2 * p + 1):
                    act.wait_ge(hy["seg"], 4 * (n + 1))
                    if n >= 2:
                        act.wait_ge(hy["y_ps"], n - 1)
                    nc.scalar.activation((tmp_c, tmp_d)[n % 2][:, :], (tmp_a, tmp_b)[n % 2][:, :], ACT.Exp)\
                        .then_inc(hy["exp"], 1)
                if p:
                    round_slab(HZ + p - 1 + RING)
                heads_b(2 * p + 1)
                act.wait_ge(slab_used, HZ + p + 1)
                if p == 0:
                    act.wait_ge(hy["off_ps"], SSD_GROUPS)
                for tile in range(TILES):
                    nc.scalar.activation(z_gate[tile][:, p * TOKENS:(p + 1) * TOKENS],
                                         acc[:, 1, tile * TOKENS:(tile + 1) * TOKENS], ACT.Silu)\
                        .then_inc(hy["z_gate"], 1)
            for h in range(HEADS, HEADS + 3):
                heads_b(h)
            round_slab(HZ + 3 + RING)
            for tile in range(TILES):
                act.wait_ge(hy["y_gated"], 1 + tile)
                nc.scalar.activation(z_gate[tile][:, :], y_tok[:, tile, :], ACT.Square, scale=float(D) ** -0.5,
                                     accum_out=sumsq[:, 2 + tile:3 + tile]).then_inc(hy["sumsq"], 1)
            round_slab(HWO + RING)
            for g in range(4):
                act.wait_ge(hy["y_ps_t"], g + 1)
                copy(xh[:, 4 * (g % 2):4 * (g % 2) + 4, (g // 2) * P:(g // 2 + 1) * P],
                     up[g][:, :].rearrange("p (k n) -> p k n", k=4)).then_inc(hy["y_hi"], 1)
            for j in (1, 2, 3):
                round_slab(HWO + j + RING)
            mean_squares(6)
            operand_hi(6, HWO + 5)
            glu_part(1)
            mean_squares(7)

        @block.vector
        def _(dve):
            steps = [0]
            vec = nc.vector

            def then(ins):
                steps[0] += 1
                ins.then_inc(dve_step, 1)
                dve.wait_ge(dve_step, steps[0])

            def rest(dst, whole, high):
                return vec.tensor_tensor(dst, whole, high.bitcast(F32), ALU.subtract)

            def split_slab(m):
                if m >= N_SLABS:
                    return
                dve.wait_ge(hi_done, m + 1)
                w = width[m]
                rest(weight_lo[:, m % RING, 0:w], raw[:, m % RING, 0:w], weight_hi[:, m % RING, 0:w])\
                    .then_inc(lo_done, 1)

            def split_slab_at(m, off):
                dve.wait_ge(hi_done, off + (m + 1))
                w = width[m]
                rest(weight_lo[:, m % RING, 0:w], raw[:, m % RING, 0:w], weight_hi[:, m % RING, 0:w])\
                    .then_inc(lo_done, 1)

            def halves(a):
                return a.rearrange("p (h n) -> p h n", h=2)

            def operand_lo(b, tiles=range(TILES)):
                for tile in tiles:
                    for h in range(2):
                        g = 2 * tile + h
                        dve.wait_ge(operand_high, 4 * b + g + 1)
                        rest(xl[:, 4 * h:4 * h + 4, tile * P:(tile + 1) * P],
                             up[g][:, :].rearrange("p (k n) -> p k n", k=4),
                             xh[:, 4 * h:4 * h + 4, tile * P:(tile + 1) * P]).then_inc(operand_low, 1)

            def product_done(b, tile, h, last):
                if tile == 0:
                    dve.wait_ge(acc_part, 2 * (b - 1) + 1)
                elif h == 0:
                    dve.wait_ge(acc_part, 2 * (b - 1) + 2)
                else:
                    dve.wait_ge(slab_used, last + 1)

            HALVES = (slice(0, HALF), slice(HALF, D))

            def layer_norm(b, last, rows_landed, ready, middle=None):
                for tile in range(TILES):
                    x = x_tok[:, tile, :]
                    for h, c in enumerate(HALVES):
                        product_done(b, tile, h, last)
                        ins = vec.bn_stats(stat[:, tile, h, :], acc[:, 2 * tile + h, :])
                    then(ins)
                    vec.bn_aggr(mean_var[:, tile, :], stat[:, tile, :, :].rearrange("p a b -> p (a b)"))\
                        .then_inc(norm[b]["stat"], 1)
                    if tile and middle:
                        middle()
                    dve.wait_ge(norm[b]["rows"], rows_landed)
                    dve.wait_ge(norm[b]["stat"], tile + 1)
                    for h, c in enumerate(HALVES):
                        ins = vec.scalar_tensor_tensor(x[:, c], acc[:, 2 * tile + h, :], mean_var[:, tile, 0:1], gain[:, c],
                                                       ALU.subtract, ALU.mult)
                    then(ins)
                    dve.wait_ge(norm[b]["rstd"], tile + 1)
                    for c in HALVES:
                        vec.scalar_tensor_tensor(x[:, c], x[:, c], rstd[:, tile:tile + 1], bias[:, c],
                                                 ALU.mult, ALU.add).then_inc(norm[b][ready], 1)

            def add_product(b, last, factor, parts=range(2 * TILES)):
                for n in parts:
                    tile, h = n // 2, n % 2
                    x = x_tok[:, tile, HALVES[h]]
                    product_done(b, tile, h, last)
                    vec.scalar_tensor_tensor(x, acc[:, n, :], factor, x, ALU.mult, ALU.add)\
                        .then_inc(norm[b]["resid"], 1)

            def rms_norm(b, row, roots_before, rows_landed, tiles=range(TILES)):
                for tile in tiles:
                    dve.wait_ge(norm[b]["rstd"], roots_before + tile + 1)
                    dve.wait_ge(norm[b]["rows"], rows_landed)
                    for c in HALVES:
                        vec.scalar_tensor_tensor(normed[:, tile, c], x_tok[:, tile, c], rstd[:, 2 + tile:3 + tile],
                                                 row[:, c], ALU.mult, ALU.mult).then_inc(norm[b]["tok"], 1)

            operand_lo(0)
            dve.wait_ge(first_hi, 1)
            rest(weight_lo[:, 0, 0:SLAB // 2], raw[:, 0, 0:SLAB // 2], weight_hi[:, 0, 0:SLAB // 2]).then_inc(first_lo, 1)
            dve.wait_ge(hi_done, 1)
            rest(weight_lo[:, 0, SLAB // 2:], raw[:, 0, SLAB // 2:], weight_hi[:, 0, SLAB // 2:]).then_inc(lo_done, 1)
            for m in range(1, RING):
                split_slab(m)

            m = S_SC
            for c in range(SC_CHUNKS):
                split_slab(m + RING)
                split_slab(m + 1 + RING)
                dve.wait_ge(slab_used, m + 3)
                dve.wait_ge(sc["c_copied"], c + 1)
                vec.tensor_tensor(tmp_b[:, :], up[2][:, :], tmp_a[:, :], ALU.mult).then_inc(sc["ch_made"], 1)
                if c == 0:
                    dve.wait_ge(cols_ready, 1)
                dve.wait_ge(sc["conv0"], CT * (c + 1))
                for back in (1, 2):
                    for f in range(CT):
                        o = f * TOKENS
                        row = ROW_SC + (SC_TAPS - 1 - back) * KD + CT * c + f
                        ins = vec.scalar_tensor_tensor(
                            tmp_c[:, o + back:o + TOKENS], tmp_b[:, o:o + TOKENS - back], cols[:, row:row + 1],
                            tmp_c[:, o + back:o + TOKENS], ALU.mult, ALU.add)
                    then(ins)
                b_bank = up[3 if c % 2 else 0]
                vec.tensor_tensor(tmp_d[:, :], b_bank[:, :], tmp_c[:, :], ALU.mult).then_inc(sc["y_made"], 1)
                dve.wait_ge(sc["y_hi"], c + 1)
                rest(hl[:, CT * (c % 2):CT * (c % 2) + CT, :], tmp_d[:, :].rearrange("p (f n) -> p f n", f=CT),
                     hh[:, CT * (c % 2):CT * (c % 2) + CT, :]).then_inc(sc["chunk"], 1)
                split_slab(m + 2 + RING)
                m += 3
                if c:
                    if c < SC_CHUNKS - 1:
                        split_slab(m + RING)
                    m += 1
            layer_norm(1, S_SC + N_SC - 1, 32, "tok")
            operand_lo(1)

            def followers(last):
                split_slab(last - 1 + RING)
                split_slab(last + RING)

            followers(S_FF[0] - 1)

            def hidden_lo(par):
                return rest(hl[:, CT * par:CT * par + CT, :], tmp_b[:, :].rearrange("p (f n) -> p f n", f=CT),
                            hh[:, CT * par:CT * par + CT, :])

            def mlp_part(i):
                s, q = S_FF[i], mlp[i]

                def square():
                    vec.tensor_tensor(tmp_b[:, :], tmp_a[:, :], tmp_a[:, :], ALU.mult).then_inc(q["squared"], 1)

                dve.wait_ge(q["relu"], 1)
                square()
                split_slab(s + RING)
                dve.wait_ge(q["hidden_hi"], 1)
                hidden_lo(0).then_inc(q["chunk"], 1)
                with dve.Fori(0, FF_CHUNKS // 2 - 1) as it:
                    for j in range(4):
                        n = s + 1 + j
                        par = (1, 0)[j // 2]
                        if j % 2 == 0:
                            dve.wait_ge(q["relu"], 2 * it + (2 + j // 2))
                            square()
                        split_slab_at(n + RING, 4 * it)
                        if j % 2 == 0:
                            dve.wait_ge(q["hidden_hi"], 2 * it + (2 + j // 2))
                            hidden_lo(par).then_inc(q["chunk"], 1)
                n = s + N_FF - 3
                dve.wait_ge(q["relu"], FF_CHUNKS)
                square()
                dve.wait_ge(q["hidden_hi"], FF_CHUNKS)
                hidden_lo(1).then_inc(q["chunk"], 1)
                split_slab(n + RING)

            def glu_part(i):
                s, q = S_SG[i], glu[i]

                def gated(par):
                    vec.tensor_tensor(tmp_b[:, :], up[2 * par + 1][:, :], tmp_a[:, :], ALU.mult)\
                        .then_inc(q["hidden"], 1)

                split_slab(s + RING)
                dve.wait_ge(slab_used, s + 2)
                dve.wait_ge(q["gate"], 1)
                gated(0)
                split_slab(s + 1 + RING)
                dve.wait_ge(q["hidden_hi"], 1)
                hidden_lo(0).then_inc(q["chunk"], 1)

                def two_chunks(off, chunk, split):
                    for j in range(8):
                        n = s + 2 + j
                        par = (1, 0)[j // 4]
                        if j % 4 == 1:
                            dve.wait_ge(slab_used, off + (n + 1))
                            dve.wait_ge(q["gate"], chunk + (2 + j // 4))
                            gated(par)
                        split(n + RING)
                        if j % 4 == 1:
                            dve.wait_ge(q["hidden_hi"], chunk + (2 + j // 4))
                            hidden_lo(par).then_inc(q["chunk"], 1)

                with dve.Fori(0, GLU_PASSES) as it:
                    two_chunks(8 * it, 2 * it, lambda m: split_slab_at(m, 8 * it))
                two_chunks(8 * GLU_PASSES, 2 * GLU_PASSES,
                           lambda m: split_slab(m + 8 * GLU_PASSES) if m + 8 * GLU_PASSES < s + N_SG + 1 else None)

            mlp_part(0)
            layer_norm(2, S_MLA - 1, 32, "tok", lambda: operand_lo(2, [0]))
            operand_lo(2, [1])
            followers(S_MLA - 1)

            dve.wait_ge(mla["rows"], 32)
            dve.wait_ge(mla["rstd"], 1)
            for tile in range(TILES):
                vec.scalar_tensor_tensor(latent_q[:, tile, :], acc[:, 2 * tile, 0:Q_LORA], rstd[:, tile:tile + 1], g_q,
                                         ALU.mult, ALU.mult).then_inc(mla["latent"], 1)
            split_slab(DQ + RING)
            split_slab(DQ + 1 + RING)
            for tile in range(TILES):
                dve.wait_ge(mla["rstd"], 2 + tile)
                vec.scalar_tensor_tensor(latent_kv[:, tile, :], acc[:, 2 * tile + 1, 0:KV_LORA],
                                         rstd[:, 2 + tile:3 + tile], g_kv, ALU.mult, ALU.mult)\
                    .then_inc(mla["latent"], 1)

            def rotate(r, dst):
                dve.wait_ge(mla["swapped"], r + 1)
                if r >= 1:
                    dve.wait_ge(mla["rotated"], r)
                vec.tensor_tensor(tmp_c[:, 0:TOKENS], pe_raw[:, r % 2, :], cos, ALU.mult)
                then(vec.tensor_tensor(tmp_d[:, 0:TOKENS], acc[:, 3, 0:TOKENS], sin, ALU.mult))
                vec.tensor_tensor(dst, tmp_c[:, 0:TOKENS], tmp_d[:, 0:TOKENS], ALU.add).then_inc(mla["rotated"], 1)

            for g, (k, n) in enumerate(((0, 2), (2, 1), (3, 2))):
                dve.wait_ge(mla["t_hi"], g + 1)
                rest(xl[:, k:k + n, :], up[1 + g][:, 0:n * TOKENS].rearrange("p (k n) -> p k n", k=n),
                     xh[:, k:k + n, :]).then_inc(mla["t_lo"], 1)
            split_slab(KV + RING)
            split_slab(KV + 1 + RING)
            rotate(0, k_rot)
            for j in range(4):
                if j < 2:
                    split_slab(UQ + j + RING)
                rotate(j + 1, q_rot[:, j, :])
            split_slab(UQ + 2 + RING)
            split_slab(UQ + 3 + RING)
            dve.wait_ge(slab_used, UV + 1)
            vec.tensor_copy(halves(v_a[:, 1, :]), acc[:, 2:4, :]).then_inc(mla["v1"], 1)

            def attention(i, scale, prob, s_bank, o_part, o_lo, o_hi, lag, late=False):
                q = att[i]

                def step(h, between=None):
                    if 1 <= h <= HEADS:
                        g = h - 1
                        dve.wait_ge(q["probs"], 2 * g + 2)
                        then(vec.reciprocal(head_sum[:, 1, g, :], head_sum[:, 0, g, :]))
                        for a, b, n in ((0, P, 0), (P, 384, 1)):
                            vec.tensor_scalar(prob[:, g % 2, a:b], prob[:, g % 2, a:b], head_sum[:, 1, g, n:n + 1], None,
                                              ALU.mult).then_inc(q["normed"], 1)
                    if h < HEADS:
                        dve.wait_ge(q["scores"], h + 1)
                        S = s_bank[h % 2]
                        vec.reduce_max(head_max[:, 0, h, 0:1], S[:, 0:P], axis=AX_X)
                        then(vec.reduce_max(head_max[:, 0, h, 1:2], S[:, P:384], axis=AX_X))
                        vec.tensor_scalar(head_max[:, 1, h, :], head_max[:, 0, h, :], -scale, None, ALU.mult)\
                            .then_inc(q["negmax"], 1)
                    if between:
                        between()
                    for g in range(max(h - lag - (late and h == HEADS), 0), h - lag + (not late or h != HEADS - 1)):
                        dve.wait_ge(q["o_hi"], g + 1)
                        dst, src = o_part(g)
                        rest(o_lo(dst), src, o_hi(dst)).then_inc(q["o_lo"], 1)
                return step

            heads_a = attention(0, QK_SCALE, prob_a, up[0:2], mla_out, lambda d: xl[d[0], d[1], :],
                                lambda d: xh[d[0], d[1], :], 3)
            for h in range(HEADS + 3):
                heads_a(h)
                if h in (7, 8):
                    split_slab((UK, UV)[h - 7] + RING)
            split_slab(WO + RING)
            split_slab(WO + 1 + RING)
            layer_norm(3, WO + 3, 32, "tok")
            operand_lo(3)
            followers(WO + 3)

            mlp_part(1)
            layer_norm(4, S_SG[0] - 1, 48, "resid")
            rms_norm(4, gain2[:, :], TILES, 48)
            operand_lo(4)
            followers(S_SG[0] - 1)
            glu_part(0)
            add_product(5, S_HY - 1, 0.5, range(3))
            rms_norm(5, gain[:, :], 0, 16, [0])
            add_product(5, S_HY - 1, 0.5, [3])
            split_slab(HV + 1)
            rms_norm(5, gain[:, :], 0, 16, [1])
            operand_lo(5)
            followers(S_HY - 1)

            split_slab(HV + RING)
            split_slab(HV + 1 + RING)
            x_dt, neg_abs, e_dt, z_dt, z2_dt, series, dt, _, adt, exp_a = [dt_work[:, i, :] for i in range(10)]
            minus_adt = z_dt
            dve.wait_ge(slab_used, HDT + 1)
            dve.wait_ge(hy["rows"], 64)
            for tile in range(TILES):
                sl = slice(tile * SSD_HEADS, (tile + 1) * SSD_HEADS)
                ins = vec.tensor_tensor(x_dt[:, sl], acc[:, 2, sl], dtb_row, ALU.add)
            then(ins)
            then(vec.tensor_scalar(neg_abs, x_dt, -1.0, None, ALU.mult))
            vec.tensor_tensor(neg_abs, neg_abs, x_dt, ALU.min).then_inc(hy["dt_abs"], 1)
            split_slab(HDT + RING)
            dve.wait_ge(hy["dt_exp"], 2)
            then(vec.tensor_scalar(z_dt, e_dt, 2.0, None, ALU.add))
            then(vec.reciprocal(z_dt, z_dt))
            then(vec.tensor_tensor(z_dt, z_dt, e_dt, ALU.mult))
            then(vec.tensor_tensor(z2_dt, z_dt, z_dt, ALU.mult))
            then(vec.tensor_scalar(series, z2_dt, 1.0 / 19, None, ALU.mult))
            for k in (17, 15, 13, 11, 9, 7, 5, 3):
                then(vec.scalar_tensor_tensor(series, series, 1.0 / k, z2_dt, ALU.add, ALU.mult))
            then(vec.scalar_tensor_tensor(series, series, 1.0, z_dt, ALU.add, ALU.mult))
            then(vec.tensor_scalar(dt, x_dt, 0.0, None, ALU.max))
            then(vec.scalar_tensor_tensor(dt, series, 2.0, dt, ALU.mult, ALU.add))
            for tile in range(TILES):
                sl = slice(tile * SSD_HEADS, (tile + 1) * SSD_HEADS)
                ins = vec.tensor_tensor(minus_adt[:, sl], dt[:, sl], exp_a[:, 0:SSD_HEADS], ALU.mult)
            then(ins)
            vec.tensor_scalar(adt, minus_adt, -1.0, None, ALU.mult).then_inc(hy["adt"], 1)
            for j in range(6):
                cy, ps = (tmp_a, tmp_b)[j % 2], up[j % 4]
                dve.wait_ge(hy["tap0"], CT * (j + 1))
                for back in (1, 2, 3):
                    for f in range(CT):
                        o = f * TOKENS
                        row = ROW_XBC + (XBC_TAPS - 1 - back) * XT + CT * j + f
                        ins = vec.scalar_tensor_tensor(
                            cy[:, o + back:o + TOKENS], ps[:, o:o + TOKENS - back], cols[:, row:row + 1],
                            cy[:, o + back:o + TOKENS], ALU.mult, ALU.add)
                    if back < 3:
                        then(ins)
                ins.then_inc(hy["conv"], 1)
                split_slab(HX + j + RING)
                if j == 4:
                    dve.wait_ge(hy["cum_ps"], 1)
                    for tile, c in enumerate((64, 48)):
                        vec.tensor_copy(dt_work[:, 4, tile * SSD_HEADS:(tile + 1) * SSD_HEADS], acc[:, 2, c:c + SSD_HEADS])\
                            .then_inc(hy["cum_out"], 1)

            dve.wait_ge(hy["cum_out"], TILES)
            split_slab(HQK + RING)
            for g in range(4):
                tile, h = g // 2, g % 2
                dve.wait_ge(hy["xs_out"], g + 1)
                hd = tile * SSD_HEADS + 8 * h
                vec.tensor_tensor(heads(xdt[:, tile, h * HALF:(h + 1) * HALF]), heads(acc[:, g, :]),
                                  per_head(dt[:, hd:hd + 8]), ALU.mult).then_inc(hy["xdt"], 1)
                if g == 1:
                    dve.wait_ge(hy["decays"], 1)
                    dve.wait_ge(hy["xdt"], 2)
                    vec.tensor_tensor(heads(xdt_end, SSD_HEADS), heads(xdt[:, 0, :], SSD_HEADS),
                                      per_head(dt_work[:, 7, 0:SSD_HEADS], SSD_HEADS), ALU.mult).then_inc(hy["cb"], 1)
            split_slab(HQK + 1 + RING)
            for g in range(SSD_GROUPS):
                dve.wait_ge(hy["cb_act"], g + 1)
                for tile in range(TILES):
                    vec.tensor_tensor(cb_diag[:, 2 * g + tile, :], up[g][:, 2 * P * tile:2 * P * tile + P], tri, ALU.mult)\
                        .then_inc(hy["cb"], 1)
            split_slab(HQK + 2 + RING)
            dve.wait_ge(hy["y_skip"], 4)
            for g in range(SSD_GROUPS):
                dve.wait_ge(hy["off_ps"], g + 1)
                part = (tmp_a, tmp_b)[g][:, :]
                vec.tensor_tensor(heads(part), heads(up[g][:, :]),
                                  per_head(dt_work[:, 7, SSD_HEADS + 8 * g:SSD_HEADS + 8 * g + 8]), ALU.mult)\
                    .then_inc(hy["off_taken"], 1)
            dve.wait_ge(hy["off_taken"], SSD_GROUPS)
            for g in range(SSD_GROUPS):
                y = y_tok[:, 1, g * HALF:(g + 1) * HALF]
                vec.tensor_tensor(y, y, (tmp_a, tmp_b)[g][:, :], ALU.add).then_inc(hy["y_sum"], 1)
            dve.wait_ge(hy["y_sum"], SSD_GROUPS)
            split_slab(HQK + 3 + RING)
            dve.wait_ge(hy["cb"], 5)
            heads_b = attention(1, 1.0, prob_b, up[2:4], hybrid_out, lambda d: hl[d[0], d[1], :],
                                lambda d: hh[d[0], d[1], :], 3, late=True)

            def add_scan(p):
                g, tile = p % 2, p // 2
                y = y_tok[:, tile, g * HALF:(g + 1) * HALF]
                dve.wait_ge(hy["y_ps"], 2 * p + 2)
                vec.tensor_tensor(y, acc[:, 0, :], y, ALU.add).then_inc(hy["y_sum"], 1)

            for p in range(4):
                g, tile = p % 2, p // 2
                heads_b(2 * p, lambda: add_scan(p - 1) if p else None)
                for n in (2 * p, 2 * p + 1):
                    dve.wait_ge(hy["seg_ps"], n + 1)
                    if n >= 2:
                        dve.wait_ge(hy["exp"], n - 1)
                    for q in range(4):
                        c = slice(q * P, (q + 1) * P)
                        vec.tensor_scalar((tmp_a, tmp_b)[n % 2][:, c], up[n % 2][:, c], cum_head(tile, 4 * (n % 4) + q), 0.0,
                                          ALU.subtract, ALU.min).then_inc(hy["seg"], 1)
                for n in (2 * p, 2 * p + 1):
                    dve.wait_ge(hy["exp"], n + 1)
                    w = (tmp_c, tmp_d)[n % 2][:, :].rearrange("p (h l) -> p h l", h=4)
                    cb = cb_diag[:, 2 * g + tile:2 * g + tile + 1, :].to_broadcast([P, 4, P])
                    vec.tensor_tensor(w, w, cb, ALU.mult).then_inc(hy["seg_w"], 1)
                heads_b(2 * p + 1, lambda: split_slab(HZ + p - 1 + RING) if p in (1, 2) else None)
            heads_b(HEADS, lambda: add_scan(3))
            heads_b(HEADS + 1)
            heads_b(HEADS + 2)
            for tile in range(TILES):
                y = y_tok[:, tile, :]
                dve.wait_ge(hy["y_sum"], 4 + 2 * tile)
                dve.wait_ge(hy["z_gate"], 4 * TILES)
                vec.tensor_tensor(y, y, z_gate[tile][:, :], ALU.mult).then_inc(hy["y_gated"], 1)
            split_slab(HZ + 2 + RING)
            split_slab(HZ + 3 + RING)
            for tile in range(TILES):
                y = y_tok[:, tile, :]
                dve.wait_ge(hy["rstd"], tile + 1)
                for c in HALVES:
                    vec.scalar_tensor_tensor(y[:, c], y[:, c], rstd[:, tile:tile + 1], gain2[:, c], ALU.mult, ALU.mult)\
                        .then_inc(hy["y_n"], 1)
            split_slab(HWO + RING)
            for g in range(4):
                tile, f = g // 2, g % 2
                dve.wait_ge(hy["y_hi"], g + 1)
                rest(xl[:, 4 * f:4 * f + 4, tile * P:(tile + 1) * P], up[g][:, :].rearrange("p (k n) -> p k n", k=4),
                     xh[:, 4 * f:4 * f + 4, tile * P:(tile + 1) * P]).then_inc(hy["y_lo"], 1)
            for j in (1, 2, 3):
                split_slab(HWO + j + RING)
            add_product(6, HWO + 5, 1.0)
            rms_norm(6, gain[:, :], 0, 16)
            operand_lo(6)
            followers(HWO + 5)
            glu_part(1)
            add_product(7, S_SG[1] + N_SG - 1, 0.5)
            rms_norm(7, gain[:, :], 0, 16)

        @block.tensor
        def _(pe):
            mm = nc.tensor.matmul

            def weights(m, off=0):
                pe.wait_ge(lo_done, off + (m + 1))

            def up_block(dst, m, col, step, k_tiles, x_tile=0, w_tile=0, first=True, last=True):
                for k in range(k_tiles):
                    c = (w_tile + k) * step + col
                    w_h = weight_hi[:, m % RING, c:c + P]
                    w_l = weight_lo[:, m % RING, c:c + P]
                    mm(dst, w_h, xh[:, x_tile + k, :], start=first and k == 0, stop=False)
                    mm(dst, w_h, xl[:, x_tile + k, :], start=False, stop=False)
                    ins = mm(dst, w_l, xh[:, x_tile + k, :], start=False, stop=last and k == k_tiles - 1)
                return ins

            def up_product(m, bank, b=None):
                for f in range(CT):
                    dst = bank[:, f * TOKENS:(f + 1) * TOKENS]
                    if b is None:
                        ins = up_block(dst, m, f * P, CHUNK_F, KD)
                        continue
                    w_h, w_l = [[w[:, m % RING, k * CHUNK_F + f * P:k * CHUNK_F + f * P + P] for k in range(KD)]
                                for w in (weight_hi, weight_lo)]
                    for k in range(KD):
                        if (f, k) == (0, 0):
                            pe.wait_ge(operand_low, 4 * b + 1)
                        if f == 0 and k in (0, KD // 2):
                            pe.wait_ge(operand_high, 4 * b + 3 + k // 4)
                            if b == 0:
                                pe.wait_ge(*((lo_done, 1) if k else (first_lo, 1)))
                        mm(dst, w_h[k], xh[:, k, :], start=k == 0, stop=False)
                        mm(dst, w_l[k], xh[:, k, :], start=False, stop=False)
                    pe.wait_ge(operand_low, 4 * b + 4)
                    for k in range(KD):
                        ins = mm(dst, w_h[k], xl[:, k, :], start=False, stop=k == KD - 1)
                ins.then_inc(slab_used, 1)

            def token_block(dst, s_h, s_l, w_h, w_l, first, last):
                open_group = dict(skip_group_check=True)
                for d, h, l in zip(dst, w_h, w_l):
                    mm(d, s_h, h, start=first, stop=False, **open_group)
                    mm(d, s_h, l, start=False, stop=False, **open_group)
                for d, h in zip(dst, w_h):
                    ins = mm(d, s_l, h, start=False, stop=last, **open_group)
                return ins

            def down_block(m, s_h, s_l, j, tile, halves, first, last):
                cut = slice(tile * P, (tile + 1) * P)
                c = [slice(j * D + h * HALF, j * D + (h + 1) * HALF) for h in halves]
                return token_block([acc[:, 2 * tile + h, :] for h in halves], s_h(j)[:, cut], s_l(j)[:, cut],
                                   [weight_hi[:, m % RING, x] for x in c], [weight_lo[:, m % RING, x] for x in c],
                                   first, last)

            def down_product(m, s_h, s_l, k_tiles, between=None):
                for j in range(k_tiles):
                    if j and between:
                        between()
                    for tile in range(TILES):
                        ins = down_block(m, s_h, s_l, j, tile, (0, 1), False, False)
                ins.then_inc(slab_used, 1)

            def last_products(b, k_tiles, slabs):
                for tile, halves in ((0, (0, 1)), (1, (0,)), (1, (1,))):
                    for n, (m, s_h, s_l, ready) in enumerate(slabs):
                        if tile == 0:
                            weights(m)
                            ready()
                        for j in range(k_tiles):
                            ins = down_block(m, s_h, s_l, j, tile, halves, False, (n, j) == (len(slabs) - 1, k_tiles - 1))
                        if tile and halves == (1,):
                            ins.then_inc(slab_used, 1)
                    if halves != (1,):
                        ins.then_inc(acc_part, 1)

            def hidden(par, j0=0):
                return (lambda j: hh[:, CT * par + j0 + j, :]), (lambda j: hl[:, CT * par + j0 + j, :])

            def keep_warm(n):
                for _ in range(n):
                    mm(up[3][:, :], zeros[:, 0:P], zeros[:, :], start=True, stop=True)

            def turn_tile(b, src, tile):
                if b == 0:
                    pe.wait_ge(x_landed[tile], 16)
                for h in range(2):
                    if b:
                        pe.wait_ge(norm[b]["tok"], 2 * tile + h + 1)
                    for j in range(4):
                        f = (4 * h + j) * P
                        ins = nc.tensor.transpose(up[2 * tile + h][:, j * P:(j + 1) * P], src[:, tile, f:f + P], ident)
                    ins.then_inc(turned, 1)

            def turn(b, src):
                if b:
                    keep_warm(WARM[b][0])
                turn_tile(b, src, 0)
                if b in (1, 3):
                    carry(0)
                if b:
                    keep_warm(WARM[b][1])
                turn_tile(b, src, 1)
                if b in (4, 6):
                    clear_acc()

            def carry(tile, halves=(0, 1)):
                for h in halves:
                    mm(acc[:, 2 * tile + h, :], alpha_ident, x_tok[:, tile, h * HALF:(h + 1) * HALF], start=True,
                       stop=False, skip_group_check=True)

            def clear_acc():
                for n in range(4):
                    mm(acc[:, n, :], zeros[0:1, 0:P], zeros[0:1, :], start=True, stop=False, skip_group_check=True)

            WARM = {1: (9, 8), 3: (4, 3), 4: (22, 0), 5: (6, 7), 6: (7, 2)}

            pe.wait_ge(zeros_ready, 4)
            keep_warm(8)
            pe.wait_ge(ident_landed, 16)
            turn(0, x_tok)
            carry(0)
            carry(1)

            m = S_SC
            for c in range(SC_CHUNKS):
                if c == 1:
                    for n in range(10):
                        mm(acc[:, n % 4, :], zeros[:, 0:P], zeros[:, :], start=False, stop=False, skip_group_check=True)
                    pe.wait_ge(cols_ready, 1)
                if c:
                    weights(m)
                up_product(m, up[3 if c % 2 else 0], 0 if c == 0 else None)
                weights(m + 1)
                if c:
                    pe.wait_ge(sc["c_copied"], c)
                up_product(m + 1, up[1])
                if c == 0:
                    pe.wait_ge(const_landed, 64)
                    nc.tensor.transpose(up[3][:, 0:ROWS], rows[:, :], ident[0:ROWS, 0:ROWS]).then_inc(cols_turned, 1)
                weights(m + 2)
                if c:
                    pe.wait_ge(sc["ch_made"], c)
                up_product(m + 2, up[2])
                m += 3
                if c:
                    weights(m)
                    pe.wait_ge(sc["chunk"], c)
                    down_product(m, *hidden((c - 1) % 2), CT)
                    m += 1
            last_products(1, CT, [(m, *hidden((SC_CHUNKS - 1) % 2), lambda: pe.wait_ge(sc["chunk"], SC_CHUNKS))])

            def mlp_part(i, b):
                s, q = S_FF[i], mlp[i]
                weights(s)
                carry(1, (0,))
                up_product(s, up[0], b - 1)
                carry(1, (1,))
                with pe.Fori(0, FF_CHUNKS // 2 - 1) as it:
                    for j in range(4):
                        m = s + 1 + j
                        weights(m, 4 * it)
                        if j % 2 == 0:
                            up_product(m, up[(1, 0)[j // 2]])
                        else:
                            pe.wait_ge(q["chunk"], 2 * it + (1 + j // 2))
                            down_product(m, *hidden(j // 2), CT)
                m = s + N_FF - 3
                weights(m)
                up_product(m, up[1])
                last_products(b, CT, [(m + 1, *hidden(0), lambda: pe.wait_ge(q["chunk"], FF_CHUNKS - 1)),
                                      (m + 2, *hidden(1), lambda: pe.wait_ge(q["chunk"], FF_CHUNKS))])

            def glu_part(i, b):
                s, q = S_SG[i], glu[i]
                for j in range(2):
                    weights(s + j)
                    up_product(s + j, up[j], None if j else b - 1)
                with pe.Fori(0, (SG_CHUNKS - 1) // 2) as it:
                    for j in range(8):
                        m = s + 2 + j
                        weights(m, 8 * it)
                        par = (1, 0)[j // 4]
                        if j % 4 < 2:
                            up_product(m, up[2 * par + j % 4])
                        else:
                            if j % 4 == 2:
                                pe.wait_ge(q["chunk"], 2 * it + (1 + j // 4))
                            down_product(m, *hidden(1 - par, j % 4 - 2), 1)
                m = s + N_SG - 2
                last_products(b, 1, [(m + j, *hidden(0, j), lambda: pe.wait_ge(q["chunk"], SG_CHUNKS)) for j in range(2)])

            turn(1, x_tok)
            mlp_part(0, 2)
            turn_tile(2, x_tok, 0)

            def token_product(m, dst, n, step, k_tiles, x_tile, first, last, tiles=range(TILES)):
                for tile in tiles:
                    for k in range(k_tiles):
                        c = k * step
                        cut = slice(tile * P, (tile + 1) * P)
                        ins = token_block([dst(tile)], xh[:, x_tile + k, cut], xl[:, x_tile + k, cut],
                                          [weight_hi[:, m % RING, c:c + n]], [weight_lo[:, m % RING, c:c + n]],
                                          first and k == 0, last and k == k_tiles - 1)
                return ins

            def fresh_product(b, m, dst, n, tile, middle=lambda: None):
                open_group = dict(skip_group_check=True)
                blocks = [(j, 4 * j + k, slice(k * n, (k + 1) * n)) for j in range(2) for k in range(4)]
                cut = slice(tile * P, (tile + 1) * P)
                for j, f, c in blocks:
                    if f % 4 == 0:
                        pe.wait_ge(operand_high, 4 * b + 2 * tile + j + 1)
                        weights(m + j)
                    mm(dst, xh[:, f, cut], weight_hi[:, (m + j) % RING, c], start=f == 0, stop=False, **open_group)
                    mm(dst, xh[:, f, cut], weight_lo[:, (m + j) % RING, c], start=False, stop=False, **open_group)
                middle()
                for j, f, c in blocks:
                    if f % 4 == 0:
                        pe.wait_ge(operand_low, 4 * b + 2 * tile + j + 1)
                    ins = mm(dst, xl[:, f, cut], weight_hi[:, (m + j) % RING, c], start=False, stop=f == 7, **open_group)
                    if tile and f % 4 == 3:
                        ins.then_inc(slab_used, 1)


            def key_latent(j, tile):
                return token_product(KV + j, lambda t: acc[:, 2 * t + 1, 0:KV_LORA], KV_LORA, KV_COLS, 4, 4 * j,
                                     j == 0, j == 1, [tile])

            fresh_product(2, DQ, acc[:, 0, 0:Q_LORA], Q_LORA, 0)
            turn_tile(2, x_tok, 1)
            fresh_product(2, DQ, acc[:, 2, 0:Q_LORA], Q_LORA, 1)
            for tile in range(TILES):
                for j in range(2):
                    weights(KV + j)
                    ins = key_latent(j, tile)
                ins.then_inc(mla["latent_ps"], 1)
            for j in range(2):
                up_block(up[0][:, 0:TOKENS], KV + j, KV_LORA, KV_COLS, 4, 4 * j, 0, j == 0, j == 1)\
                    .then_inc(slab_used, 1)

            def partner(r):
                pe.wait_ge(mla["pe"], r + 1)
                if r:
                    pe.wait_ge(mla["rotated"], r)
                mm(acc[:, 3, 0:TOKENS], swap, pe_raw[:, r % 2, :], start=True, stop=True).then_inc(mla["swapped"], 1)

            for g in range(3):
                pe.wait_ge(mla["latent"], TILES if g < 2 else 2 * TILES)
                blocks = (((0, 0), (0, 1), (1, 0), (1, 1)), ((2, 0), (2, 1)), ((0, 0), (0, 1), (1, 0), (1, 1)))[g]
                src = latent_kv if g == 2 else latent_q
                for n, (k, tile) in enumerate(blocks):
                    ins = nc.tensor.transpose(up[1 + g][:, n * P:(n + 1) * P], src[:, tile, k * P:(k + 1) * P], ident)
                ins.then_inc(mla["turned"], 1)
            partner(0)
            pe.wait_ge(mla["t_lo"], 3)
            for j in range(4):
                weights(UQ + j)
                if j >= 2:
                    pe.wait_ge(mla["q_out"], j - 1)
                for f in range(2):
                    up_block(up[j % 2][:, f * TOKENS:(f + 1) * TOKENS], UQ + j, f * NOPE, UQ_COLS, KQ)
                up_block(up[2 + j % 2][:, 0:TOKENS], UQ + j, 2 * NOPE, UQ_COLS, KQ).then_inc(slab_used, 1)
                if j:
                    partner(j)
            weights(UK)
            pe.wait_ge(mla["q_out"], 4)
            for j in range(4):
                for f in range(2):
                    ins = up_block(up[j][:, f * TOKENS:(f + 1) * TOKENS], UK, (2 * j + f) * NOPE, D, KKV, KQ)
                ins.then_inc(mla["k_ps"] if j < 3 else slab_used, 1)
                if j == 1:
                    partner(4)
            weights(UV)
            pe.wait_ge(mla["rotated"], 5)
            for k in range(KKV):
                for tile in range(TILES):
                    cut = slice(tile * P, (tile + 1) * P)
                    c = [slice(k * D + h * HALF, k * D + (h + 1) * HALF) for h in range(2)]
                    ins = token_block([acc[:, 2 * tile + h, :] for h in range(2)],
                                      xh[:, KQ + k, cut], xl[:, KQ + k, cut],
                                      [weight_hi[:, UV % RING, x] for x in c], [weight_lo[:, UV % RING, x] for x in c],
                                      k == 0, k == KKV - 1)
            ins.then_inc(slab_used, 1)

            def attention(i, score, prob, v, s_bank, t_bank, o_dst, o_banks):
                q = att[i]

                def scores(h):
                    if h >= 2:
                        pe.wait_ge(q["probs"], 2 * (h - 2) + 2)
                    S = s_bank[h % 2]
                    score(h, 0, S[:, 0:P])
                    mm(S[:, P - ATTN_CHUNK:P], mask_row[:, :], mask_ones[:, :], start=False, stop=True,
                       skip_group_check=True)
                    score(h, 1, S[:, P:384])
                    mm(S[:, 384 - ATTN_CHUNK:384], mask_row[:, :], mask_ones[:, :], start=False, stop=True,
                       skip_group_check=True).then_inc(q["scores"], 1)

                def turn_probs(g):
                    pe.wait_ge(q["normed"], 2 * g + 2)
                    if g:
                        pe.wait_ge(q["t_out"], g)
                    for n in range(3):
                        ins = nc.tensor.transpose(t_bank[:, n * P:(n + 1) * P], prob[:, g % 2, n * P:(n + 1) * P], ident)
                    ins.then_inc(q["turned"], 1)

                def outputs(g):
                    pe.wait_ge(q["t_out"], g + 1)
                    if g >= o_banks:
                        pe.wait_ge(q["o_lo"], g - o_banks + 1)
                    o = o_dst(g)
                    mm(o, v(0, g), prob_t[:, g % 2, 0:TOKENS], start=True, stop=False, skip_group_check=True)
                    mm(o[:, P:TOKENS], v(1, g), prob_t[:, g % 2, TOKENS:384], start=False, stop=True,
                       skip_group_check=True).then_inc(q["o_ps"], 1)

                def step(g, between=None):
                    if g < HEADS:
                        turn_probs(g)
                    if g + 2 < HEADS:
                        scores(g + 2)
                    if between:
                        between()
                    if g:
                        outputs(g - 1)

                return scores, step

            def mla_score(h, tile, dst):
                queries, keys = slice(tile * P, (tile + 1) * P), slice(0, (tile + 1) * P)
                r = slice(ROPE * (h % 2), ROPE * (h % 2) + ROPE)
                mm(dst, q_nope[:, h, queries], k_nope[:, h, keys], start=True, stop=False, skip_group_check=True)
                mm(dst, q_rot[r, h // 2, queries], k_rot[r, keys], start=False, stop=False, skip_group_check=True)

            def latent_rows(c):
                return (lambda j: xh[:, CT * c + j, :]), (lambda j: xl[:, CT * c + j, :])

            def heads_out(c):
                pe.wait_ge(att[0]["o_lo"], CT * c + 2)

            pe.wait_ge(mla["k_out"], 4)
            scores, step = attention(0, mla_score, prob_a, lambda kt, h: v_a[:, kt, h * P:(h + 1) * P], up[0:2], up[2],
                                     lambda h: up[3][:, 0:TOKENS], 1)
            scores(0)
            scores(1)
            keep_warm(12)

            def values_ready():
                pe.wait_ge(mla["v0"], 1)
                pe.wait_ge(mla["v1"], 1)

            def first_rows(c):
                weights(WO + c)
                heads_out(c)
                down_product(WO + c, *latent_rows(c), CT)

            for g in range(HEADS + 1):
                if g == 1:
                    step(g, values_ready)
                elif g in (6, 7):
                    step(g, lambda: first_rows(g - 6))
                else:
                    step(g)
                if 1 <= g <= 4:
                    carry((g - 1) // 2, ((g - 1) % 2,))
            last_products(3, CT, [(WO + c, *latent_rows(c), lambda c=c: heads_out(c)) for c in (2, 3)])

            turn(3, x_tok)
            mlp_part(1, 4)
            turn(4, normed)
            glu_part(0, 5)
            keep_warm(WARM[5][0])
            turn_tile(5, normed, 0)
            keep_warm(WARM[5][1])

            fresh_product(5, HV, acc[:, 0, :], HALF, 0, lambda: turn_tile(5, normed, 1))
            fresh_product(5, HV, acc[:, 1, :], HALF, 1)
            weights(HDT)
            token_product(HDT, lambda t: acc[:, 2, t * SSD_HEADS:(t + 1) * SSD_HEADS], SSD_HEADS, SSD_HEADS, KD, 0, True, True)\
                .then_inc(slab_used, 1)
            for j in range(6):
                weights(HX + j)
                if j >= 4:
                    pe.wait_ge(hy["conv"], j - 3)
                up_product(HX + j, up[j % 4])
                if j == 3:
                    pe.wait_ge(hy["adt"], 1)
                    mm(acc[:, 2, 32:32 + SSD_HEADS], after, adt_tile(0), start=True, stop=True)
                    mm(acc[:, 2, 32 + SSD_HEADS:64], tri, adt_tile(1), start=True, stop=True)
                    mm(acc[:, 2, 64:64 + SSD_HEADS], tri, adt_tile(0), start=True, stop=True).then_inc(hy["cum_ps"], 1)

            def keys_queries(j):
                weights(HQK + j)
                if j < 2:
                    pe.wait_ge(hy["conv"], 3 + j)
                else:
                    pe.wait_ge(hy["qk_out"], j - 1)
                up_product(HQK + j, up[2 + j % 2])

            keys_queries(0)
            pe.wait_ge(hy["xbc"], 4)
            pe.wait_ge(hy["v_out"], TILES)
            pe.wait_ge(hy["decays"], 1)
            for g in range(4):
                tile, h = g // 2, g % 2
                for j in range(4):
                    ins = nc.tensor.transpose(acc[:, g, j * P:(j + 1) * P], xs_t[:, 4 * h + j, tile * P:(tile + 1) * P],
                                              ident)
                ins.then_inc(hy["xs_ps"], 1)
            keys_queries(1)
            pe.wait_ge(hy["xbc"], 6)
            for g in range(SSD_GROUPS):
                mm(up[g][:, 0:TOKENS], bc_t[:, g, 0:P], bc_t[:, 2 + g, :], start=True, stop=True)
                mm(up[g][:, TOKENS:384], bc_t[:, g, P:TOKENS], bc_t[:, 2 + g, P:TOKENS], start=True, stop=True)\
                    .then_inc(hy["cb_ps"], 1)
            keys_queries(2)
            pe.wait_ge(hy["cb"], 5)
            pe.wait_ge(hy["cb_act"], 2)
            for g in range(SSD_GROUPS):
                mm(up[g][:, :], cb_off[:, g, :], xdt_end[:, g * HALF:(g + 1) * HALF], start=True, stop=True)\
                    .then_inc(hy["off_ps"], 1)
            keys_queries(3)

            def decay_sums(n):
                tile, h0 = n // 4, 4 * (n % 4)
                bank = up[n % 2]
                if n >= 2:
                    pe.wait_ge(hy["seg"], 4 * (n - 1))
                else:
                    pe.wait_ge(hy["off_taken"], n + 1)
                for q in range(4):
                    ins = mm(bank[:, q * P:(q + 1) * P], adt_tile(tile)[:, h0 + q:h0 + q + 1].to_broadcast([P, P]),
                             tri, start=True, stop=True)
                ins.then_inc(hy["seg_ps"], 1)

            def scan_outputs(n):
                tile, h0 = n // 4, 4 * (n % 4)
                if n == 0:
                    pe.wait_ge(hy["xdt"], 4)
                    pe.wait_ge(hy["xs_out"], 4)
                elif n % 2 == 0:
                    pe.wait_ge(hy["y_sum"], 2 + n // 2)
                pe.wait_ge(hy["seg_w"], n + 1)
                for q in range(4):
                    h = h0 + q
                    ins = mm(acc[:, 0, h % 8 * SSD_HD:(h % 8 + 1) * SSD_HD],
                             (tmp_c, tmp_d)[n % 2][:, q * P:(q + 1) * P], xdt[:, tile, h * SSD_HD:(h + 1) * SSD_HD],
                             start=True, stop=True)
                ins.then_inc(hy["y_ps"], 1)

            def hybrid_score(h, tile, dst):
                queries, keys = slice(tile * P, (tile + 1) * P), slice(0, (tile + 1) * P)
                r = slice(ATT_HD * (h % 2), ATT_HD * (h % 2) + ATT_HD)
                mm(dst, q_b[r, h // 2, queries], k_b[r, h // 2, keys], start=True, stop=False, skip_group_check=True)
                for kt in range(tile + 1):
                    w0 = (tile - kt) * P
                    mm(dst[:, kt * P:(kt + 1) * P], hankel[:, h, w0:w0 + P], anti, start=False, stop=False,
                       skip_group_check=True)

            scores, step = attention(1, hybrid_score, prob_b, lambda kt, h: v_b[:, kt, h * ATT_HD:(h + 1) * ATT_HD],
                                     up[2:4], acc[:, 2, :],
                                     lambda h: acc[ATT_HD * (h % 2):ATT_HD * (h % 2) + ATT_HD, 3, 0:TOKENS], 2)
            for p in range(4):
                if p == 0:
                    pe.wait_ge(hy["xdt"], 4)
                    pe.wait_ge(hy["xs_out"], 4)
                    pe.wait_ge(hy["hank"], 16 * HEADS)
                    pe.wait_ge(hy["qk_out"], 4)
                    scores(0)
                    scores(1)
                else:
                    step(2 * p - 1)
                decay_sums(2 * p)
                decay_sums(2 * p + 1)
                weights(HZ + p)
                if p:
                    pe.wait_ge(hy["z_gate"], 2 * p)
                token_product(HZ + p, lambda t: acc[:, 1, t * TOKENS:(t + 1) * TOKENS], CHUNK_F, CHUNK_F, KD, 0,
                              True, True).then_inc(slab_used, 1)
                scan_outputs(2 * p)
                scan_outputs(2 * p + 1)
                step(2 * p)
            step(HEADS - 1)
            step(HEADS, lambda: keep_warm(7))

            def turn_y():
                for n in range(2 * TILES):
                    tile, h = n // 2, n % 2
                    pe.wait_ge(hy["y_n"], n + 1)
                    for j in range(4):
                        f = (4 * h + j) * P
                        ins = nc.tensor.transpose(up[n][:, j * P:(j + 1) * P], y_tok[:, tile, f:f + P], ident)
                    ins.then_inc(hy["y_ps_t"], 1)

            def head_rows(c):
                return (lambda j: hh[:, CT * c + j, :]), (lambda j: hl[:, CT * c + j, :])

            pe.wait_ge(hy["z_gate"], 4 * TILES)
            pe.wait_ge(hy["y_sum"], 2 + 4)
            weights(HWO)
            pe.wait_ge(att[1]["o_lo"], 4)
            for tile in range(TILES):
                if tile:
                    pe.wait_ge(att[1]["o_lo"], HEADS)
                for j in range(CT):
                    ins = down_block(HWO, *head_rows(0), j, tile, (0, 1), j == 0, False)
            ins.then_inc(slab_used, 1)
            weights(HWO + 1)
            down_product(HWO + 1, *head_rows(1), CT, between=turn_y)
            pe.wait_ge(hy["y_lo"], 4)
            for c in range(2):
                weights(HWO + 2 + c)
                down_product(HWO + 2 + c, *latent_rows(c), CT)
            last_products(6, CT, [(HWO + 2 + c, *latent_rows(c), lambda: None) for c in (2, 3)])
            turn(6, normed)
            glu_part(1, 7)


_NAMES = [
    "x", "sc_w_in", "sc_conv_w", "sc_w_out", "mla_w_dq", "mla_g_q", "mla_w_uq", "mla_w_dkv", "mla_g_kv",
    "mla_w_uk", "mla_w_uv", "mla_w_o", "ff_w1", "ff_w2", "ln_mix_g", "ln_mix_b", "ln_ff_g", "ln_ff_b",
    "ffn1_norm_2", "ffn1_w_gate_2", "ffn1_w_up_2", "ffn1_w_down_2", "mix_norm_2", "w_in_2", "conv_w_2",
    "conv_b_2", "dt_bias_2", "a_log_2", "d_skip_2", "ssd_norm_2", "rel_bias_2", "w_out_2", "ffn2_norm_2",
    "ffn2_w_gate_2", "ffn2_w_up_2", "ffn2_w_down_2", "final_norm_2",
]


def kernel(**inputs):
    import concourse.bacc as bacc
    from concourse.bass_utils import run_bass_kernel_spmd

    nc = bacc.Bacc("TRN2", target_bir_lowering=False, num_devices=1)
    arrays = {name: np.ascontiguousarray(inputs[name]) for name in _NAMES}
    arrays["shape_consts"] = shape_constants()
    aps = {n: nc.dram_tensor(f"in_{n}", a.shape, mybir.dt.from_np(a.dtype), kind="ExternalInput").ap()
           for n, a in arrays.items()}
    out = nc.dram_tensor("out", (1, TOKENS, D), F32, kind="ExternalOutput").ap()
    two_blocks(nc, aps, aps["shape_consts"], out)
    r = run_bass_kernel_spmd(nc, [{f"in_{n}": a for n, a in arrays.items()}], core_ids=[0])
    return r.results[0]["out"]
```
